# Optimizing a Trainium2 kernel written in Bass

```python
import math
import jax, jax.numpy as jnp
from jax import lax
import numpy as np

D_MODEL = 1024
BATCH = 1
SEQ = 256
DEPTH = 2

N_MIXERS = 4
RMS_EPS = 1e-6
LN_EPS = 1e-5
NEG_INF = -1e30
BIG = 1e9
D_FF = -(-8 * D_MODEL // (3 * 256)) * 256

CONV_WIDTH = 31

NSA_HEAD_DIM = 64
NSA_HEADS = D_MODEL // NSA_HEAD_DIM
NSA_KV_GROUPS = 4
NSA_CMP_BLOCK = 32
NSA_CMP_STRIDE = 16
NSA_SLC_BLOCK = 64
NSA_TOP_N = 16
NSA_LOCAL_BLOCKS = 2
NSA_WINDOW = 512
NSA_Q_CHUNK = 32
NSA_PROJ = NSA_HEADS * NSA_HEAD_DIM + 6 * NSA_KV_GROUPS * NSA_HEAD_DIM + 3 * NSA_HEADS
ROPE_THETA = 500000.0
ROPE_DIMS = NSA_HEAD_DIM // 4

S5_GROUP = 16
S5_STATE = 64
S5_N_GROUPS = D_MODEL // S5_GROUP

POOL_WINDOWS = (2, 4, 8, 16)
POOL_GROUP = D_MODEL // len(POOL_WINDOWS)


def _n_layers_of(m):
    return (DEPTH - m + N_MIXERS - 1) // N_MIXERS

def rmsnorm(x, g):
    xf = x.astype(jnp.float32)
    y = xf * lax.rsqrt(jnp.mean(xf * xf, axis=-1, keepdims=True) + RMS_EPS)
    return (y * g.astype(jnp.float32)).astype(x.dtype)

def partial_rope(x, positions):
    half = ROPE_DIMS // 2
    inv_freq = ROPE_THETA ** (-jnp.arange(half, dtype=jnp.float32) / half)
    ang = positions.astype(jnp.float32)[:, None] * inv_freq[None, :]
    cos, sin = jnp.cos(ang), jnp.sin(ang)
    xr = x[..., :ROPE_DIMS].astype(jnp.float32)
    x1, x2 = xr[..., :half], xr[..., half:]
    rot = jnp.concatenate([x1 * cos - x2 * sin, x2 * cos + x1 * sin], axis=-1)
    return jnp.concatenate([rot.astype(x.dtype), x[..., ROPE_DIMS:]], axis=-1)

def masked_softmax(s, mask):
    s = jnp.where(mask, s.astype(jnp.float32), NEG_INF)
    return jax.nn.softmax(s, axis=-1) * mask.astype(jnp.float32)

def swiglu_ffn(h, w_in, w_out):
    gate, up = jnp.split(h @ w_in, 2, axis=-1)
    return (jax.nn.silu(gate) * up) @ w_out

def conformer_conv_module(h, w_in, b_in, w_dw, b_dw, ln_g, ln_b, w_out):
    a, g = jnp.split(h @ w_in + b_in, 2, axis=-1)
    u = a * jax.nn.sigmoid(g)
    u = lax.conv_general_dilated(
        u, w_dw[:, None, :].astype(u.dtype), window_strides=(1,),
        padding=[(CONV_WIDTH - 1, 0)], dimension_numbers=('NWC', 'WIO', 'NWC'),
        feature_group_count=D_MODEL) + b_dw
    uf = u.astype(jnp.float32)
    mu = jnp.mean(uf, axis=-1, keepdims=True)
    var = jnp.mean(jnp.square(uf - mu), axis=-1, keepdims=True)
    uf = (uf - mu) * lax.rsqrt(var + LN_EPS) * ln_g.astype(jnp.float32) + ln_b.astype(jnp.float32)
    u = jax.nn.silu(uf).astype(h.dtype)
    return u @ w_out

def nsa_attention(h, positions, w_in, q_gain, k_gain, cmp_pos, cmp_w1, cmp_b1, cmp_w2, w_out):
    bsz, seq, _ = h.shape
    H, G, dh = NSA_HEADS, NSA_KV_GROUPS, NSA_HEAD_DIM
    R = H // G
    qd, kvd = H * dh, 6 * G * dh
    proj = h @ w_in
    q = proj[..., :qd].reshape(bsz, seq, H, dh).transpose(0, 2, 1, 3)
    kv = proj[..., qd:qd + kvd].reshape(bsz, seq, 3, 2, G, dh).transpose(2, 3, 0, 4, 1, 5)
    gates = jax.nn.sigmoid(proj[..., qd + kvd:].astype(jnp.float32)).reshape(bsz, seq, 3, H)
    q = partial_rope(rmsnorm(q, q_gain), positions)
    k = partial_rope(rmsnorm(kv[:, 0], k_gain[:, None, None, None, :]), positions)
    v = kv[:, 1]

    n_cmp = (seq - NSA_CMP_BLOCK) // NSA_CMP_STRIDE + 1
    blk_idx = np.arange(n_cmp)[:, None] * NSA_CMP_STRIDE + np.arange(NSA_CMP_BLOCK)[None, :]
    kv_c = jnp.stack([k[0], v[0]])
    blocks = kv_c[:, :, :, blk_idx, :] + cmp_pos[:, None, None, None]
    flat = blocks.reshape(2, bsz, G, n_cmp, NSA_CMP_BLOCK * dh)
    hid = jax.nn.gelu(jnp.einsum('cbgnf,cfe->cbgne', flat, cmp_w1) + cmp_b1[:, None, None, None, :])
    comp = jnp.einsum('cbgne,cef->cbgnf', hid, cmp_w2)
    k_cmp, v_cmp = comp[0], comp[1]
    cmp_end = jnp.asarray(blk_idx[:, -1])

    n_sel = seq // NSA_SLC_BLOCK
    top_n = min(NSA_TOP_N, n_sel)
    c_start = np.arange(n_cmp) * NSA_CMP_STRIDE
    c_end = c_start + NSA_CMP_BLOCK - 1
    s_start = np.arange(n_sel) * NSA_SLC_BLOCK
    s_end = s_start + NSA_SLC_BLOCK - 1
    overlap = jnp.asarray(((c_start[:, None] <= s_end[None, :]) &
                           (c_end[:, None] >= s_start[None, :])).astype(np.float32))
    k_slc, v_slc = k[1], v[1]
    pad = ((0, 0), (0, 0), (NSA_WINDOW, 0), (0, 0))
    k_win, v_win = jnp.pad(k[2], pad), jnp.pad(v[2], pad)
    scale = dh ** -0.5
    sel_offsets = jnp.arange(NSA_SLC_BLOCK)
    blk_ids = jnp.arange(n_sel)
    gather = jax.vmap(jax.vmap(lambda arr, idx: arr[idx]))

    def chunk(c):
        q0 = c * NSA_Q_CHUNK
        t = q0 + jnp.arange(NSA_Q_CHUNK)
        qc = lax.dynamic_slice_in_dim(q, q0, NSA_Q_CHUNK, axis=2).reshape(bsz, G, R, NSA_Q_CHUNK, dh)
        s_c = jnp.einsum('bgrqd,bgnd->bgrqn', qc, k_cmp) * scale
        p_c = masked_softmax(s_c, cmp_end[None, :] <= t[:, None])
        o_c = jnp.einsum('bgrqn,bgnd->bgrqd', p_c, v_cmp)
        imp = jnp.einsum('bgrqn,ns->bgqs', p_c, overlap)
        cur = t // NSA_SLC_BLOCK
        valid = blk_ids[None, :] <= cur[:, None]
        forced = (blk_ids[None, :] == 0) | (blk_ids[None, :] >= cur[:, None] - (NSA_LOCAL_BLOCKS - 1))
        score = jnp.where(valid, jnp.where(forced, BIG, imp), -BIG)
        _, sel = lax.top_k(score, top_n)
        tok = (sel[..., None] * NSA_SLC_BLOCK + sel_offsets).reshape(bsz, G, -1)
        k_s = gather(k_slc, tok).reshape(bsz, G, NSA_Q_CHUNK, top_n * NSA_SLC_BLOCK, dh)
        v_s = gather(v_slc, tok).reshape(bsz, G, NSA_Q_CHUNK, top_n * NSA_SLC_BLOCK, dh)
        tok = tok.reshape(bsz, G, 1, NSA_Q_CHUNK, top_n * NSA_SLC_BLOCK)
        s_s = jnp.einsum('bgrqd,bgqkd->bgrqk', qc, k_s) * scale
        p_s = masked_softmax(s_s, tok <= t[:, None])
        o_s = jnp.einsum('bgrqk,bgqkd->bgrqd', p_s, v_s)
        kw = lax.dynamic_slice_in_dim(k_win, q0, NSA_Q_CHUNK + NSA_WINDOW, axis=2)
        vw = lax.dynamic_slice_in_dim(v_win, q0, NSA_Q_CHUNK + NSA_WINDOW, axis=2)
        kpos = q0 - NSA_WINDOW + jnp.arange(NSA_Q_CHUNK + NSA_WINDOW)
        rel = t[:, None] - kpos[None, :]
        mask_w = (rel >= 0) & (rel < NSA_WINDOW) & (kpos[None, :] >= 0)
        s_w = jnp.einsum('bgrqd,bgkd->bgrqk', qc, kw) * scale
        p_w = masked_softmax(s_w, mask_w)
        o_w = jnp.einsum('bgrqk,bgkd->bgrqd', p_w, vw)
        g = lax.dynamic_slice_in_dim(gates, q0, NSA_Q_CHUNK, axis=1)
        g = g.transpose(2, 0, 3, 1).reshape(3, bsz, G, R, NSA_Q_CHUNK, 1)
        return g[0] * o_c + g[1] * o_s + g[2] * o_w

    o = lax.map(chunk, jnp.arange(seq // NSA_Q_CHUNK))
    o = o.transpose(1, 0, 4, 2, 3, 5).reshape(bsz, seq, H * dh)
    return o.astype(h.dtype) @ w_out

def _linear_recurrence(e1, e2):
    a1, b1 = e1
    a2, b2 = e2
    return a1 * a2, a2 * b1 + b2

def s5_ssm(h, lam_re, lam_im, log_step, b_re, b_im, c_re, c_im, d_skip, w_glu, b_glu):
    bsz, seq, _ = h.shape
    f32 = jnp.float32
    lam = lax.complex(lam_re.astype(f32), lam_im.astype(f32))
    step = jnp.exp(log_step.astype(f32))[:, None]
    lam_bar = jnp.exp(lam * step)
    b_bar = ((lam_bar - 1.0) / lam)[:, :, None] * lax.complex(b_re.astype(f32), b_im.astype(f32))
    c_mat = lax.complex(c_re.astype(f32), c_im.astype(f32))

    def run_sequence(u):
        ug = u.astype(f32).reshape(seq, S5_N_GROUPS, S5_GROUP)
        bu = jnp.einsum('gpc,sgc->sgp', b_bar, ug)
        a = jnp.broadcast_to(lam_bar, bu.shape)
        _, states = lax.associative_scan(_linear_recurrence, (a, bu), axis=0)
        return jnp.einsum('gcp,sgp->sgc', c_mat, states).real.reshape(seq, D_MODEL)

    y = lax.map(run_sequence, h) + d_skip.astype(f32) * h.astype(f32)
    y = jax.nn.gelu(y).astype(h.dtype)
    a, g = jnp.split(y @ w_glu + b_glu, 2, axis=-1)
    return a * jax.nn.sigmoid(g)

def multiscale_pool(h, w_grp, scale):
    bsz, seq, _ = h.shape
    f32 = jnp.float32
    hf = h.astype(f32)
    csum = jnp.concatenate([jnp.zeros((bsz, 1, D_MODEL), f32), lax.cumsum(hf, axis=1)], axis=1)
    t = jnp.arange(seq)
    outs = []
    for gi, win in enumerate(POOL_WINDOWS):
        lo, hi = gi * POOL_GROUP, (gi + 1) * POOL_GROUP
        start = jnp.maximum(t + 1 - win, 0)
        cnt = (t + 1 - start).astype(f32)[None, :, None]
        pooled = (csum[:, 1:, lo:hi] - csum[:, start, lo:hi]) / cnt - hf[:, :, lo:hi]
        outs.append(jnp.einsum('bsc,cd->bsd', pooled, w_grp[gi].astype(f32)))
    return (jnp.concatenate(outs, axis=-1) * scale.astype(f32)).astype(h.dtype)

def first_inputs(seed: int = 0) -> dict:
    key = jax.random.key(seed)
    keys = iter(jax.random.split(key, 64))
    f32 = jnp.float32

    def nrm(shape, s):
        return jax.random.normal(next(keys), shape, f32) * s

    nA, nB, nC, nD = [_n_layers_of(m) for m in range(N_MIXERS)]
    D, F = D_MODEL, D_FF
    H, G, dh, L = NSA_HEADS, NSA_KV_GROUPS, NSA_HEAD_DIM, NSA_CMP_BLOCK
    Gs, P, C = S5_N_GROUPS, S5_STATE, S5_GROUP
    inv2 = math.sqrt(0.5)
    return {
        'x': nrm((BATCH, SEQ, D), 1.0),
        'positions': jnp.arange(SEQ, dtype=jnp.int32),
        'norm_mix': 1.0 + nrm((DEPTH, D), 0.02),
        'norm_ffn': 1.0 + nrm((DEPTH, D), 0.02),
        'ffn_w_in': nrm((DEPTH, D, 2 * F), D ** -0.5),
        'ffn_w_out': nrm((DEPTH, F, D), F ** -0.5),
        'conv_w_in': nrm((nA, D, 2 * D), D ** -0.5),
        'conv_b_in': nrm((nA, 2 * D), 0.02),
        'conv_w_dw': nrm((nA, CONV_WIDTH, D), CONV_WIDTH ** -0.5),
        'conv_b_dw': nrm((nA, D), 0.02),
        'conv_ln_g': 1.0 + nrm((nA, D), 0.02),
        'conv_ln_b': nrm((nA, D), 0.02),
        'conv_w_out': nrm((nA, D, D), D ** -0.5),
        'nsa_w_in': nrm((nB, D, NSA_PROJ), D ** -0.5),
        'nsa_q_gain': 1.0 + nrm((nB, dh), 0.02),
        'nsa_k_gain': 1.0 + nrm((nB, 3, dh), 0.02),
        'nsa_cmp_pos': nrm((nB, 2, L, dh), 0.02),
        'nsa_cmp_w1': nrm((nB, 2, L * dh, dh), (L * dh) ** -0.5),
        'nsa_cmp_b1': nrm((nB, 2, dh), 0.02),
        'nsa_cmp_w2': nrm((nB, 2, dh, dh), dh ** -0.5),
        'nsa_w_out': nrm((nB, H * dh, D), (H * dh) ** -0.5),
        's5_lam_re': jnp.full((nC, Gs, P), -0.5, f32),
        's5_lam_im': jnp.broadcast_to(math.pi * jnp.arange(P, dtype=f32), (nC, Gs, P)),
        's5_log_step': jax.random.uniform(next(keys), (nC, Gs), f32, math.log(1e-3), math.log(1e-1)),
        's5_b_re': nrm((nC, Gs, P, C), inv2 * C ** -0.5),
        's5_b_im': nrm((nC, Gs, P, C), inv2 * C ** -0.5),
        's5_c_re': nrm((nC, Gs, C, P), inv2 * P ** -0.5),
        's5_c_im': nrm((nC, Gs, C, P), inv2 * P ** -0.5),
        's5_d': nrm((nC, D), 0.5),
        's5_w_glu': nrm((nC, D, 2 * D), D ** -0.5),
        's5_b_glu': nrm((nC, 2 * D), 0.02),
        'pool_w': nrm((nD, len(POOL_WINDOWS), POOL_GROUP, POOL_GROUP), POOL_GROUP ** -0.5),
        'pool_scale': 1.0 + nrm((nD, D), 0.05),
    }

def first_block(x, positions, norm_mix, norm_ffn, ffn_w_in, ffn_w_out,
              conv_w_in, conv_b_in, conv_w_dw, conv_b_dw, conv_ln_g, conv_ln_b, conv_w_out,
              nsa_w_in, nsa_q_gain, nsa_k_gain, nsa_cmp_pos, nsa_cmp_w1, nsa_cmp_b1, nsa_cmp_w2, nsa_w_out,
              s5_lam_re, s5_lam_im, s5_log_step, s5_b_re, s5_b_im, s5_c_re, s5_c_im, s5_d, s5_w_glu, s5_b_glu,
              pool_w, pool_scale):
    for i in range(DEPTH):
        m, j = i % N_MIXERS, i // N_MIXERS
        h = rmsnorm(x, norm_mix[i])
        if m == 0:
            y = conformer_conv_module(h, conv_w_in[j], conv_b_in[j], conv_w_dw[j], conv_b_dw[j],
                                      conv_ln_g[j], conv_ln_b[j], conv_w_out[j])
        elif m == 1:
            y = nsa_attention(h, positions, nsa_w_in[j], nsa_q_gain[j], nsa_k_gain[j], nsa_cmp_pos[j],
                              nsa_cmp_w1[j], nsa_cmp_b1[j], nsa_cmp_w2[j], nsa_w_out[j])
        elif m == 2:
            y = s5_ssm(h, s5_lam_re[j], s5_lam_im[j], s5_log_step[j], s5_b_re[j], s5_b_im[j],
                       s5_c_re[j], s5_c_im[j], s5_d[j], s5_w_glu[j], s5_b_glu[j])
        else:
            y = multiscale_pool(h, pool_w[j], pool_scale[j])
        x = x + y.astype(x.dtype)
        h = rmsnorm(x, norm_ffn[i])
        x = x + swiglu_ffn(h, ffn_w_in[i], ffn_w_out[i]).astype(x.dtype)
    return x


N_A_LAYERS = DEPTH // 2
N_B_LAYERS = DEPTH - N_A_LAYERS
N_META = 16
EPS = 1e-6
NEG_INF_2 = -1e30

D_FF_2 = 2816

GLA_HEADS = 4
GLA_DK = D_MODEL // 2 // GLA_HEADS
GLA_DV = D_MODEL // GLA_HEADS
GLA_QK = GLA_HEADS * GLA_DK
GLA_V = GLA_HEADS * GLA_DV
GLA_RANK = 16
GLA_TAU = 16.0
GLA_IN = 2 * GLA_QK + 2 * GLA_V + GLA_RANK
CHUNK = 64

N_Q_HEADS = 16
N_KV_HEADS = 4
HEAD_DIM = 64
GROUP = N_Q_HEADS // N_KV_HEADS
WINDOW = 128
ROT_DIM = HEAD_DIM // 4


def rmsnorm_2(x, g):
    xf = x.astype(jnp.float32)
    y = xf * lax.rsqrt(jnp.mean(xf * xf, axis=-1, keepdims=True) + EPS)
    return (y * g.astype(jnp.float32)).astype(x.dtype)

def swiglu(x, w_in, w_out):
    gate, up = jnp.split(x @ w_in, 2, axis=-1)
    return (jax.nn.silu(gate) * up) @ w_out

def rope_tables(length):
    inv_freq = ROPE_THETA ** (-jnp.arange(0, ROT_DIM, 2, dtype=jnp.float32) / ROT_DIM)
    ang = jnp.arange(length, dtype=jnp.float32)[:, None] * inv_freq[None, :]
    return jnp.cos(ang), jnp.sin(ang)

def apply_partial_rope(x, cos, sin):
    half = ROT_DIM // 2
    shape = (cos.shape[0],) + (1,) * (x.ndim - 3) + (half,)
    c, s = cos.reshape(shape), sin.reshape(shape)
    x1 = x[..., :half].astype(jnp.float32)
    x2 = x[..., half:ROT_DIM].astype(jnp.float32)
    return jnp.concatenate([(x1 * c - x2 * s).astype(x.dtype), (x2 * c + x1 * s).astype(x.dtype),
                            x[..., ROT_DIM:]], axis=-1)

def gla_mixer(hn, w_in, w_gate, b_gate, g_head, w_out):
    B, L, _ = hn.shape
    q, k, v, r, lr = jnp.split(hn @ w_in, [GLA_QK, 2 * GLA_QK, 2 * GLA_QK + GLA_V, 2 * GLA_QK + 2 * GLA_V], axis=-1)
    gk = jax.nn.log_sigmoid((lr @ w_gate + b_gate).astype(jnp.float32)) / GLA_TAU
    pad = CHUNK - N_META
    padf = lambda t: jnp.pad(t, ((0, 0), (pad, 0), (0, 0)))
    Lp = L + pad
    nC = Lp // CHUNK
    def chunks(t, d):
        return t.reshape(B, nC, CHUNK, GLA_HEADS, d).transpose(0, 3, 1, 2, 4)
    qf = chunks(padf(q).astype(jnp.float32), GLA_DK) * (GLA_DK ** -0.5)
    kf = chunks(padf(k).astype(jnp.float32), GLA_DK)
    vf = chunks(padf(v).astype(jnp.float32), GLA_DV)
    bcum = jnp.cumsum(chunks(padf(gk), GLA_DK), axis=3)
    q_dec = qf * jnp.exp(bcum)
    k_dec = kf * jnp.exp(-bcum)
    causal = jnp.tril(jnp.ones((CHUNK, CHUNK), dtype=bool))
    att = jnp.where(causal, jnp.einsum('bhncd,bhnsd->bhncs', q_dec, k_dec), 0.0)
    o_intra = jnp.einsum('bhncs,bhnsv->bhncv', att, vf)
    b_last = bcum[:, :, :, -1:, :]
    chunk_kv = jnp.einsum('bhnsd,bhnsv->bhndv', kf * jnp.exp(b_last - bcum), vf)
    decay = jnp.exp(b_last[:, :, :, 0, :])

    def step(S, inp):
        kv_c, dec_c = inp
        return dec_c[..., None] * S + kv_c, S
    S0 = jnp.zeros((B, GLA_HEADS, GLA_DK, GLA_DV), jnp.float32)
    _, states = lax.scan(step, S0, (jnp.moveaxis(chunk_kv, 2, 0), jnp.moveaxis(decay, 2, 0)))
    states = jnp.moveaxis(states, 0, 2)
    o = o_intra + jnp.einsum('bhncd,bhndv->bhncv', q_dec, states)
    o = o.reshape(B, GLA_HEADS, Lp, GLA_DV)[:, :, pad:].transpose(0, 2, 1, 3)
    o = rmsnorm_2(o, g_head) * jax.nn.silu(r.astype(jnp.float32)).reshape(B, L, GLA_HEADS, GLA_DV)
    return o.reshape(B, L, GLA_V).astype(hn.dtype) @ w_out

def shared_kv(h, g_kv, w_kv, cos, sin):
    B, L, _ = h.shape
    k, v = jnp.split(rmsnorm_2(h, g_kv) @ w_kv, 2, axis=-1)
    k = apply_partial_rope(k.reshape(B, L, N_KV_HEADS, HEAD_DIM), cos, sin)
    v = v.reshape(B, L, N_KV_HEADS, HEAD_DIM)
    return k.transpose(0, 2, 1, 3), v.transpose(0, 2, 1, 3)

def sink_softmax(s, mask, sink):
    s = jnp.where(mask, s.astype(jnp.float32), NEG_INF_2)
    m = jnp.maximum(jnp.max(s, axis=-1, keepdims=True), sink)
    p = jnp.exp(s - m)
    return p / (jnp.sum(p, axis=-1, keepdims=True) + jnp.exp(sink - m))

def swa_mixer(hn, w_q, sinks, w_out, k, v, cos, sin):
    B, L, _ = hn.shape
    S = L - N_META
    nB = S // WINDOW
    q = (hn @ w_q).reshape(B, L, N_KV_HEADS, GROUP, HEAD_DIM)
    q = (apply_partial_rope(q, cos, sin) * (HEAD_DIM ** -0.5)).transpose(0, 2, 3, 1, 4)
    sink_b = sinks.reshape(N_KV_HEADS, GROUP).astype(jnp.float32)
    k_meta, v_meta = k[:, :, :N_META], v[:, :, :N_META]
    s_meta = jnp.einsum('bkgqd,bkmd->bkgqm', q[:, :, :, :N_META], k_meta)
    p_meta = sink_softmax(s_meta, jnp.tril(jnp.ones((N_META, N_META), dtype=bool)), sink_b[None, :, :, None, None])
    o_meta = jnp.einsum('bkgqm,bkmd->bkgqd', p_meta.astype(v.dtype), v_meta)
    q_blk = q[:, :, :, N_META:].reshape(B, N_KV_HEADS, GROUP, nB, WINDOW, HEAD_DIM)
    def band(t):
        t_meta = t[:, :, :N_META]
        t_blk = t[:, :, N_META:].reshape(B, N_KV_HEADS, nB, WINDOW, HEAD_DIM)
        prev = jnp.concatenate([jnp.zeros_like(t_blk[:, :, :1]), t_blk[:, :, :-1]], axis=2)
        meta = jnp.broadcast_to(t_meta[:, :, None], (B, N_KV_HEADS, nB, N_META, HEAD_DIM))
        return jnp.concatenate([meta, prev, t_blk], axis=3)
    k_band, v_band = band(k), band(v)
    s = jnp.einsum('bkgnqd,bknsd->bkgnqs', q_blk, k_band)
    i = jnp.arange(WINDOW)[:, None]
    j = jnp.arange(WINDOW)[None, :]
    blk = jnp.arange(nB)[:, None, None]
    mask = jnp.concatenate([
        jnp.ones((nB, WINDOW, N_META), dtype=bool),
        (j > i)[None] & (blk > 0),
        jnp.broadcast_to((j <= i)[None], (nB, WINDOW, WINDOW)),
    ], axis=-1)
    p = sink_softmax(s, mask, sink_b[None, :, :, None, None, None])
    o_real = jnp.einsum('bkgnqs,bknsd->bkgnqd', p.astype(v.dtype), v_band).reshape(B, N_KV_HEADS, GROUP, S, HEAD_DIM)
    o = jnp.concatenate([o_meta, o_real], axis=3).transpose(0, 3, 1, 2, 4).reshape(B, L, N_Q_HEADS * HEAD_DIM)
    return o @ w_out

def second_inputs(seed: int = 0) -> dict:
    key = jax.random.key(seed)
    ks = jax.random.split(key, 16)
    nrm = lambda k, shape, fan_in: jax.random.normal(k, shape, jnp.float32) * (fan_in ** -0.5)
    return {
        "x": jax.random.normal(ks[0], (BATCH, SEQ, D_MODEL), jnp.float32),
        "meta_tokens": jax.random.normal(ks[1], (N_META, D_MODEL), jnp.float32),
        "norm_gains": 1.0 + 0.02 * jax.random.normal(ks[2], (DEPTH, 6, D_MODEL), jnp.float32),
        "w_ffn_in": nrm(ks[3], (DEPTH, 2, D_MODEL, 2 * D_FF_2), D_MODEL),
        "w_ffn_out": nrm(ks[4], (DEPTH, 2, D_FF_2, D_MODEL), D_FF_2),
        "gla_w_in": nrm(ks[5], (N_A_LAYERS, D_MODEL, GLA_IN), D_MODEL),
        "gla_w_gate": nrm(ks[6], (N_A_LAYERS, GLA_RANK, GLA_QK), GLA_RANK),
        "gla_b_gate": 0.1 * jax.random.normal(ks[7], (N_A_LAYERS, GLA_QK), jnp.float32),
        "gla_norm": 1.0 + 0.02 * jax.random.normal(ks[8], (N_A_LAYERS, GLA_DV), jnp.float32),
        "gla_w_out": nrm(ks[9], (N_A_LAYERS, GLA_V, D_MODEL), GLA_V),
        "kv_norm": 1.0 + 0.02 * jax.random.normal(ks[10], (D_MODEL,), jnp.float32),
        "w_kv": nrm(ks[11], (D_MODEL, 2 * N_KV_HEADS * HEAD_DIM), D_MODEL),
        "swa_w_q": nrm(ks[12], (N_B_LAYERS, D_MODEL, N_Q_HEADS * HEAD_DIM), D_MODEL),
        "swa_sinks": 0.5 * jax.random.normal(ks[13], (N_B_LAYERS, N_Q_HEADS), jnp.float32),
        "swa_w_out": nrm(ks[14], (N_B_LAYERS, N_Q_HEADS * HEAD_DIM, D_MODEL), N_Q_HEADS * HEAD_DIM),
    }

def second_block(x, meta_tokens, norm_gains, w_ffn_in, w_ffn_out, gla_w_in, gla_w_gate, gla_b_gate, gla_norm,
              gla_w_out, kv_norm, w_kv, swa_w_q, swa_sinks, swa_w_out):
    B = x.shape[0]
    meta = jnp.broadcast_to(meta_tokens.astype(x.dtype)[None], (B, N_META, D_MODEL))
    h = jnp.concatenate([meta, x], axis=1)
    cos, sin = rope_tables(h.shape[1])
    k_sh, v_sh = None, None
    for layer in range(DEPTH):
        g = norm_gains[layer]
        h = h + 0.5 * rmsnorm_2(swiglu(rmsnorm_2(h, g[0]), w_ffn_in[layer, 0], w_ffn_out[layer, 0]), g[1])
        hn = rmsnorm_2(h, g[2])
        if layer < N_A_LAYERS:
            a = layer
            mix = gla_mixer(hn, gla_w_in[a], gla_w_gate[a], gla_b_gate[a], gla_norm[a], gla_w_out[a])
        else:
            b = layer - N_A_LAYERS
            mix = swa_mixer(hn, swa_w_q[b], swa_sinks[b], swa_w_out[b], k_sh, v_sh, cos, sin)
        h = h + rmsnorm_2(mix, g[3])
        h = h + 0.5 * rmsnorm_2(swiglu(rmsnorm_2(h, g[4]), w_ffn_in[layer, 1], w_ffn_out[layer, 1]), g[5])
        if layer == N_A_LAYERS - 1:
            k_sh, v_sh = shared_kv(h, kv_norm, w_kv, cos, sin)
    return h[:, N_META:]


def setup_inputs(seed=0):
    out = dict(first_inputs(seed))
    for name, value in second_inputs(seed + 1).items():
        if name != "x":
            out[name + "_2"] = value
    return out


def reference(
    x, positions, norm_mix, norm_ffn, ffn_w_in, ffn_w_out, conv_w_in, conv_b_in, conv_w_dw,
    conv_b_dw, conv_ln_g, conv_ln_b, conv_w_out, nsa_w_in, nsa_q_gain, nsa_k_gain, nsa_cmp_pos,
    nsa_cmp_w1, nsa_cmp_b1, nsa_cmp_w2, nsa_w_out, s5_lam_re, s5_lam_im, s5_log_step, s5_b_re,
    s5_b_im, s5_c_re, s5_c_im, s5_d, s5_w_glu, s5_b_glu, pool_w, pool_scale, meta_tokens_2,
    norm_gains_2, w_ffn_in_2, w_ffn_out_2, gla_w_in_2, gla_w_gate_2, gla_b_gate_2, gla_norm_2,
    gla_w_out_2, kv_norm_2, w_kv_2, swa_w_q_2, swa_sinks_2, swa_w_out_2,
):
    x = first_block(
        x, positions, norm_mix, norm_ffn, ffn_w_in, ffn_w_out, conv_w_in, conv_b_in, conv_w_dw,
        conv_b_dw, conv_ln_g, conv_ln_b, conv_w_out, nsa_w_in, nsa_q_gain, nsa_k_gain,
        nsa_cmp_pos, nsa_cmp_w1, nsa_cmp_b1, nsa_cmp_w2, nsa_w_out, s5_lam_re, s5_lam_im,
        s5_log_step, s5_b_re, s5_b_im, s5_c_re, s5_c_im, s5_d, s5_w_glu, s5_b_glu, pool_w,
        pool_scale,
    )
    return second_block(
        x, meta_tokens_2, norm_gains_2, w_ffn_in_2, w_ffn_out_2, gla_w_in_2, gla_w_gate_2,
        gla_b_gate_2, gla_norm_2, gla_w_out_2, kv_norm_2, w_kv_2, swa_w_q_2, swa_sinks_2,
        swa_w_out_2,
    )


_drawn_inputs = setup_inputs


def setup_inputs(seed=0):
    import zlib

    import numpy as np

    out = dict(_drawn_inputs(seed))
    spreads = {}
    factors = {'nsa_q_gain': 8.0,
     'nsa_k_gain': 8.0,
     'nsa_cmp_pos': 6.304,
     'nsa_cmp_b1': 5.514,
     'gla_norm_2': 14.813,
     'kv_norm_2': 14.544,
     'swa_sinks_2': 48.154}
    for name, (base, spread) in spreads.items():
        noise = np.random.default_rng([zlib.crc32(name.encode()), seed]).standard_normal(out[name].shape)
        drawn = base * np.exp(spread * noise) if base else spread * noise
        out[name] = __import__('jax').numpy.asarray(drawn.astype(out[name].dtype))
    for name, factor in factors.items():
        out[name] = (out[name] * factor).astype(out[name].dtype)
    return out
```

```python
from contextlib import ExitStack

import numpy as np_

import concourse.bass as bass
from concourse import mybir

ALU = mybir.AluOpType
ACT = mybir.ActivationFunctionType
AX = mybir.AxisListType
F32 = mybir.dt.float32
F32R = mybir.dt.float32r
I32 = mybir.dt.int32

P = 128
D = 1024
KD = D // P
SEQ = 256
META = 16
L = SEQ + META
FF = 2816
KF = FF // P
KF_PARTS = -(-KF // KD)
RING = 4
CONV = 31
BIG = 1e30
ROPE = 16
THETA = 500000.0
DH = 64
TWO_PI = (6.28125, 0.0019350051879882812, 3.019915981956752e-07)
PI_BELOW = 3.1415925
HALF_PI = 1.5707963267948966
NCMP = (SEQ - 32) // 16 + 1

FFN_A, FFN_B = 2 * KF, KD * KF_PARTS
STAGES = [("conv_in", 16), ("conv_out", 8), ("ffn0_a", FFN_A), ("ffn0_b", FFN_B),
          ("nsa_kv", 12), ("nsa_gate", 1), ("nsa_q", 8), ("nsa_out", 8), ("ffn1_a", FFN_A), ("ffn1_b", FFN_B),
          ("ffn2_a", FFN_A), ("ffn2_b", FFN_B),
          ("gla_lr", 1), ("gla_k", 4), ("gla_q", 4), ("gla_v", 8), ("gla_r", 8), ("gla_out", 8),
          ("ffn3_a", FFN_A), ("ffn3_b", FFN_B), ("kv", 4),
          ("ffn4_a", FFN_A), ("ffn4_b", FFN_B), ("swa_q", 8), ("swa_out", 8),
          ("ffn5_a", FFN_A), ("ffn5_b", FFN_B)]
BASE, TILE, SIZE = {}, {}, {}
HALVES = TILES = 0
for _name, _n in STAGES:
    BASE[_name], TILE[_name], SIZE[_name] = HALVES, TILES, _n
    HALVES += _n
    TILES += _n // KF_PARTS if _name.endswith("_b") else _n

PARAMS = [("mix0", 8), ("ffn0", 8), ("mix1", 8), ("ffn1", 8),
          ("conv_ba", 8), ("conv_bg", 8), ("conv_w", 8 * CONV), ("conv_b", 8), ("ln_g", 8), ("ln_b", 8),
          ("q_gain", 1), ("k_gain", 3), ("cmp_b1", 2), ("cmp_pos", 64),
          ("g2", 96), ("kv_norm", 8), ("gate_b", 4), ("gla_norm", 2), ("sinks", 16),
          ("inv_freq", 1), ("rope_sign", 1)]
COL = {}
_c = 0
for _name, _n in PARAMS:
    COL[_name] = _c
    _c += _n
NPAR = _c

NEXT_GAIN = [COL["mix0"], COL["ffn0"], COL["mix1"], COL["ffn1"]] + \
            [COL["g2"] + 8 * g for g in (0, 2, 4)] + [COL["g2"] + 48 + 8 * g for g in (0, 2, 4)]
POST_GAIN = {u: COL["g2"] + 48 * (n // 3) + 8 * (1 + 2 * (n % 3)) for n, u in enumerate(range(5, 11))}


def last(name):
    return BASE[name] + SIZE[name]


class Half:

    def __init__(self, b, i=0):
        self.slot = b % RING
        self.round = b // RING + i
        self.n = b + RING * i


class Chain:

    def __init__(self, eng, sem):
        self.eng, self.sem, self.n, self.i, self.per, self.at = eng, sem, 0, None, 0, 0

    def __call__(self, ins):
        self.n += 1
        ins.then_inc(self.sem, 1)
        self.eng.wait_ge(self.sem, self.n if self.i is None else self.n + self.i * self.per)

    def enter(self, i, per):
        self.i, self.per, self.at = (None, 0, self.n) if isinstance(i, int) else (i, per, self.n)
        return self

    def leave(self, rounds):
        if self.i is not None:
            assert self.n - self.at == self.per, (self.n - self.at, self.per)
            self.n = self.at + self.per * rounds
            self.i = None

SCRATCH = 12360
UPDATES = 10
FFN_AFTER = {1: 0, 3: 1, 4: 2, 6: 3, 7: 4, 9: 5}


def build(nc, a, out, upto):
    with ExitStack() as ctx:
        def sb(name, shape, dt=F32):
            return ctx.enter_context(nc.sbuf_tensor(name, shape, dt))

        def sem(name):
            return ctx.enter_context(nc.semaphore(name))

        x = sb("x", [P, KD, L])
        xh, xl = sb("xh", [P, KD, L], F32R), sb("xl", [P, KD, L], F32R)
        sq = sb("sq", [P, KD, L])
        y = sb("y", [P, KD, L])
        sumsq, root, rx, ry = sb("sumsq", [P, L]), sb("root", [P, L]), sb("rx", [P, L]), sb("ry", [P, L])
        hh, hl = sb("hh", [P, KF, L], F32R), sb("hl", [P, KF, L], F32R)
        raw = sb("raw", [P, RING, KD * P])
        wh, wl = sb("wh", [P, RING, KD * P], F32R), sb("wl", [P, RING, KD * P], F32R)
        par = sb("par", [P, NPAR])
        tg, ts, tu, th = (sb(n, [P, 2, L]) for n in ("tg", "ts", "tu", "th"))
        ones = sb("ones", [P, P])
        eps = sb("eps", [P, 5])
        scr = sb("scr", [P, SCRATCH])

        acc = [ctx.enter_context(nc.psum_tensor(f"acc{i}", [P, 512], F32)) for i in range(4)]
        stat = ctx.enter_context(nc.psum_tensor("stat", [P, 512], F32))
        mix = [ctx.enter_context(nc.psum_tensor(f"mix{i}", [P, 512], F32)) for i in range(3)]

        const_ok = sem("const_ok")
        in_x, in_par, in_misc = sem("in_x"), sem("in_par"), sem("in_misc")
        raw_in = [sem(f"raw_in{i}") for i in range(RING)]
        w_hi, w_lo, used, acc_used = sem("w_hi"), sem("w_lo"), sem("used"), sem("acc_used")
        x_new, x_hi, x_lo = sem("x_new"), sem("x_hi"), sem("x_lo")
        sq_new, sum_ok, mean_ok, root_ok, rms_ok = (sem(n) for n in ("sq_new", "sum_ok", "mean_ok", "root_ok", "rms_ok"))
        y_new, t_new = sem("y_new"), sem("t_new")
        f_g, f_s, f_h, f_hi, f_lo = (sem(n) for n in ("f_g", "f_s", "f_h", "f_hi", "f_lo"))
        m_hi, m_lo = sem("m_hi"), sem("m_lo")
        out_ok = sem("out_ok")
        dve_step, act_step, pool_step = sem("dve_step"), sem("act_step"), sem("pool_step")

        def col(name, k=0):
            c = (COL[name] if isinstance(name, str) else name) + k
            return par[:, c:c + 1]

        def c0(u):
            return 0 if 4 <= u <= 7 else META

        def cg(u):
            return max(c0(u), c0(u + 1))

        def norm_of(u, post=False):
            return u if u < 5 else 5 + 2 * (u - 5) + (not post)

        def bank(name, t):
            return acc[(TILE[name] + t) % 4]

        mixers = {}
        cu = scr[:, 0:KD * (SEQ + CONV - 1)].rearrange("p (k t) -> p k t", k=KD)
        _o = KD * (SEQ + CONV - 1)
        cv = scr[:, _o:_o + KD * SEQ].rearrange("p (k t) -> p k t", k=KD)
        _o += KD * SEQ
        cw = scr[:, _o:_o + 2 * SEQ].rearrange("p (k t) -> p k t", k=2)
        c_g, c_s, c_v, c_mu, c_d, c_sq, c_var, c_root, c_z, c_w, c_pad, c_tap = (
            sem(n) for n in ("c_g", "c_s", "c_v", "c_mu", "c_d", "c_sq", "c_var", "c_root", "c_z", "c_w", "c_pad", "c_tap"))

        def conv_pool(pool, step):
            pool.memset(cu[:, :, 0:CONV - 1], 0.0).then_inc(c_pad, 1)

        def conv_pe(pe, gemm):
            gemm("conv_in", xh, xl, META, (x_lo, 0))
            for j in range(KD):
                pe.wait_ge(c_v, j + 1)
                ins = nc.tensor.matmul(mix[0][:, 0:SEQ], ones[:], cv[:, j, :], start=(j == 0), stop=(j == KD - 1))
            ins.then_inc(c_mu, 1)
            for j in range(KD):
                pe.wait_ge(c_sq, j + 1)
                ins = nc.tensor.matmul(mix[1][:, 0:SEQ], ones[:], sq[:, j, META:], start=(j == 0), stop=(j == KD - 1))
            ins.then_inc(c_var, 1)
            gemm("conv_out", hh, hl, META, (m_lo, 0))

        def conv_act(act, step, ahead, residual, post_norm):
            for j in range(KD):
                b = BASE["conv_in"] + 2 * j
                ahead(b)
                act.wait_ge(c_g, j + 1)
                if j >= 2:
                    act.wait_ge(c_v, j - 1)
                nc.scalar.activation(ts[:, j % 2, META:], tg[:, j % 2, META:], ACT.Sigmoid, bias=col("conv_bg", j)).then_inc(c_s, 1)
                ahead(b + 1)
            act.wait_ge(sum_ok, 1)
            for j in range(KD):
                act.wait_ge(c_d, j + 1)
                nc.scalar.activation(sq[:, j, META:], cv[:, j, :], ACT.Square).then_inc(c_sq, 1)
            act.wait_ge(c_var, 1)
            act.wait_ge(rms_ok, 1)
            nc.scalar.activation(root[:, META:], mix[1][:, 0:SEQ], ACT.Sqrt, bias=eps[:, 2:3]).then_inc(c_root, 1)
            for j in range(KD):
                act.wait_ge(c_z, j + 1)
                nc.scalar.activation(cv[:, j, :], cv[:, j, :], ACT.Silu, scale=col("ln_g", j), bias=col("ln_b", j)).then_inc(c_w, 1)
                act.wait_ge(c_w, j + 1)
                nc.scalar.activation(hh[:, j, META:], cv[:, j, :], ACT.Copy).then_inc(m_hi, 1)
            for m in range(KD):
                ahead(BASE["conv_out"] + m)
                residual(1, m)

        def conv_dve(dve, step, ahead, tail, post_norm):
            taps = 0

            def low(j):
                dve.wait_ge(m_hi, j + 1)
                nc.vector.tensor_tensor(hl[:, j, META:], cv[:, j, :], hh[:, j, META:].bitcast(F32), ALU.subtract).then_inc(m_lo, 1)

            for j in range(KD):
                b = BASE["conv_in"] + 2 * j
                dve.wait_ge(used, b + 1)
                step(nc.vector.tensor_tensor(tu[:, j % 2, META:], bank("conv_in", 2 * j)[:, 0:SEQ], rx[:, META:], ALU.mult))
                ahead(b)
                dve.wait_ge(used, b + 2)
                nc.vector.tensor_tensor(tg[:, j % 2, META:], bank("conv_in", 2 * j + 1)[:, 0:SEQ], rx[:, META:], ALU.mult).then_inc(c_g, 1)
                dve.wait_ge(c_g, j + 1)
                dve.sem_inc(acc_used, 2)
                ahead(b + 1)
                dve.wait_ge(c_s, j + 1)
                dve.wait_ge(c_pad, 1)
                step(nc.vector.scalar_tensor_tensor(cu[:, j, CONV - 1:], tu[:, j % 2, META:], col("conv_ba", j),
                                                    ts[:, j % 2, META:], ALU.add, ALU.mult))
                for n in range(CONV):
                    if n >= 2:
                        dve.wait_ge(c_tap, taps - 1)
                    w = col("conv_w", CONV * j + n)
                    if n == 0:
                        ins = nc.vector.tensor_scalar(cw[:, 0, :], cu[:, j, 0:SEQ], w, col("conv_b", j), ALU.mult, ALU.add)
                    elif n == 1:
                        ins = nc.vector.tensor_scalar(cw[:, 1, :], cu[:, j, 1:1 + SEQ], w, None, ALU.mult)
                    else:
                        ins = nc.vector.scalar_tensor_tensor(cw[:, n % 2, :], cu[:, j, n:n + SEQ], w, cw[:, n % 2, :], ALU.mult, ALU.add)
                    ins.then_inc(c_tap, 1)
                    taps += 1
                dve.wait_ge(c_tap, taps)
                nc.vector.tensor_tensor(cv[:, j, :], cw[:, 0, :], cw[:, 1, :], ALU.add).then_inc(c_v, 1)
                dve.wait_ge(c_v, j + 1)
            dve.wait_ge(c_mu, 1)
            for j in range(KD):
                nc.vector.tensor_tensor(cv[:, j, :], cv[:, j, :], mix[0][:, 0:SEQ], ALU.subtract).then_inc(c_d, 1)
            dve.wait_ge(c_root, 1)
            step(nc.vector.reciprocal(ry[:, META:], root[:, META:]))
            for j in range(KD):
                dve.wait_ge(c_sq, j + 1)
                nc.vector.tensor_tensor(cv[:, j, :], cv[:, j, :], ry[:, META:], ALU.mult).then_inc(c_z, 1)
                if j:
                    low(j - 1)
            low(KD - 1)
            for m in range(KD):
                tail(1, m, "conv_out", BASE["conv_out"] + m)

        mixers.setdefault("pool", {})[0] = conv_pool
        mixers.setdefault("pe", {})[0] = conv_pe
        mixers.setdefault("act", {})[0] = conv_act
        mixers.setdefault("dve", {})[0] = conv_dve
        ident, rot, bones, rowmask = sb("ident", [P, P]), sb("rot", [P, P]), sb("bones", [P, P]), sb("rowmask", [P, 4])
        cosT, sinT = sb("cosT", [P, SEQ + L]), sb("sinT", [P, SEQ + L])
        tab_ok, in_pos, shape_ok = sem("tab_ok"), sem("in_pos"), sem("shape_ok")
        tpos, tang, tint, tred = (scr[:, 6000 + n * 528:6528 + n * 528] for n in range(4))

        def tables_pool(pool, step):
            pool.iota(tpos[:, SEQ:], [[1, L]], base=0, channel_multiplier=0, allow_small_or_imprecise_dtypes=True).then_inc(tab_ok, 1)
            pool.dma_start(tint[:, 0:SEQ].bitcast(I32), a["positions"].partition_broadcast(P)).then_inc(in_pos, 16)
            step(pool.memset(ident[:], 0.0))
            step(pool.memset(rot[:], 0.0))
            step(pool.memset(bones[:], 0.0))
            step(pool.memset(rowmask[:], 0.0))
            shapes = [0]

            def shape(ins):
                shapes[0] += 1
                ins.then_inc(shape_ok, 1)
                pool.wait_ge(shape_ok, shapes[0])

            shape(pool.affine_select(out=ident[:], in_=ident[:], compare_op=ALU.not_equal, fill=1.0, base=0,
                                     pattern=[[-1, P]], channel_multiplier=1))
            for h in range(2):
                for s in range(2):
                    v = rot[:, DH * h + 8 * s:DH * h + 8 * s + 8]
                    shape(pool.affine_select(out=v, in_=v, compare_op=ALU.not_equal, fill=1.0, base=-(DH * h + 8 * (1 - s)),
                                             pattern=[[-1, 8]], channel_multiplier=1))
                shape(pool.memset(bones[DH * h:DH * h + DH, DH * h:DH * h + DH], 1.0 / DH))
            for r in range(4):
                shape(pool.memset(rowmask[32 * r:32 * r + 32, r:r + 1], 1.0))

        def tables_dve(dve, step):
            dve.wait_ge(in_pos, 16)
            dve.wait_ge(in_par, 16)
            dve.wait_ge(tab_ok, 1)
            step(nc.vector.tensor_copy(tpos[:, 0:SEQ], tint[:, 0:SEQ].bitcast(I32)))
            step(nc.vector.tensor_scalar(tang, tpos, col("inv_freq"), None, ALU.mult))
            step(nc.vector.tensor_scalar(tint.bitcast(I32), tang, float(np_.float32(1 / (2 * np_.pi))), None, ALU.mult))
            step(nc.vector.tensor_copy(tred, tint.bitcast(I32)))
            for part in TWO_PI:
                step(nc.vector.scalar_tensor_tensor(tang, tred, -part, tang, ALU.mult, ALU.add))
            step(nc.vector.tensor_scalar(tang, tang, PI_BELOW, -PI_BELOW, ALU.min, ALU.max))
            nc.vector.scalar_tensor_tensor(tred, tang, -1.0, tang, ALU.mult, ALU.max).then_inc(tab_ok, 1)
            dve.wait_ge(tab_ok, 4)
            nc.vector.tensor_scalar(sinT[:], sinT[:], col("rope_sign"), None, ALU.mult).then_inc(tab_ok, 1)

        def tables_act(act):
            act.wait_ge(tab_ok, 2)
            nc.scalar.activation(sinT[:], tang, ACT.Sin).then_inc(tab_ok, 1)
            nc.scalar.activation(cosT[:], tred, ACT.Sin, scale=-1.0, bias=eps[:, 3:4]).then_inc(tab_ok, 1)

        at = {"o": 0}

        def area(n):
            at["o"] += n
            assert at["o"] <= SCRATCH, at["o"]
            return scr[:, at["o"] - n:at["o"]]

        nw1 = area(4096).rearrange("p (c l e) -> p c l e", c=2, l=32)
        nw2 = area(128).rearrange("p (c e) -> p c e", c=2)
        nk = area(1536).rearrange("p (m t) -> p m t", m=6)
        nvt = area(1024).rearrange("p (b n) -> p b n", b=2)
        ngate = area(96).rearrange("p (a n) -> p a n", a=2)
        nkc = area(32).rearrange("p (t n) -> p t n", t=2)
        nhk = area(64).rearrange("p (g n) -> p g n", g=4)
        nhv = area(512).rearrange("p (g r n) -> p g r n", g=4, r=4)
        nvc = area(1024).rearrange("p (g r d) -> p g r d", g=4, r=4)
        nmask = area(384)
        ncm = area(32).rearrange("p (a n) -> p a n", a=2)
        nc01 = area(32).rearrange("p (a n) -> p a n", a=2)
        nbias = area(2)
        nstat = area(64)
        nroot = area(512).rearrange("p (b t) -> p b t", b=2)
        nr = area(256)
        nt = area(256)
        _sm = area(2304)
        nsq = _sm[:, 0:2048].rearrange("p (m t) -> p m t", m=8)
        nS, nP, nPT = (_sm[:, 768 * n:768 * n + 768].rearrange("p (b n) -> p b n", b=2) for n in range(3))
        nq = sq[:, :, META:]
        nv = y[:, :, META:]
        npc = scr[:, 0:1024].rearrange("p (h b n) -> p h b n", h=2, b=4)
        npct = scr[:, 1024:2048].rearrange("p (h t q) -> p h t q", h=2, t=2)
        ncs = scr[:, 2048:2560].rearrange("p (h a n) -> p h a n", h=2, a=2)
        n_w, n_a, n_v, n_gate, n_sig, n_sq, n_mean, n_root, n_n, n_perm, n_k = (
            sem("n_" + s) for s in ("w", "a", "v", "gate", "sig", "sq", "mean", "root", "n", "perm", "k"))
        n_mask, n_tr, n_vt, n_gt, n_hid, n_pos, n_gelu, n_comp, n_kc, n_vc = (
            sem("n_" + s) for s in ("mask", "tr", "vt", "gt", "hid", "pos", "gelu", "comp", "kc", "vc"))
        n_cs, n_cexp, n_csub, n_cp, n_ct, n_cpt = (sem("n_" + s) for s in ("cs", "cexp", "csub", "cp", "ct", "cpt"))
        n_s, n_min, n_exp, n_p, n_pt, n_ptc, n_o = (sem("n_" + s) for s in ("s", "min", "exp", "p", "pt", "ptc", "o"))
        KTILES = (0, 1, 4, 5, 8, 9)
        VTILES = (2, 3, 6, 7, 10, 11)
        UNITS = [(j, h, b) for j in range(KD) for h in range(2) for b in range(2)]

        def nsa_pool(pool, step):
            pool.wait_ge(m_lo, 8)
            pool.dma_start(nw1, a["cmp_w1"].rearrange("p (c l e) -> p c l e", c=2, l=32)).then_inc(n_w, 16)
            pool.dma_start(nw2[0:DH], a["cmp_w2"].rearrange("p (c e) -> p c e", c=2)).then_inc(n_w, 16)
            step(pool.memset(nmask, 0.0))
            step(pool.memset(ncm, 0.0))
            step(pool.memset(nc01, 1.0))
            for s in (0, 256):
                pool.affine_select(out=nmask[:, s:s + P], in_=nmask[:, s:s + P], compare_op=ALU.is_ge, fill=BIG, base=0,
                                   pattern=[[-1, P]], channel_multiplier=1).then_inc(n_mask, 1)
            for m, fill in ((ncm, BIG), (nc01, 0.0)):
                pool.affine_select(out=m, in_=m, compare_op=ALU.is_ge, fill=fill, base=-31,
                                   pattern=[[P, 2], [-16, 16]], channel_multiplier=1).then_inc(n_mask, 1)
            pool.memset(nhk, 0.0).then_inc(n_mask, 1)
            pool.memset(nhv, 0.0).then_inc(n_mask, 1)

        def nsa_pe(pe, gemm):
            pe.wait_ge(shape_ok, 11)

            def mean(m):
                pe.wait_ge(n_sq, m + 1)
                if m >= 1:
                    pe.wait_ge(n_root, m if m < 6 else m - 3 if m >= 10 else 6)
                nc.tensor.matmul(mean_bank(m)[:, 0:SEQ], bones[:], nsq[:, m % 8, :], start=True, stop=True).then_inc(n_mean, 1)

            def perm(m):
                pe.wait_ge(n_n, m + 1)
                if m >= 2:
                    pe.wait_ge(n_k, m - 1)
                v = nk[:, m, :] if m < 6 else nq[:, m - 6, :]
                nc.tensor.matmul(mix[1 + m % 2][:, 0:SEQ], rot[:], v, start=True, stop=True).then_inc(n_perm, 1)

            gemm("nsa_kv", xh, xl, META, (x_lo, 16))
            gemm("nsa_gate", xh, xl, META, None)
            for m in range(KD):
                if m < 6:
                    mean(m)
                gemm("nsa_q", xh, xl, META, None, only=m)
                if m < 6:
                    perm(m)
            pe.wait_ge(acc_used, TILE["nsa_q"] + 8)
            for m in range(6, 10):
                mean(m)
            pe.wait_ge(n_sig, 1)
            for qt in range(2):
                ins = nc.tensor.transpose(stat[:, P * qt:P * qt + P], tg[:, 1, META + P * qt:META + P * qt + P], ident[:])
            ins.then_inc(n_tr, 1)
            perm(6)
            for m in range(10, 14):
                mean(m)
                perm(m - 3)
            pe.wait_ge(n_w, 32)
            pe.wait_ge(n_k, 2)
            pe.wait_ge(n_v, 2)
            pe.wait_ge(n_root, 14)
            for l in range(32):
                for c in range(2):
                    ins = nc.tensor.matmul(acc[2][0:DH, c:c + 1], nw1[0:DH, c, l, :], par[0:DH, COL["cmp_pos"] + 32 * c + l:COL["cmp_pos"] + 32 * c + l + 1],
                                           start=(l == 0 and c == 0), stop=(l == 31), skip_group_check=True)
            ins.then_inc(n_pos, 1)
            for h in range(2):
                for c in range(2):
                    src = (nk, nv)[c]
                    for l in range(32):
                        ins = nc.tensor.matmul(acc[h][0:DH, 32 * c:32 * c + 2 * NCMP], nw1[DH * h:DH * h + DH, c, l, :],
                                               src[DH * h:DH * h + DH, 0:2, l:l + 16 * (NCMP - 1) + 1:16],
                                               start=(l == 0), stop=(l == 31))
                ins.then_inc(n_hid, 1)
            for m in range(11, 14):
                perm(m)
            pe.wait_ge(n_v, 6)
            pe.wait_ge(n_gt, 1)
            for b in range(2):
                for kt in range(2):
                    for t in range(2):
                        ins = nc.tensor.transpose((stat, acc[3])[b][:, 256 * kt + P * t:256 * kt + P * t + P],
                                                  nv[:, 2 + 2 * b + t, P * kt:P * kt + P], ident[:])
                ins.then_inc(n_tr, 1)
            pe.wait_ge(n_gelu, 6)
            for h in range(2):
                for t in range(2):
                    nc.tensor.matmul(acc[2][DH * h:DH * h + DH, 16 * t:16 * t + 16], nw2[0:DH, 0, :], nhk[0:DH, 2 * t + h, :],
                                     start=(t == 0), stop=True, skip_group_check=True)
            for g in range(4):
                ins = nc.tensor.matmul(mix[0][:, DH * g:DH * g + DH], nhv[0:DH, g].rearrange("p r n -> p (r n)"), nw2[0:DH, 1, :],
                                       start=True, stop=True)
            ins.then_inc(n_comp, 1)
            pe.wait_ge(n_kc, 1)
            pe.wait_ge(n_k, 14)
            for h in range(2):
                for qt in range(2):
                    for j in range(KD):
                        ins = nc.tensor.matmul(acc[h][:, P * qt + 16 * j:P * qt + 16 * j + 16], nq[DH * h:DH * h + DH, j, P * qt:P * qt + P],
                                               nkc[DH * h:DH * h + DH, j // 4, :], start=True, stop=True)
                ins.then_inc(n_cs, 1)

            def scores(n):
                j, h, b = UNITS[n]
                if n >= 3:
                    pe.wait_ge(n_min, n - 2)
                else:
                    pe.wait_ge(n_csub, 2)
                for qt in range(2):
                    ins = nc.tensor.matmul(acc[n % 3][:, P * qt:P * qt + P * (qt + 1)], nq[DH * h:DH * h + DH, j, P * qt:P * qt + P],
                                           nk[DH * h:DH * h + DH, 2 + 2 * b + j // 4, 0:P * (qt + 1)], start=True, stop=True)
                ins.then_inc(n_s, 1)

            def turned(n):
                pe.wait_ge(n_p, n + 1)
                if n >= 2:
                    pe.wait_ge(n_ptc, n - 1)
                else:
                    pe.wait_ge(n_cpt, 4)
                dst = (acc[3], stat)[n % 2]
                for at_, src in ((0, 0), (P, P), (2 * P, 2 * P)):
                    ins = nc.tensor.transpose(dst[:, at_:at_ + P], nP[:, n % 2, src:src + P], ident[:])
                ins.then_inc(n_pt, 1)

            def values(n):
                j, h, b = UNITS[n]
                t = j // 4
                g = 2 * t + h
                dst = mix[j % 2][DH * h:DH * h + DH]
                if b == 0:
                    if j >= 2:
                        pe.wait_ge(m_lo, 8 + j - 1)
                    nc.tensor.matmul(dst[:, 0:SEQ], nvc[:, g, j % 4, :], npct[:, h, t, :], start=True, stop=False)
                pe.wait_ge(n_ptc, n + 1)
                nc.tensor.matmul(dst[:, 0:SEQ], nvt[:, b, DH * g:DH * g + DH], nPT[:, n % 2, 0:SEQ], start=False, stop=False)
                ins = nc.tensor.matmul(dst[:, P:SEQ], nvt[:, b, 256 + DH * g:256 + DH * g + DH], nPT[:, n % 2, SEQ:SEQ + P],
                                       start=False, stop=(b == 1))
                ins.then_inc(n_o, 1)

            scores(0)
            scores(1)
            pe.wait_ge(n_cp, 2)
            for h in range(2):
                for t in range(2):
                    pe.wait_ge(n_vt, 2)
                    if t == 1 or h == 1:
                        pe.wait_ge(n_cpt, 2 * h + t)
                    for qt in range(2):
                        ins = nc.tensor.transpose(stat[:, P * qt:P * qt + P], npc[:, h, 2 * qt + t, :], ident[:])
                    ins.then_inc(n_ct, 1)
            pe.wait_ge(n_vc, 4)
            for n in range(len(UNITS) + 1):
                if n + 2 < len(UNITS):
                    scores(n + 2)
                if n < len(UNITS):
                    turned(n)
                if n:
                    values(n - 1)
            pe.wait_ge(m_lo, 16)
            gemm("nsa_out", hh, hl, META, (m_lo, 8))

        def mean_bank(m):
            return mix[0] if m < 6 else acc[(m - 6) % 4]

        def nsa_act(act, step, ahead, residual, post_norm):
            def squared(m, src, more=None):
                act.wait_ge(n_a, m + 1)
                if m >= 8:
                    act.wait_ge(n_mean, m - 7)
                nc.scalar.activation(nsq[:, m % 8, :], src, ACT.Square).then_inc(n_sq, 1)

            def rooted(m):
                act.wait_ge(n_mean, m + 1)
                if m >= 2:
                    act.wait_ge(n_n, m - 1)
                s = 1.0 if m < 6 else 64.0
                nc.scalar.activation(nroot[:, m % 2, :], mean_bank(m)[:, 0:SEQ], ACT.Sqrt, scale=s,
                                     bias=eps[:, 0:1] if m < 6 else eps[:, 4:5]).then_inc(n_root, 1)

            for m in range(12):
                ahead(BASE["nsa_kv"] + m)
                if m in KTILES:
                    i = KTILES.index(m)
                    squared(i, nk[:, i, :])
            act.wait_ge(n_gate, 1)
            nc.scalar.activation(tg[:, 1, META:], tg[:, 0, META:], ACT.Sigmoid).then_inc(n_sig, 1)
            ahead(BASE["nsa_gate"])
            for m in range(KD):
                if m < 6:
                    rooted(m)
                ahead(BASE["nsa_q"] + m)
                squared(6 + m, nq[:, m, :])
            for m in range(6, 14):
                rooted(m)
            act.wait_ge(n_hid, 2)
            act.wait_ge(n_pos, 2)
            act.wait_ge(n_mask, 6)
            for h in range(2):
                nc.scalar.activation(nhk[0:DH, h:4:2, 0:NCMP], acc[h][0:DH, 0:2 * NCMP].rearrange("p (t n) -> p t n", t=2),
                                     ACT.Gelu_apprx_tanh, bias=nbias[0:DH, 0:1]).then_inc(n_gelu, 1)
                for t in range(2):
                    src = acc[h][0:DH, 32 + NCMP * t:32 + NCMP * t + NCMP]
                    nc.scalar.activation(nhv[0:DH, 2 * t + h, :, 0:NCMP], src.unsqueeze(1).to_broadcast([DH, 4, NCMP]),
                                         ACT.Gelu_apprx_tanh, bias=nbias[0:DH, 1:2]).then_inc(n_gelu, 1)
            act.wait_ge(n_tr, 3)
            nc.scalar.activation(nvt[:, 0, :], stat[:, :], ACT.Copy).then_inc(n_vt, 1)
            nc.scalar.activation(nvt[:, 1, :], acc[3][:, :], ACT.Copy).then_inc(n_vt, 1)
            for h in range(2):
                act.wait_ge(n_csub, h + 1)
                nc.scalar.activation(ncs[:, h], ncs[:, h], ACT.Exp, scale=-1.0).then_inc(n_cexp, 1)

            def exps(n):
                act.wait_ge(n_min, n + 1)
                if n >= 2:
                    act.wait_ge(n_pt, n - 1)
                for qt in range(2):
                    s = slice(P * qt, P * qt + P * (qt + 1))
                    act.wait_ge(n_p, n - 1) if n >= 2 else None
                    nc.scalar.activation(nP[:, n % 2, s], nS[:, n % 2, s], ACT.Exp, scale=-1.0, bias=nstat[:, 2 * (n % 2) + qt:2 * (n % 2) + qt + 1],
                                         accum_out=nstat[:, 8 + 2 * (n % 2) + qt:9 + 2 * (n % 2) + qt]).then_inc(n_exp, 1)

            exps(0)
            for n in range(4):
                h, t = divmod(n, 2)
                act.wait_ge(n_ct, n + 1)
                nc.scalar.activation(npct[:, h, t, :], stat[:, 0:SEQ], ACT.Copy).then_inc(n_cpt, 1)
            for n in range(len(UNITS)):
                if n + 1 < len(UNITS):
                    exps(n + 1)
                act.wait_ge(n_pt, n + 1)
                if n >= 2:
                    act.wait_ge(n_o, n - 1)
                nc.scalar.activation(nPT[:, n % 2, :], (acc[3], stat)[n % 2][:, 0:384], ACT.Copy).then_inc(n_ptc, 1)
                if n % 4 == 0 and n:
                    attn_hi(act, n // 4 - 1, n_o, n)
            attn_hi(act, KD - 1, n_o, len(UNITS))
            for m in range(KD):
                ahead(BASE["nsa_out"] + m)
                residual(3, m)

        def attn_hi(act, j, o, count, idx=1):
            act.wait_ge(o, count)
            nc.scalar.activation(hh[:, j, META:], mix[j % 2][:, 0:SEQ], ACT.Copy).then_inc(m_hi, 1)

        def attn_lo(dve, j, idx=1):
            dve.wait_ge(m_hi, 8 * idx + j + 1)
            nc.vector.tensor_tensor(hl[:, j, META:], mix[j % 2][:, 0:SEQ], hh[:, j, META:].bitcast(F32), ALU.subtract).then_inc(m_lo, 1)

        def nsa_dve(dve, step, ahead, tail, post_norm):
            def normed(m):
                v = nk[:, m, :] if m < 6 else nq[:, m - 6, :]
                dve.wait_ge(n_root, m + 1)
                if m:
                    dve.wait_ge(n_n, m)
                step(nc.vector.reciprocal(nr, nroot[:, m % 2, :]))
                nc.vector.scalar_tensor_tensor(v, v, col("k_gain", m // 2) if m < 6 else col("q_gain"), nr,
                                               ALU.mult, ALU.mult).then_inc(n_n, 1)

            def rotated(m):
                v = nk[:, m, :] if m < 6 else nq[:, m - 6, :]
                dve.wait_ge(n_perm, m + 1)
                if m:
                    dve.wait_ge(n_k, m)
                step(nc.vector.tensor_tensor(nt, mix[1 + m % 2][:, 0:SEQ], sinT[:, 0:SEQ], ALU.mult))
                step(nc.vector.tensor_tensor(v, v, cosT[:, 0:SEQ], ALU.mult))
                nc.vector.tensor_tensor(v, v, nt, ALU.add).then_inc(n_k, 1)

            dve.wait_ge(tab_ok, 5)
            for m in range(12):
                b = BASE["nsa_kv"] + m
                dve.wait_ge(used, b + 1)
                if m in KTILES:
                    ins = nc.vector.tensor_tensor(nk[:, KTILES.index(m), :], bank("nsa_kv", m)[:, 0:SEQ], rx[:, META:], ALU.mult)
                    ins.then_inc(n_a, 1)
                    dve.wait_ge(n_a, KTILES.index(m) + 1)
                else:
                    ins = nc.vector.tensor_tensor(nv[:, VTILES.index(m), :], bank("nsa_kv", m)[:, 0:SEQ], rx[:, META:], ALU.mult)
                    ins.then_inc(n_v, 1)
                    dve.wait_ge(n_v, VTILES.index(m) + 1)
                dve.sem_inc(acc_used, 1)
                ahead(b)
            dve.wait_ge(used, BASE["nsa_gate"] + 1)
            nc.vector.tensor_tensor(tg[:, 0, META:], bank("nsa_gate", 0)[:, 0:SEQ], rx[:, META:], ALU.mult).then_inc(n_gate, 1)
            dve.wait_ge(n_gate, 1)
            dve.sem_inc(acc_used, 1)
            ahead(BASE["nsa_gate"])
            for m in range(KD):
                if m < 6:
                    normed(m)
                dve.wait_ge(used, BASE["nsa_q"] + m + 1)
                dve.wait_ge(sum_ok, 3)
                nc.vector.scalar_tensor_tensor(nq[:, m, :], bank("nsa_q", m)[:, 0:SEQ], -1.0, rx[:, META:],
                                               ALU.mult, ALU.mult).then_inc(n_a, 1)
                dve.wait_ge(n_a, 6 + m + 1)
                dve.sem_inc(acc_used, 1)
                ahead(BASE["nsa_q"] + m)
                if m < 6:
                    rotated(m)
            normed(6)
            dve.wait_ge(n_tr, 1)
            nc.vector.tensor_copy(ngate, stat[:, 0:SEQ].rearrange("p (a n) -> p a n", a=2)[:, :, 0:48]).then_inc(n_gt, 1)
            for m in range(7, 14):
                normed(m)
                rotated(m - 1)
            dve.wait_ge(n_pos, 1)
            nc.vector.tensor_tensor(nbias[0:DH, :], acc[2][0:DH, 0:2], par[0:DH, COL["cmp_b1"]:COL["cmp_b1"] + 2], ALU.add).then_inc(n_pos, 1)
            rotated(13)
            dve.wait_ge(n_comp, 1)
            nc.vector.tensor_copy(nkc, acc[2][:, 0:32].rearrange("p (t n) -> p t n", t=2)).then_inc(n_kc, 1)
            for r in range(4):
                nc.vector.tensor_scalar(nvc[:, :, r, :], mix[0][:, 0:SEQ].rearrange("p (g d) -> p g d", g=4), rowmask[:, r:r + 1],
                                        None, ALU.mult).then_inc(n_vc, 1)
            step(nc.vector.memset(npc.rearrange("p h b n -> p (h b n)"), 0.0))
            for h in range(2):
                dve.wait_ge(n_cs, h + 1)
                s = ncs[:, h].rearrange("p a (j n) -> p a j n", j=KD)
                step(nc.vector.tensor_tensor(s, acc[h][:, 0:SEQ].rearrange("p (a j n) -> p a j n", a=2, j=KD),
                                             ncm.unsqueeze(2).to_broadcast([P, 2, KD, 16]), ALU.add))
                least = nstat[:, 16:32].rearrange("p (a j) -> p a j", a=2)
                step(nc.vector.tensor_reduce(least, s, AX.X, ALU.min))
                nc.vector.tensor_tensor(s, s, least.unsqueeze(3).to_broadcast([P, 2, KD, 16]), ALU.subtract).then_inc(n_csub, 1)
            for h in range(2):
                dve.wait_ge(n_cexp, h + 1)
                s = ncs[:, h].rearrange("p a (j n) -> p a j n", j=KD)
                tot = nstat[:, 32:48]
                tot3 = tot.rearrange("p (a j) -> p a j", a=2)
                step(nc.vector.tensor_reduce(tot3, s, AX.X, ALU.add))
                step(nc.vector.reciprocal(tot, tot))
                step(nc.vector.tensor_tensor(tot.rearrange("p (a t r) -> p a t r", a=2, t=2), tot.rearrange("p (a t r) -> p a t r", a=2, t=2),
                                             ngate[:, :, 0:16].rearrange("p a (t g r) -> p a t g r", t=2, g=2)[:, :, :, h, :], ALU.mult))
                step(nc.vector.tensor_tensor(s, s, tot3.unsqueeze(3).to_broadcast([P, 2, KD, 16]), ALU.mult))
                nc.vector.tensor_tensor(npc[:, h].rearrange("p (a t) (r n) -> p a (t r) n", a=2, n=32)[:, :, :, 0:16], s,
                                        nc01.unsqueeze(2).to_broadcast([P, 2, KD, 16]), ALU.mult).then_inc(n_cp, 1)

            def least(n):
                dve.wait_ge(n_s, n + 1)
                dve.wait_ge(n_mask, 4)
                if n >= 2:
                    dve.wait_ge(n_exp, 2 * n - 2)
                for qt in range(2):
                    s = slice(P * qt, P * qt + P * (qt + 1))
                    ins = nc.vector.tensor_tensor_reduce(nS[:, n % 2, s], acc[n % 3][:, s], nmask[:, s], 1.0, 3e38, ALU.add,
                                                         ALU.min, nstat[:, 2 * (n % 2) + qt:2 * (n % 2) + qt + 1])
                ins.then_inc(n_min, 1)

            least(0)
            for n in range(len(UNITS)):
                if n + 1 < len(UNITS):
                    least(n + 1)
                j, h, b = UNITS[n]
                head = 8 * (j // 4) + 4 * h + j % 4
                dve.wait_ge(n_exp, 2 * n + 2)
                rec = nstat[:, 12:14]
                if n:
                    dve.wait_ge(n_p, n)
                step(nc.vector.reciprocal(rec, nstat[:, 8 + 2 * (n % 2):10 + 2 * (n % 2)]))
                for qt in range(2):
                    s = slice(P * qt, P * qt + P * (qt + 1))
                    g = 16 * (b + 1) + head
                    ins = nc.vector.tensor_scalar(nP[:, n % 2, s], nP[:, n % 2, s], rec[:, qt:qt + 1], ngate[:, qt, g:g + 1],
                                                  ALU.mult, ALU.mult)
                ins.then_inc(n_p, 1)
                if n % 4 == 1 and n > 4:
                    attn_lo(dve, n // 4 - 1)
            attn_lo(dve, KD - 1)
            for m in range(KD):
                tail(3, m, "nsa_out", BASE["nsa_out"] + m)

        mixers["pool"][2], mixers["pe"][2], mixers["act"][2], mixers["dve"][2] = nsa_pool, nsa_pe, nsa_act, nsa_dve
        at["o"] = 0
        gls = area(1536).rearrange("p (a n) -> p a n", a=3)
        ge = area(1536).rearrange("p (a n) -> p a n", a=3)
        gv = scr[:, 0:3072].rearrange("p (a n) -> p a n", a=3)
        gb = area(1088).rearrange("p (h t) -> p h t", h=4)
        gkk = area(1088).rearrange("p (h t) -> p h t", h=4)
        gq = area(1088).rearrange("p (h t) -> p h t", h=4)
        gk = area(1088).rearrange("p (h t) -> p h t", h=4)
        gkt = area(1536).rearrange("p (a n) -> p a n", a=3)
        gS = area(1024).rearrange("p (h n) -> p h n", h=4)
        gatt = area(512).rearrange("p (b h n) -> p b h n", b=2, h=4)
        gwg = area(512)
        gdec = area(20).rearrange("p (h n) -> p h n", h=4)
        gtri = area(128)
        gsq = scr[:, 3072:3072 + 2176].rearrange("p (m t) -> p m t", m=8)
        gkr, gqr = (tg, ts), (tu, th)
        g_w, g_tri, g_lr, g_z, g_e, g_ln, g_ls, g_kr, g_b, g_bc, g_qr, g_dif, g_eq = (
            sem("g_" + s) for s in ("w", "tri", "lr", "z", "e", "ln", "ls", "kr", "b", "bc", "qr", "dif", "eq"))
        g_dec, g_v, g_vt, g_vc, g_kt, g_kc, g_r, g_rs, g_att, g_attc, g_kv, g_S, g_o, g_oc = (
            sem("g_" + s) for s in ("dec", "v", "vt", "vc", "kt", "kc", "r", "rs", "att", "attc", "kv", "S", "o", "oc"))
        g_sq, g_mean, g_root, g_f = (sem("g_" + s) for s in ("sq", "mean", "root", "f"))
        TOK = ((0, META), (META, P), (META + P, P))
        CHUNKS = [(0, META, 0, 0)] + [(META + 64 * n, 64, 1 + n // 2, 64 * (n % 2)) for n in range(4)]

        def gla_pool(pool, step):
            pool.wait_ge(m_lo, 16)
            step(pool.memset(gwg[0:64, :], 0.0))
            pool.dma_start(gwg[0:16, :], a["w_gate"]).then_inc(g_w, 16)
            pool.dma_start(gwg[32:33, :], a["gate_row"]).then_inc(g_w, 16)
            step(pool.memset(gtri, 1.0))
            step(pool.affine_select(out=gtri, in_=gtri, compare_op=ALU.is_ge, fill=0.0, base=0, pattern=[[1, P]], channel_multiplier=-1))
            pool.memset(gtri[0:64, 64:P], 0.0).then_inc(g_tri, 1)
            pool.memset(gatt.rearrange("p b h n -> p (b h n)"), 0.0).then_inc(g_tri, 1)

        def gla_pe(pe, gemm):
            gemm("gla_lr", xh, xl, 0, (x_lo, 40))
            pe.wait_ge(g_w, 32)
            pe.wait_ge(g_lr, 2)
            for n, (s, w) in enumerate(TOK):
                ins = nc.tensor.matmul(mix[n][0:w, :], ry[0:33, s:s + w], gwg[0:33, :], start=True, stop=True)
            ins.then_inc(g_z, 1)
            gemm("gla_k", xh, xl, 0, None)
            pe.wait_ge(g_ls, 3)
            pe.wait_ge(g_tri, 2)
            for h in range(4):
                for n, (s, w) in enumerate(TOK):
                    ins = nc.tensor.matmul((mix + [stat])[h][:, s:s + w], gls[0:w, n, P * h:P * h + P], gtri[0:w, 0:w], start=True, stop=True)
                ins.then_inc(g_b, 1)
            gemm("gla_q", xh, xl, 0, None)
            gemm("gla_v", xh, xl, 0, None)
            pe.wait_ge(g_bc, 4)
            for n, (s, w) in enumerate(TOK):
                for e in range(2):
                    i = 2 * n + e
                    pe.wait_ge(g_v, 4 * e + 4)
                    if i >= 3:
                        pe.wait_ge(g_vc, i - 2)
                    for m in range(4):
                        ins = nc.tensor.transpose(mix[i % 3][0:w, P * m:P * m + P], y[:, 4 * e + m, s:s + w], ident[:])
                    ins.then_inc(g_vt, 1)
            pe.wait_ge(g_eq, 12)
            for n, (s, w) in enumerate(TOK):
                pe.wait_ge(g_vc, 4 + n)
                for h in range(4):
                    ins = nc.tensor.transpose(mix[n][0:w, P * h:P * h + P], gkk[:, h, s:s + w], ident[:])
                ins.then_inc(g_kt, 1)
            gemm("gla_r", xh, xl, 0, None)
            pe.wait_ge(acc_used, TILE["gla_r"] + 8)
            pe.wait_ge(g_kc, 3)

            def att(c):
                s, w, n, base = CHUNKS[c]
                if c >= 2:
                    pe.wait_ge(g_attc, c - 1)
                for h in range(4):
                    ins = nc.tensor.matmul(acc[c % 2][base:base + w, 64 * h:64 * h + w], gk[:, h, s:s + w], gq[:, h, s:s + w],
                                           start=True, stop=True)
                ins.then_inc(g_att, 1)

            def kv(c):
                s, w, n, base = CHUNKS[c]
                if c:
                    pe.wait_ge(g_S, 4 * c)
                for h in range(4):
                    ins = nc.tensor.matmul((mix[2], stat)[h // 2][:, 256 * (h % 2):256 * (h % 2) + 256], gkt[base:base + w, n, P * h:P * h + P],
                                           gv[base:base + w, n, 256 * h:256 * h + 256], start=True, stop=True)
                ins.then_inc(g_kv, 1)

            att(0)
            kv(0)
            for c, (s, w, n, base) in enumerate(CHUNKS):
                if c + 1 < 5:
                    att(c + 1)
                pe.wait_ge(g_attc, c + 1)
                if c >= 2:
                    pe.wait_ge(g_oc, c - 1)
                for h in range(4):
                    if c:
                        pe.wait_ge(g_S, 4 * (c - 1) + h + 1)
                    for v in range(2):
                        dst = acc[2 + c % 2][:, 64 * (2 * h + v):64 * (2 * h + v) + w]
                        ins = nc.tensor.matmul(dst, gv[base:base + w, n, 256 * h + P * v:256 * h + P * v + P], gatt[base:base + w, c % 2, h, 0:w],
                                               start=True, stop=(c == 0))
                        if c:
                            ins = nc.tensor.matmul(dst, gS[:, h, P * v:P * v + P], gq[:, h, s:s + w], start=False, stop=True)
                ins.then_inc(g_o, 1)
                if 0 < c + 1 < 4:
                    kv(c + 1)
            for h in range(4):
                pe.wait_ge(g_sq, 2 * h + 2)
                if h == 3:
                    pe.wait_ge(g_root, 1)
                for v in range(2):
                    ins = nc.tensor.matmul(mix[h % 3][:, 0:L], ones[:], gsq[:, 2 * h + v, :], start=(v == 0), stop=(v == 1))
                ins.then_inc(g_mean, 1)
            gemm("gla_out", hh, hl, 0, (m_lo, 16))

        def gla_act(act, step, ahead, residual, post_norm):
            ahead(BASE["gla_lr"])
            act.wait_ge(g_z, 1)
            for n, (s, w) in enumerate(TOK):
                nc.scalar.activation(ge[0:w, n, :], mix[n][0:w, :], ACT.Abs).then_inc(g_e, 1)
            for m in range(2):
                ahead(BASE["gla_k"] + m)
            for n, (s, w) in enumerate(TOK):
                act.wait_ge(g_e, n + 1)
                nc.scalar.activation(ge[0:w, n, :], ge[0:w, n, :], ACT.Exp, scale=-1.0).then_inc(g_e, 1)
            act.wait_ge(g_e, 6)
            for n, (s, w) in enumerate(TOK):
                nc.scalar.activation(ge[0:w, n, :], ge[0:w, n, :], ACT.Ln, bias=1.0).then_inc(g_ln, 1)
            for m in range(2, 4):
                ahead(BASE["gla_k"] + m)
            for h in range(4):
                act.wait_ge(g_b, h + 1)
                src = (mix + [stat])[h][:, 0:L]
                nc.scalar.activation(gb[:, h, :], src, ACT.Copy).then_inc(g_bc, 1)
                nc.scalar.activation(gq[:, h, :], src, ACT.Exp, scale=1.0 / 16).then_inc(g_e, 1)
                nc.scalar.activation(gk[:, h, :], src, ACT.Exp, scale=-1.0 / 16).then_inc(g_e, 1)
                ahead(BASE["gla_q"] + h)
            act.wait_ge(g_bc, 4)
            act.wait_ge(g_dif, 3)
            nc.scalar.activation(gkk.rearrange("p h t -> p (h t)"), gkk.rearrange("p h t -> p (h t)"), ACT.Exp, scale=1.0 / 16).then_inc(g_e, 1)
            nc.scalar.activation(gdec.rearrange("p h t -> p (h t)"), gdec.rearrange("p h t -> p (h t)"), ACT.Exp, scale=1.0 / 16).then_inc(g_dec, 1)
            for m in range(KD):
                ahead(BASE["gla_v"] + m)
            for i in range(6):
                n, e = divmod(i, 2)
                act.wait_ge(g_vt, i + 1)
                w = TOK[n][1]
                nc.scalar.activation(gv[0:w, n, 512 * e:512 * e + 512], mix[i % 3][0:w, :], ACT.Copy).then_inc(g_vc, 1)
            for n in range(3):
                act.wait_ge(g_kt, n + 1)
                w = TOK[n][1]
                nc.scalar.activation(gkt[0:w, n, :], mix[n][0:w, :], ACT.Copy).then_inc(g_kc, 1)
            for m in range(KD):
                ahead(BASE["gla_r"] + m)
                act.wait_ge(g_r, m + 1)
                nc.scalar.activation(sq[:, m, :], sq[:, m, :], ACT.Silu).then_inc(g_rs, 1)
            for c, (s, w, n, base) in enumerate(CHUNKS):
                act.wait_ge(g_o, c + 1)
                nc.scalar.activation(y[:, :, s:s + w], acc[2 + c % 2][:, :].rearrange("p (m t) -> p m t", m=8)[:, :, 0:w], ACT.Copy).then_inc(g_oc, 1)
            act.wait_ge(g_oc, 5)
            for m in range(KD):
                nc.scalar.activation(gsq[:, m, :], y[:, m, :], ACT.Square).then_inc(g_sq, 1)
            for h in range(4):
                act.wait_ge(g_mean, h + 1)
                nc.scalar.activation(gsq[:, 2 * h, :], mix[h % 3][:, 0:L], ACT.Sqrt, scale=4.0, bias=eps[:, 0:1]).then_inc(g_root, 1)
            for m in range(KD):
                act.wait_ge(g_f, m + 1)
                nc.scalar.activation(hh[:, m, :], y[:, m, :], ACT.Copy).then_inc(m_hi, 1)
            for m in range(KD):
                ahead(BASE["gla_out"] + m)
                residual(6, m)
            post_norm(6)

        def gla_dve(dve, step, ahead, tail, post_norm):
            def evac(name, m, out_, signal, count, scale=None):
                b = BASE[name] + m
                dve.wait_ge(used, b + 1)
                src = bank(name, m)[:, 0:L]
                if scale is None:
                    ins = nc.vector.tensor_tensor(out_, src, rx[:], ALU.mult)
                else:
                    ins = nc.vector.scalar_tensor_tensor(out_, src, scale, rx[:], ALU.mult, ALU.mult)
                ins.then_inc(signal, 1)
                dve.wait_ge(signal, count)
                dve.sem_inc(acc_used, 1)
                ahead(b)

            evac("gla_lr", 0, ry[:], g_lr, 1)
            nc.vector.memset(ry[32:33, :], 1.0).then_inc(g_lr, 1)
            for m in range(4):
                evac("gla_k", m, gkr[m // 2][:, m % 2, :], g_kr, m + 1)
                if m:
                    n, w = m - 1, TOK[m - 1][1]
                    dve.wait_ge(g_ln, n + 1)
                    nc.vector.scalar_tensor_tensor(gls[0:w, n, :], mix[n][0:w, :], 0.0, ge[0:w, n, :], ALU.min, ALU.subtract).then_inc(g_ls, 1)
            for m in range(4):
                evac("gla_q", m, gqr[m // 2][:, m % 2, :], g_qr, m + 1, float(P) ** -0.5)
            dve.wait_ge(g_bc, 4)
            for h in range(4):
                v = gb[:, h, META:].rearrange("p (c t) -> p c t", c=4)
                nc.vector.tensor_tensor(gkk[:, h, META:].rearrange("p (c t) -> p c t", c=4), v[:, :, 63:64].to_broadcast([P, 4, 64]), v,
                                        ALU.subtract).then_inc(g_dif, 1) if h == 3 else \
                    nc.vector.tensor_tensor(gkk[:, h, META:].rearrange("p (c t) -> p c t", c=4), v[:, :, 63:64].to_broadcast([P, 4, 64]), v,
                                            ALU.subtract)
            nc.vector.tensor_tensor(gkk[:, :, 0:META], gb[:, :, META - 1:META].to_broadcast([P, 4, META]), gb[:, :, 0:META],
                                    ALU.subtract).then_inc(g_dif, 1)
            nc.vector.tensor_copy(gdec, gb[:, :, META - 1:L:64]).then_inc(g_dif, 1)
            for m in range(KD):
                evac("gla_v", m, y[:, m, :], g_v, m + 1)
                if m < 4:
                    r, q = gkr[m // 2][:, m % 2, :], gqr[m // 2][:, m % 2, :]
                    dve.wait_ge(g_e, 15)
                    nc.vector.tensor_tensor(gq[:, m, :], gq[:, m, :], q, ALU.mult).then_inc(g_eq, 1)
                    nc.vector.tensor_tensor(gk[:, m, :], gk[:, m, :], r, ALU.mult).then_inc(g_eq, 1)
                    nc.vector.tensor_tensor(gkk[:, m, :], gkk[:, m, :], r, ALU.mult).then_inc(g_eq, 1)
            dve.wait_ge(sum_ok, norm_of(5) + 1)
            for m in range(KD):
                evac("gla_r", m, sq[:, m, :], g_r, m + 1)
            dve.wait_ge(g_dec, 1)

            def masked(c):
                s, w, n, base = CHUNKS[c]
                dve.wait_ge(g_att, c + 1)
                if c >= 2:
                    dve.wait_ge(g_o, c - 1)
                rows = slice(base, base + w)
                mask = gtri[rows, base:base + w].bitcast(I32).unsqueeze(1).to_broadcast([w, 4, w])
                nc.vector.copy_predicated(gatt[rows, c % 2, :, 0:w], mask,
                                          acc[c % 2][rows, 0:256].rearrange("p (h t) -> p h t", h=4)[:, :, 0:w]).then_inc(g_attc, 1)

            masked(0)
            for c in range(5):
                if c + 1 < 5:
                    masked(c + 1)
                if c < 4:
                    dve.wait_ge(g_kv, c + 1)
                    if c:
                        dve.wait_ge(g_o, c + 1)
                    for h in range(4):
                        src = (mix[2], stat)[h // 2][:, 256 * (h % 2):256 * (h % 2) + 256]
                        if c == 0:
                            nc.vector.tensor_copy(gS[:, h, :], src).then_inc(g_S, 1)
                        else:
                            nc.vector.scalar_tensor_tensor(gS[:, h, :], gS[:, h, :], gdec[:, h, c:c + 1], src, ALU.mult, ALU.add).then_inc(g_S, 1)
                    dve.wait_ge(g_S, 4 * c + 4)
            dve.wait_ge(g_rs, 8)

            def low(m):
                dve.wait_ge(m_hi, 16 + m + 1)
                nc.vector.tensor_tensor(hl[:, m, :], y[:, m, :], hh[:, m, :].bitcast(F32), ALU.subtract).then_inc(m_lo, 1)

            for h in range(4):
                dve.wait_ge(g_root, h + 1)
                step(nc.vector.reciprocal(gsq[:, 2 * h, :], gsq[:, 2 * h, :]))
                for v in range(2):
                    m = 2 * h + v
                    step(nc.vector.scalar_tensor_tensor(y[:, m, :], y[:, m, :], col("gla_norm", v), gsq[:, 2 * h, :], ALU.mult, ALU.mult))
                    nc.vector.tensor_tensor(y[:, m, :], y[:, m, :], sq[:, m, :], ALU.mult).then_inc(g_f, 1)
                    if m:
                        low(m - 1)
            low(7)
            for m in range(KD):
                tail(6, m, "gla_out", BASE["gla_out"] + m)
            post_norm(6)

        mixers["pool"][5], mixers["pe"][5], mixers["act"][5], mixers["dve"][5] = gla_pool, gla_pe, gla_act, gla_dve
        at["o"] = 0
        sk = area(544).rearrange("p (m t) -> p m t", m=2)
        svt = area(544).rearrange("p (m t) -> p m t", m=2)
        sv = area(768).rearrange("p (a n) -> p a n", a=3)
        smask = area(416)
        snk = area(16)
        sstat = area(32)
        snt = area(272)
        sS = area(832).rearrange("p (b n) -> p b n", b=2)
        sP = area(832).rearrange("p (b n) -> p b n", b=2)
        sPT = area(768).rearrange("p (b n) -> p b n", b=2)
        sPM = area(512).rearrange("p (b n) -> p b n", b=2)
        sq_q = y[:, :, META:]
        kv_hi, kv_lo, s_kv, s_q, s_perm, s_k, s_tr, s_v, s_mask, s_nk = (
            sem("s_" + n) for n in ("kvhi", "kvlo", "kv", "q", "perm", "k", "tr", "v", "mask", "nk"))
        s_s, s_min, s_exp, s_es, s_p, s_pt, s_ptc, s_pmc, s_o = (
            sem("s_" + n) for n in ("s", "min", "exp", "es", "p", "pt", "ptc", "pmc", "o"))
        SUNITS = [(j, h) for j in range(KD) for h in range(2)]
        SQ = ((0, 144, 0), (144, 272, P))

        def swa_pool(pool, step):
            pool.wait_ge(m_lo, 24)
            step(pool.memset(smask, 0.0))
            for s in (META, 144 + META + P):
                v = smask[:, s:s + P]
                pool.affine_select(out=v, in_=v, compare_op=ALU.is_ge, fill=BIG, base=0, pattern=[[-1, P]], channel_multiplier=1).then_inc(s_mask, 1)
            v = smask[:, 144 + META:144 + META + P]
            pool.affine_select(out=v, in_=v, compare_op=ALU.is_gt, fill=BIG, base=0, pattern=[[1, P]], channel_multiplier=-1).then_inc(s_mask, 1)

        def kv_pe(pe, gemm):
            gemm("kv", hh, hl, 0, (kv_lo, 0))

        def kv_act(act, k):
            nc.scalar.activation(hh[:, k, :], x[:, k, :], ACT.Copy, scale=col("kv_norm", k)).then_inc(kv_hi, 1)

        def kv_low(dve, k):
            dve.wait_ge(kv_hi, k + 1)
            nc.vector.scalar_tensor_tensor(hl[:, k, :], x[:, k, :], col("kv_norm", k), hh[:, k, :].bitcast(F32), ALU.mult, ALU.subtract).then_inc(kv_lo, 1)

        def kv_dve(dve, ahead):
            for m in range(4):
                b = BASE["kv"] + m
                dve.wait_ge(used, b + 1)
                nc.vector.tensor_tensor((sk, svt)[m // 2][:, m % 2, :], bank("kv", m)[:, 0:L], rx[:], ALU.mult).then_inc(s_kv, 1)
                dve.wait_ge(s_kv, m + 1)
                dve.sem_inc(acc_used, 1)
                ahead(b)

        def swa_pe(pe, gemm):
            pe.wait_ge(s_kv, 4)
            for m in range(2):
                ins = nc.tensor.matmul(mix[1 + m][:, 0:L], rot[:], sk[:, m, :], start=True, stop=True)
                ins.then_inc(s_perm, 1)
            pe.wait_ge(root_ok, norm_of(8) + 1)
            for kt in range(2):
                for t in range(2):
                    nc.tensor.transpose(stat[:, 256 * kt + P * t:256 * kt + P * t + P], svt[:, t, META + P * kt:META + P * kt + P], ident[:])
            for t in range(2):
                ins = nc.tensor.transpose(mix[0][0:META, P * t:P * t + P], svt[:, t, 0:META], ident[:])
            ins.then_inc(s_tr, 1)

            def perm(m):
                pe.wait_ge(s_q, m + 1)
                pe.wait_ge(s_k, m + 1)
                nc.tensor.matmul(mix[1 + m % 2][:, 0:SEQ], rot[:], sq_q[:, m, :], start=True, stop=True).then_inc(s_perm, 1)

            for m in range(KD):
                gemm("swa_q", xh, xl, META, (x_lo, 64) if m == 0 else None, only=m)
                if m:
                    perm(m - 1)
            perm(KD - 1)
            pe.wait_ge(acc_used, TILE["swa_q"] + 8)
            pe.wait_ge(s_v, 2)

            def scores(n):
                j, h = SUNITS[n]
                pe.wait_ge(s_k, 2 + j + 1)
                if n >= 2:
                    pe.wait_ge(s_min, n - 1)
                for qt, (c, e, q) in enumerate(SQ):
                    ins = nc.tensor.matmul(acc[n % 2][:, c:c + e], sq_q[DH * h:DH * h + DH, j, q:q + P], sk[DH * h:DH * h + DH, j // 4, 0:e],
                                           start=True, stop=True)
                ins.then_inc(s_s, 1)

            def turned(n):
                pe.wait_ge(s_p, n + 1)
                if n >= 2:
                    pe.wait_ge(s_ptc, n - 1)
                    pe.wait_ge(s_pmc, n - 1)
                for d, s in ((0, META), (P, 144 + META), (2 * P, 144 + META + P)):
                    nc.tensor.transpose(acc[2 + n % 2][:, d:d + P], sP[:, n % 2, s:s + P], ident[:])
                for qt in range(2):
                    ins = nc.tensor.transpose((stat, mix[2])[n % 2][0:META, P * qt:P * qt + P], sP[:, n % 2, 144 * qt:144 * qt + META], ident[:])
                ins.then_inc(s_pt, 1)

            def values(n):
                j, h = SUNITS[n]
                g = 2 * (j // 4) + h
                dst = mix[j % 2][DH * h:DH * h + DH]
                if j >= 2 and h == 0:
                    pe.wait_ge(m_lo, 24 + j - 1)
                elif j < 2:
                    pe.wait_ge(s_k, 10)
                pe.wait_ge(s_ptc, n + 1)
                w = slice(DH * g, DH * g + DH)
                nc.tensor.matmul(dst[:, 0:SEQ], sv[:, 0, w], sPT[:, n % 2, 0:SEQ], start=True, stop=False)
                nc.tensor.matmul(dst[:, P:SEQ], sv[:, 1, w], sPT[:, n % 2, SEQ:SEQ + P], start=False, stop=False)
                pe.wait_ge(s_pmc, n + 1)
                nc.tensor.matmul(dst[:, 0:SEQ], sv[0:META, 2, w], sPM[0:META, n % 2, :], start=False, stop=True).then_inc(s_o, 1)

            scores(0)
            for n in range(len(SUNITS) + 1):
                if n + 1 < len(SUNITS):
                    scores(n + 1)
                if n:
                    values(n - 1)
                if n < len(SUNITS):
                    turned(n)
            gemm("swa_out", hh, hl, META, (m_lo, 24))

        def swa_act(act, step, ahead, residual, post_norm):
            act.wait_ge(s_tr, 1)
            nc.scalar.activation(sv[:, 0:2, :].rearrange("p a n -> p (a n)"), stat[:, :], ACT.Copy).then_inc(s_v, 1)
            nc.scalar.activation(sv[0:META, 2, :], mix[0][0:META, 0:256], ACT.Copy).then_inc(s_v, 1)
            for m in range(KD):
                ahead(BASE["swa_q"] + m)

            def exps(n):
                j, h = SUNITS[n]
                head = 2 * j + h
                act.wait_ge(s_min, n + 1)
                if n >= 2:
                    act.wait_ge(s_pt, n - 1)
                b = 2 * (n % 2)
                for qt, (c, e, q) in enumerate(SQ):
                    nc.scalar.activation(sP[:, n % 2, c:c + e], sS[:, n % 2, c:c + e], ACT.Exp, scale=-1.0, bias=sstat[:, b + qt:b + qt + 1],
                                         accum_out=sstat[:, 8 + b + qt:9 + b + qt]).then_inc(s_exp, 1)
                nc.scalar.activation(sstat[:, 16 + b:18 + b], sstat[:, b:b + 2], ACT.Exp, bias=col("sinks", head)).then_inc(s_es, 1)

            exps(0)
            for n in range(len(SUNITS)):
                if n + 1 < len(SUNITS):
                    exps(n + 1)
                act.wait_ge(s_pt, n + 1)
                if n >= 2:
                    act.wait_ge(s_o, n - 1)
                nc.scalar.activation(sPT[:, n % 2, :], acc[2 + n % 2][:, 0:384], ACT.Copy).then_inc(s_ptc, 1)
                if n % 2 == 0 and n:
                    attn_hi(act, n // 2 - 1, s_o, n)
            attn_hi(act, KD - 1, s_o, len(SUNITS))
            for m in range(KD):
                ahead(BASE["swa_out"] + m)
                residual(9, m)
            post_norm(9)

        def swa_dve(dve, step, ahead, tail, post_norm):
            def rotated(i, v, w, tab):
                dve.wait_ge(s_perm, i + 1)
                if i:
                    dve.wait_ge(s_k, i)
                step(nc.vector.tensor_tensor(snt[:, 0:w], mix[1 + i % 2][:, 0:w], sinT[:, tab:], ALU.mult))
                step(nc.vector.tensor_tensor(v, v, cosT[:, tab:], ALU.mult))
                nc.vector.tensor_tensor(v, v, snt[:, 0:w], ALU.add).then_inc(s_k, 1)

            nc.vector.tensor_scalar(snk, par[:, COL["sinks"]:COL["sinks"] + 16], -1.0, None, ALU.mult).then_inc(s_nk, 1)
            for m in range(2):
                rotated(m, sk[:, m, :], L, SEQ)
            for m in range(KD):
                b = BASE["swa_q"] + m
                dve.wait_ge(used, b + 1)
                nc.vector.scalar_tensor_tensor(sq_q[:, m, :], bank("swa_q", m)[:, 0:SEQ], -0.125, rx[:, META:], ALU.mult, ALU.mult).then_inc(s_q, 1)
                dve.wait_ge(s_q, m + 1)
                dve.sem_inc(acc_used, 1)
                ahead(b)
                if m:
                    rotated(m + 1, sq_q[:, m - 1, :], SEQ, SEQ + META)
            rotated(KD + 1, sq_q[:, KD - 1, :], SEQ, SEQ + META)
            dve.wait_ge(s_nk, 1)
            dve.wait_ge(s_mask, 3)

            def least(n):
                j, h = SUNITS[n]
                dve.wait_ge(s_s, n + 1)
                if n >= 2:
                    dve.wait_ge(s_es, n - 1)
                b = 2 * (n % 2)
                for qt, (c, e, q) in enumerate(SQ):
                    ins = nc.vector.tensor_tensor_reduce(sS[:, n % 2, c:c + e], acc[n % 2][:, c:c + e], smask[:, c:c + e], 1.0,
                                                         snk[:, 2 * j + h:2 * j + h + 1], ALU.add, ALU.min, sstat[:, b + qt:b + qt + 1])
                ins.then_inc(s_min, 1)

            least(0)
            for n in range(len(SUNITS)):
                b = 2 * (n % 2)
                if n + 1 < len(SUNITS):
                    least(n + 1)
                dve.wait_ge(s_es, n + 1)
                tot = sstat[:, 24:26]
                if n:
                    dve.wait_ge(s_p, n)
                step(nc.vector.tensor_tensor(tot, sstat[:, 8 + b:10 + b], sstat[:, 16 + b:18 + b], ALU.add))
                step(nc.vector.reciprocal(tot, tot))
                for qt, (c, e, q) in enumerate(SQ):
                    ins = nc.vector.tensor_scalar(sP[:, n % 2, c:c + e], sP[:, n % 2, c:c + e], tot[:, qt:qt + 1], None, ALU.mult)
                ins.then_inc(s_p, 1)
                if n % 2 == 1 and n > 1:
                    attn_lo(dve, n // 2 - 1, 3)
                dve.wait_ge(s_pt, n + 1)
                if n >= 2:
                    dve.wait_ge(s_o, n - 1)
                nc.vector.tensor_copy(sPM[0:META, n % 2, :], (stat, mix[2])[n % 2][0:META, 0:SEQ]).then_inc(s_pmc, 1)
            attn_lo(dve, KD - 1, 3)
            for m in range(KD):
                tail(9, m, "swa_out", BASE["swa_out"] + m)
            post_norm(9)

        mixers["pool"][8], mixers["pe"][8], mixers["act"][8], mixers["dve"][8] = swa_pool, swa_pe, swa_act, swa_dve
        block = ctx.enter_context(nc.Block())

        @block.sync
        def _(sp):
            for s in range(RING):
                sp.dma_start(raw[:, s, :], a["w"][s]).then_inc(raw_in[s], 16)
            with sp.Fori(1, HALVES // RING) as i:
                for s in range(RING):
                    sp.wait_ge(w_lo, RING * i - RING + s + 1)
                    sp.dma_start(raw[:, s, :], a["w"][bass.ds(RING * i + s, 1)].rearrange("a p n -> p (a n)")) \
                        .then_inc(raw_in[s], 16)
            for n in range(HALVES // RING * RING, HALVES):
                sp.wait_ge(w_lo, n - RING + 1)
                sp.dma_start(raw[:, n % RING, :], a["w"][n]).then_inc(raw_in[n % RING], 16)
            for k in range(KD):
                sp.wait_ge(x_new, 8 * upto + k + 9)
                sp.dma_start(out[k], x[:, k, META:]).then_inc(out_ok, 16)
            sp.wait_ge(out_ok, 16 * KD)

        @block.gpsimd
        def _(pool):
            step = Chain(pool, pool_step)
            pool.memset(ones[:], 1.0 / D).then_inc(const_ok, 1)
            for n, v in enumerate((1e-6, 4e-6, 1e-5, HALF_PI, 64e-6)):
                pool.memset(eps[:, n:n + 1], v).then_inc(const_ok, 1)

            tables_pool(pool, step)

            def norm_sum(v, c):
                pool.wait_ge(sq_new, 8 * v + 2)
                if v:
                    pool.wait_ge(mean_ok, v)
                step(pool.tensor_tensor(sumsq[:, c:], sq[:, 0, c:], sq[:, 1, c:], ALU.add))
                for k in range(2, KD):
                    pool.wait_ge(sq_new, 8 * v + k + 1)
                    ins = pool.tensor_tensor(sumsq[:, c:], sumsq[:, c:], sq[:, k, c:], ALU.add)
                    if k < KD - 1:
                        step(ins)
                ins.then_inc(sum_ok, 1)

            def post_update(u):
                norm_sum(norm_of(u, True), c0(u))
                for k in range(KD):
                    pool.wait_ge(t_new, 8 * (u - 5) + k + 1)
                    pool.tensor_tensor(x[:, k, c0(u):], x[:, k, c0(u):], y[:, k, c0(u):], ALU.add).then_inc(x_new, 1)

            for u in range(0, upto + 1):
                if u in mixers.get("pool", {}):
                    mixers["pool"][u](pool, step)
                if u >= 5:
                    post_update(u)
                if u < upto:
                    norm_sum(norm_of(u), c0(u))

        @block.tensor
        def _(pe):
            pe.wait_ge(const_ok, 6)

            def half(h, q, name, t, part, hi, lo, c, kt, wait):
                pe.wait_ge(w_lo, h.n + 1)
                if part == 0 and q is not None:
                    pe.wait_ge(acc_used, q - 3)
                ks = range(part * KD, min(kt, part * KD + KD))
                for k in ks:
                    if wait:
                        pe.wait_ge(wait[0], wait[1] + k + 1)
                    w = slice((k % KD) * P, (k % KD + 1) * P)
                    for w_part, v_part in ((wh, hi), (wh, lo), (wl, hi)):
                        ins = nc.tensor.matmul(bank(name, t)[:, 0:L - c], w_part[:, h.slot, w], v_part[:, k, c:],
                                               start=(k == 0 and w_part is wh and v_part is hi),
                                               stop=(k == kt - 1 and w_part is wl))
                ins.then_inc(used, 1)

            def gemm(name, hi, lo, c, wait, kt=KD, only=None):
                parts = -(-kt // KD)
                body = 4 * parts
                rounds = SIZE[name] // body

                def tiles(i, ts):
                    for t in ts:
                        for part in range(parts):
                            b = BASE[name] + t * parts + part
                            q = TILE[name] + t + 4 * i
                            if isinstance(q, int) and q < 4:
                                q = None
                            half(Half(b, i * parts), q, name, t, part, hi, lo, c, kt,
                                 wait if t == 0 else None)

                if only is not None:
                    tiles(0, [only])
                    return
                if rounds > 1:
                    if TILE[name] < 4:
                        tiles(0, range(4))
                        with pe.Fori(1, rounds) as i:
                            tiles(i, range(4))
                    else:
                        with pe.Fori(0, rounds) as i:
                            tiles(i, range(4))
                elif rounds:
                    tiles(0, range(4))
                tiles(0, range(4 * rounds, SIZE[name] // parts))

            def mean(v, c):
                pe.wait_ge(sum_ok, v + 1)
                if v:
                    pe.wait_ge(root_ok, v)
                nc.tensor.matmul(stat[:, 0:L - c], ones[:], sumsq[:, c:], start=True, stop=True).then_inc(mean_ok, 1)

            def ffn(f, u):
                gemm(f"ffn{f}_a", xh, xl, cg(u), (x_lo, 8 * u), KD)
                gemm(f"ffn{f}_b", hh, hl, cg(u), (f_lo, KF * f), KF)

            for u in range(0, upto):
                mean(norm_of(u), c0(u))
                if u == 7:
                    kv_pe(pe, gemm)
                f = FFN_AFTER.get(u)
                if f is not None:
                    ffn(f, u)
                else:
                    mixers["pe"][u](pe, gemm)
                if u + 1 >= 5:
                    mean(norm_of(u + 1, True), c0(u + 1))

        @block.scalar
        def _(act):
            step = Chain(act, act_step)

            def split(h):
                act.wait_ge(raw_in[h.slot], 16 * h.round + 16)
                if not (isinstance(h.n, int) and h.n < RING):
                    act.wait_ge(used, h.n - RING + 1)
                nc.scalar.activation(wh[:, h.slot, :], raw[:, h.slot, :], ACT.Copy).then_inc(w_hi, 1)

            def ahead(b, i=0):
                if not isinstance(i, int) or b + RING * i + RING < HALVES:
                    split(Half(b + RING, i))

            def x_parts(u, k):
                c = c0(u)
                act.wait_ge(x_new, 8 * u + 8 + k + 1 if u else 16)
                if u < upto:
                    nc.scalar.activation(xh[:, k, c:], x[:, k, c:], ACT.Copy, scale=col(NEXT_GAIN[u], k)).then_inc(x_hi, 1)
                    squares(x, norm_of(u), k, c)

            def squares(src, v, k, c):
                if v:
                    act.wait_ge(sum_ok, v)
                nc.scalar.activation(sq[:, k, c:], src[:, k, c:], ACT.Square).then_inc(sq_new, 1)

            def rooted(v, c, post=False):
                act.wait_ge(mean_ok, v + 1)
                if v:
                    act.wait_ge(rms_ok, v)
                s = 4.0 if post else 1.0
                nc.scalar.activation(root[:, c:], stat[:, 0:L - c], ACT.Sqrt, scale=s,
                                     bias=eps[:, 1:2] if post else eps[:, 0:1]).then_inc(root_ok, 1)

            def ffn(f, u):
                base = BASE[f"ffn{f}_a"]
                c = cg(u)
                with act.Fori(0, KF // 2) as i:
                    for t in range(2):
                        n = KF * f + t + 2 * i + 1
                        act.wait_ge(f_g, n)
                        nc.scalar.activation(ts[:, t, c:], tg[:, t, c:], ACT.Silu).then_inc(f_s, 1)
                        ahead(base + 2 * t, i)
                        ahead(base + 2 * t + 1, i)
                        act.wait_ge(f_h, n)
                        act.wait_ge(const_ok, 6)
                        nc.scalar.activation(hh[:, bass.ds(2 * i + t, 1), c:], th[:, t:t + 1, c:], ACT.Copy).then_inc(f_hi, 1)
                base = BASE[f"ffn{f}_b"]
                for m in range(KD):
                    for part in range(KF_PARTS):
                        ahead(base + m * KF_PARTS + part)
                    residual(u + 1, m)
                if u + 1 >= 5:
                    post_norm(u + 1)

            def residual(u, m):
                if u < 5:
                    x_parts(u, m)
                else:
                    act.wait_ge(y_new, 8 * (u - 5) + m + 1)
                    squares(y, norm_of(u, True), m, c0(u))

            def post_norm(u):
                rooted(norm_of(u, True), c0(u), post=u not in (6, 9))
                for k in range(KD):
                    if u == 7 and u < upto:
                        act.wait_ge(x_new, 8 * u + 8 + k + 1)
                        kv_act(act, k)
                    x_parts(u, k)

            act.dma_start(par[:], a["par"]).then_inc(in_par, 16)
            act.dma_start(x[:], a["x"]).then_inc(x_new, 16)
            act.wait_ge(const_ok, 6)
            for s in range(RING):
                split(Half(s))
            act.wait_ge(in_par, 16)
            for k in range(KD):
                x_parts(0, k)
            tables_act(act)
            for u in range(0, upto):
                rooted(norm_of(u), c0(u))
                if u == 7:
                    for m in range(4):
                        ahead(BASE["kv"] + m)
                f = FFN_AFTER.get(u)
                if f is not None:
                    ffn(f, u)
                else:
                    mixers["act"][u](act, step, ahead, residual, post_norm)

        @block.vector
        def _(dve):
            step = Chain(dve, dve_step)

            def split(h):
                dve.wait_ge(w_hi, h.n + 1)
                nc.vector.tensor_tensor(wl[:, h.slot, :], raw[:, h.slot, :], wh[:, h.slot, :].bitcast(F32),
                                        ALU.subtract).then_inc(w_lo, 1)

            def ahead(b, i=0):
                if not isinstance(i, int) or b + RING * i + RING < HALVES:
                    split(Half(b + RING, i))

            def low_x(u, k):
                if u < upto:
                    c = c0(u)
                    dve.wait_ge(x_hi, 8 * u + k + 1)
                    nc.vector.scalar_tensor_tensor(xl[:, k, c:], x[:, k, c:], col(NEXT_GAIN[u], k),
                                                   xh[:, k, c:].bitcast(F32), ALU.mult, ALU.subtract).then_inc(x_lo, 1)

            def rms(v, c, dst):
                dve.wait_ge(root_ok, v + 1)
                nc.vector.reciprocal(dst[:, c:], root[:, c:]).then_inc(rms_ok, 1)
                dve.wait_ge(rms_ok, v + 1)

            def post_norm(u):
                c = c0(u)
                rms(norm_of(u, True), c, ry)
                for k in range(KD):
                    dve.wait_ge(y_new, 8 * (u - 5) + k + 1)
                    nc.vector.scalar_tensor_tensor(y[:, k, c:], y[:, k, c:], col(POST_GAIN[u], k), ry[:, c:],
                                                   ALU.mult, ALU.mult).then_inc(t_new, 1)
                for k in range(KD):
                    if u == 7 and u < upto:
                        kv_low(dve, k)
                    low_x(u, k)

            def ffn(f, u):
                name = f"ffn{f}_a"
                c = cg(u)
                with dve.Fori(0, KF // 2) as i:
                    def low_h(t):
                        dve.wait_ge(f_hi, KF * f + t + 2 * i + 1)
                        nc.vector.tensor_tensor(hl[:, bass.ds(2 * i + t, 1), c:], th[:, t:t + 1, c:],
                                                hh[:, bass.ds(2 * i + t, 1), c:].bitcast(F32), ALU.subtract).then_inc(f_lo, 1)
                    for t in range(2):
                        n = KF * f + t + 2 * i + 1
                        b = BASE[name] + 2 * t
                        dve.wait_ge(used, Half(b, i).n + 1)
                        nc.vector.tensor_tensor(tg[:, t, c:], bank(name, 2 * t)[:, 0:L - c], rx[:, c:], ALU.mult).then_inc(f_g, 1)
                        dve.wait_ge(f_g, n)
                        if t == 1:
                            low_h(0)
                        ahead(b, i)
                        dve.wait_ge(used, Half(b + 1, i).n + 1)
                        step_u = nc.vector.tensor_tensor(tu[:, t, c:], bank(name, 2 * t + 1)[:, 0:L - c], rx[:, c:], ALU.mult)
                        step_u.then_inc(acc_used, 2)
                        ahead(b + 1, i)
                        dve.wait_ge(acc_used, TILE[name] + 4 * i + 2 * t + 2)
                        dve.wait_ge(f_s, n)
                        nc.vector.tensor_tensor(th[:, t, c:], tu[:, t, c:], ts[:, t, c:], ALU.mult).then_inc(f_h, 1)
                    low_h(1)
                name = f"ffn{f}_b"
                for m in range(KD):
                    for part in range(KF_PARTS):
                        b = BASE[name] + m * KF_PARTS + part
                        if part == KF_PARTS - 1:
                            tail(u + 1, m, name, b)
                        else:
                            ahead(b)
                if u + 1 >= 5:
                    post_norm(u + 1)

            def tail(u, m, name, b):
                dve.wait_ge(used, b + 1)
                c = c0(u)
                if u < 5:
                    nc.vector.tensor_tensor(x[:, m, META:], x[:, m, META:], bank(name, m)[:, 0:SEQ], ALU.add).then_inc(x_new, 1)
                    dve.wait_ge(x_new, 8 * u + 8 + m + 1)
                else:
                    nc.vector.tensor_copy(y[:, m, c:], bank(name, m)[:, 0:L - c]).then_inc(y_new, 1)
                    dve.wait_ge(y_new, 8 * (u - 5) + m + 1)
                dve.sem_inc(acc_used, 1)
                ahead(b)
                if u < 5:
                    low_x(u, m)

            for s in range(RING):
                split(Half(s))
            dve.wait_ge(in_par, 16)
            for k in range(KD):
                low_x(0, k)
            tables_dve(dve, step)
            for u in range(0, upto):
                rms(norm_of(u), c0(u), rx)
                if u == 7:
                    kv_dve(dve, ahead)
                f = FFN_AFTER.get(u)
                if f is not None:
                    ffn(f, u)
                else:
                    mixers["dve"][u](dve, step, ahead, tail, post_norm)


def _tiles(w):
    import numpy as np
    w = np.asarray(w)
    n = w.shape[1]
    pad = -n % P
    if pad:
        w = np.concatenate([w, np.zeros((w.shape[0], pad), w.dtype)], axis=1)
    return np.ascontiguousarray(w.reshape(-1, P, (n + pad) // P, P).transpose(2, 1, 0, 3)).reshape((n + pad) // P, P, -1)


def _pairs(w):
    import numpy as np
    n = w.shape[1] // 2
    return np.stack([_tiles(w[:, :n]), _tiles(w[:, n:])], axis=1).reshape(-1, P, KD * P)


def _down(w):
    import numpy as np
    w = np.asarray(w)
    w = np.concatenate([w, np.zeros((KF_PARTS * D - FF, D), w.dtype)])
    return w.reshape(KF_PARTS, KD, P, KD, P).transpose(3, 0, 2, 1, 4).reshape(-1, P, KD * P)


def _cols(v):
    import numpy as np
    return np.asarray(v).reshape(-1, P).T


def kernel(**t):
    import numpy as np
    import concourse.bacc as bacc
    from concourse.bass_utils import run_bass_kernel_spmd as run

    t = {k: np.asarray(v) for k, v in t.items()}
    half = ROPE // 2
    heads = [g * 4 + r for t2 in range(2) for r in range(4) for g in (2 * t2, 2 * t2 + 1)]
    hcols = np.concatenate([np.arange(h * DH, h * DH + DH) for h in heads])
    nsa, gla = t["nsa_w_in"][0], t["gla_w_in_2"][0]
    w_ffn_in, w_ffn_out = t["w_ffn_in_2"], t["w_ffn_out_2"]
    by_name = {
        "conv_in": _pairs(t["conv_w_in"][0]), "conv_out": _tiles(t["conv_w_out"][0]),
        "nsa_kv": _tiles(nsa[:, 1024:2560]), "nsa_gate": _tiles(nsa[:, 2560:]), "nsa_q": _tiles(nsa[:, hcols]),
        "nsa_out": _tiles(t["nsa_w_out"][0][hcols]),
        "gla_lr": _tiles(gla[:, 3072:]), "gla_k": _tiles(gla[:, 512:1024]), "gla_q": _tiles(gla[:, :512]),
        "gla_v": _tiles(gla[:, 1024:2048]), "gla_r": _tiles(gla[:, 2048:3072]), "gla_out": _tiles(t["gla_w_out_2"][0]),
        "kv": _tiles(t["w_kv_2"]), "swa_q": _tiles(t["swa_w_q_2"][0][:, hcols]), "swa_out": _tiles(t["swa_w_out_2"][0][hcols]),
    }
    for f in range(2):
        by_name[f"ffn{f}_a"], by_name[f"ffn{f}_b"] = _pairs(t["ffn_w_in"][f]), _down(t["ffn_w_out"][f])
    for f in range(4):
        by_name[f"ffn{2 + f}_a"], by_name[f"ffn{2 + f}_b"] = _pairs(w_ffn_in[f // 2, f % 2]), _down(w_ffn_out[f // 2, f % 2])
    stream = np.concatenate([by_name[name] for name, _ in STAGES])
    assert stream.shape[0] == HALVES

    f32 = np.float32
    two = lambda v: np.concatenate([v, v], axis=-1)[..., None]
    conv_b = t["conv_b_in"][0]
    rope = np.zeros((P, 2), f32)
    for h in range(2):
        for d in range(ROPE):
            rope[h * DH + d] = (f32(THETA) ** (-f32(d % half) / f32(half)), -1.0 if d < half else 1.0)
    pieces = {
        "mix0": _cols(t["norm_mix"][0]), "mix1": _cols(t["norm_mix"][1]),
        "ffn0": _cols(t["norm_ffn"][0]), "ffn1": _cols(t["norm_ffn"][1]),
        "conv_ba": _cols(conv_b[:D]), "conv_bg": _cols(conv_b[D:]),
        "conv_w": t["conv_w_dw"][0].reshape(CONV, KD, P).transpose(2, 1, 0).reshape(P, -1),
        "conv_b": _cols(t["conv_b_dw"][0]), "ln_g": _cols(t["conv_ln_g"][0]), "ln_b": _cols(t["conv_ln_b"][0]),
        "q_gain": two(t["nsa_q_gain"][0]), "k_gain": np.tile(t["nsa_k_gain"][0].T, (2, 1)),
        "cmp_b1": np.tile(t["nsa_cmp_b1"][0].T, (2, 1)),
        "cmp_pos": np.tile(t["nsa_cmp_pos"][0].transpose(2, 0, 1).reshape(DH, 64), (2, 1)),
        "g2": _cols(t["norm_gains_2"]), "kv_norm": _cols(t["kv_norm_2"]), "gate_b": _cols(t["gla_b_gate_2"][0]),
        "gla_norm": _cols(t["gla_norm_2"][0]), "sinks": np.broadcast_to(t["swa_sinks_2"][0][heads], (P, 16)),
        "inv_freq": rope[:, 0:1], "rope_sign": rope[:, 1:2],
    }
    arrays = {
        "w": stream,
        "par": np.ascontiguousarray(np.concatenate([pieces[name].reshape(P, n) for name, n in PARAMS], axis=1)),
        "x": np.ascontiguousarray(np.concatenate([t["meta_tokens_2"], t["x"][0]]).T.reshape(KD, P, L).transpose(1, 0, 2)),
        "positions": t["positions"],
        "cmp_w1": np.ascontiguousarray(np.tile(t["nsa_cmp_w1"][0].reshape(2, 32, DH, DH).transpose(2, 0, 1, 3), (2, 1, 1, 1))).reshape(P, -1),
        "cmp_w2": np.ascontiguousarray(t["nsa_cmp_w2"][0].transpose(1, 0, 2)).reshape(DH, -1),
        "w_gate": t["gla_w_gate_2"][0], "gate_row": t["gla_b_gate_2"],
    }
    nc = bacc.Bacc("TRN2", target_bir_lowering=False, num_devices=1)
    drams = {k: nc.dram_tensor("in_" + k, v.shape, mybir.dt.from_np(v.dtype), kind="ExternalInput").ap() for k, v in arrays.items()}
    out = nc.dram_tensor("out", (KD, P, SEQ), F32, kind="ExternalOutput").ap()
    build(nc, drams, out, UPDATES)
    r = run(nc, [{"in_" + k: v for k, v in arrays.items()}], core_ids=[0])
    return np.ascontiguousarray(r.results[0]["out"].reshape(D, SEQ).T)[None]
```

```python
from contextlib import ExitStack

import numpy as np_

import concourse.bass as bass
from concourse import mybir

ALU = mybir.AluOpType
ACT = mybir.ActivationFunctionType
AX = mybir.AxisListType
F32 = mybir.dt.float32
F32R = mybir.dt.float32r
I32 = mybir.dt.int32

P = 128
D = 1024
KD = D // P
SEQ = 256
META = 16
L = SEQ + META
FF = 2816
KF = FF // P
KF_PARTS = -(-KF // KD)
RING = 4
CONV = 31
PE_TAPS = 15
BIG = 1e30
ROPE = 16
THETA = 500000.0
DH = 64
TWO_PI = (6.28125, 0.0019350051879882812, 3.019915981956752e-07)
PI_BELOW = 3.1415925
HALF_PI = 1.5707963267948966
NCMP = (SEQ - 32) // 16 + 1

FFN_A, FFN_B = 2 * KF, KD * KF_PARTS
STAGES = [("conv_in", 16), ("conv_out", 8), ("ffn0_a", FFN_A), ("ffn0_b", FFN_B),
          ("nsa_kv", 12), ("nsa_gate", 1), ("nsa_q", 8), ("nsa_out", 8), ("ffn1_a", FFN_A), ("ffn1_b", FFN_B),
          ("ffn2_a", FFN_A), ("ffn2_b", FFN_B),
          ("gla_lr", 1), ("gla_k", 4), ("gla_q", 4), ("gla_v", 8), ("gla_r", 8), ("gla_out", 8),
          ("ffn3_a", FFN_A), ("ffn3_b", FFN_B), ("kv", 4),
          ("ffn4_a", FFN_A), ("ffn4_b", FFN_B), ("swa_q", 8), ("swa_out", 8),
          ("ffn5_a", FFN_A), ("ffn5_b", FFN_B)]
BASE, TILE, SIZE = {}, {}, {}
HALVES = TILES = 0
for _name, _n in STAGES:
    BASE[_name], TILE[_name], SIZE[_name] = HALVES, TILES, _n
    HALVES += _n
    TILES += _n // KF_PARTS if _name.endswith("_b") else _n

PARAMS = [("mix0", 8), ("ffn0", 8), ("mix1", 8), ("ffn1", 8),
          ("conv_ba", 8), ("conv_bg", 8), ("conv_w", 8 * CONV), ("conv_b", 8), ("ln_g", 8), ("ln_b", 8),
          ("q_gain", 1), ("k_gain", 3), ("cmp_b1", 2), ("cmp_pos", 64),
          ("g2", 96), ("kv_norm", 8), ("gate_b", 4), ("gla_norm", 2), ("sinks", 16),
          ("inv_freq", 1), ("rope_sign", 1)]
COL = {}
_c = 0
for _name, _n in PARAMS:
    COL[_name] = _c
    _c += _n
NPAR = _c

NEXT_GAIN = [COL["mix0"], COL["ffn0"], COL["mix1"], COL["ffn1"]] + \
            [COL["g2"] + 8 * g for g in (0, 2, 4)] + [COL["g2"] + 48 + 8 * g for g in (0, 2, 4)]
POST_GAIN = {u: COL["g2"] + 48 * (n // 3) + 8 * (1 + 2 * (n % 3)) for n, u in enumerate(range(5, 11))}


def last(name):
    return BASE[name] + SIZE[name]


class Half:

    def __init__(self, b, i=0):
        self.slot = b % RING
        self.round = b // RING + i
        self.n = b + RING * i


class Chain:

    def __init__(self, eng, sem):
        self.eng, self.sem, self.n, self.i, self.per, self.at = eng, sem, 0, None, 0, 0

    def __call__(self, ins):
        self.n += 1
        ins.then_inc(self.sem, 1)
        self.eng.wait_ge(self.sem, self.n if self.i is None else self.n + self.i * self.per)

    def enter(self, i, per):
        self.i, self.per, self.at = (None, 0, self.n) if isinstance(i, int) else (i, per, self.n)
        return self

    def leave(self, rounds):
        if self.i is not None:
            assert self.n - self.at == self.per, (self.n - self.at, self.per)
            self.n = self.at + self.per * rounds
            self.i = None

SCRATCH = 12360
UPDATES = 10
FFN_AFTER = {1: 0, 3: 1, 4: 2, 6: 3, 7: 4, 9: 5}


def build(nc, a, out, upto):
    with ExitStack() as ctx:
        def sb(name, shape, dt=F32):
            return ctx.enter_context(nc.sbuf_tensor(name, shape, dt))

        def sem(name):
            return ctx.enter_context(nc.semaphore(name))

        x = sb("x", [P, KD, L])
        xh, xl = sb("xh", [P, KD, L], F32R), sb("xl", [P, KD, L], F32R)
        sq = sb("sq", [P, KD, L])
        y = sb("y", [P, KD, L])
        sumsq, root, rx, ry = sb("sumsq", [P, L]), sb("root", [P, L]), sb("rx", [P, L]), sb("ry", [P, L])
        hh, hl = sb("hh", [P, KF, L], F32R), sb("hl", [P, KF, L], F32R)
        raw = sb("raw", [P, RING, KD * P])
        wh, wl = sb("wh", [P, RING, KD * P], F32R), sb("wl", [P, RING, KD * P], F32R)
        par = sb("par", [P, NPAR])
        tg, ts, tu, th = (sb(n, [P, 2, L]) for n in ("tg", "ts", "tu", "th"))
        ones, ones4 = sb("ones", [P, P]), sb("ones4", [P, P])
        eps = sb("eps", [P, 5])
        scr = sb("scr", [P, SCRATCH])

        acc = [ctx.enter_context(nc.psum_tensor(f"acc{i}", [P, 512], F32)) for i in range(4)]
        stat = ctx.enter_context(nc.psum_tensor("stat", [P, 512], F32))
        mix = [ctx.enter_context(nc.psum_tensor(f"mix{i}", [P, 512], F32)) for i in range(3)]

        const_ok = sem("const_ok")
        in_x, in_par = sem("in_x"), sem("in_par")
        raw_in = [sem(f"raw_in{i}") for i in range(RING)]
        w_hi, w_lo, used, acc_used = sem("w_hi"), sem("w_lo"), sem("used"), sem("acc_used")
        x_new = [sem("x_even"), sem("x_odd")]
        x_hi, x_lo = sem("x_hi"), sem("x_lo")
        sq_new, sum_ok, mean_ok, root_ok, rms_ok = (sem(n) for n in ("sq_new", "sum_ok", "mean_ok", "root_ok", "rms_ok"))
        y_new, t_new = sem("y_new"), sem("t_new")
        f_g, f_s, f_h, f_hi, f_lo = (sem(n) for n in ("f_g", "f_s", "f_h", "f_hi", "f_lo"))
        m_hi, m_lo = sem("m_hi"), sem("m_lo")
        out_ok = sem("out_ok")
        dve_step, act_step, pool_step = sem("dve_step"), sem("act_step"), sem("pool_step")

        def col(name, k=0):
            c = (COL[name] if isinstance(name, str) else name) + k
            return par[:, c:c + 1]

        def c0(u):
            return 0 if 4 <= u <= 7 else META

        def cg(u):
            return max(c0(u), c0(u + 1))

        def norm_of(u, post=False):
            return u if u < 5 else 5 + 2 * (u - 5) + (not post)

        def bank(name, t):
            return acc[(TILE[name] + t) % 4]

        def updated(u, k):
            return 4 * (u - 1) + k // 2 + 1

        def halved(v):
            return v in [norm_of(u, True) for u in (5, 7, 8, 10)]

        mixers = {}
        cu = scr[:, 0:KD * (SEQ + CONV - 1)].rearrange("p (k t) -> p k t", k=KD)
        _o = KD * (SEQ + CONV - 1)
        cv = scr[:, _o:_o + KD * SEQ].rearrange("p (k t) -> p k t", k=KD)
        _o += KD * SEQ
        cw = scr[:, _o:_o + 4 * SEQ].rearrange("p (b k t) -> p b k t", b=2, k=2)
        _o = 8200
        cdiag = scr[:, _o:_o + 2 * PE_TAPS * P].rearrange("p (b n c) -> p b n c", b=2, n=PE_TAPS)
        c_u, c_diag, c_pe = sem("c_u"), sem("c_diag"), sem("c_pe")
        c_g, c_s, c_v, c_mu, c_d, c_sq, c_var, c_root, c_z, c_w, c_pad, c_tap = (
            sem(n) for n in ("c_g", "c_s", "c_v", "c_mu", "c_d", "c_sq", "c_var", "c_root", "c_z", "c_w", "c_pad", "c_tap"))

        def conv_pool(pool, step):
            pool.memset(cu[:, :, 0:CONV - 1], 0.0).then_inc(c_pad, 1)

        def conv_pe(pe, gemm, begin, opening):
            begin(0, ("conv_in", 0), ("conv_in", 1))
            for j in range(KD + 2):
                if 0 < j < KD:
                    gemm("conv_in", xh, xl, META, None, first=2 * j, last=2 * j + 2)
                if 0 < j <= KD:
                    pe.wait_ge(c_u, j)
                    pe.wait_ge(c_diag, j)
                    if j >= 3:
                        pe.wait_ge(c_v, j - 2)
                    for n in range(PE_TAPS):
                        s = CONV - PE_TAPS + n
                        ins = nc.tensor.matmul(mix[1 + j % 2][:, 0:SEQ], cdiag[:, j % 2, n, :], cu[:, j - 1, s:s + SEQ],
                                               start=(n == 0), stop=(n == PE_TAPS - 1))
                    ins.then_inc(c_pe, 1)
                if j >= 2:
                    pe.wait_ge(c_v, j - 1)
                    ins = nc.tensor.matmul(mix[0][:, 0:SEQ], ones[:], cv[:, j - 2, :], start=(j == 2), stop=(j == KD + 1))
            ins.then_inc(c_mu, 1)
            for j in range(KD):
                pe.wait_ge(c_sq, j + 1)
                ins = nc.tensor.matmul(mix[1][:, 0:SEQ], ones[:], sq[:, j, META:], start=(j == 0), stop=(j == KD - 1))
            ins.then_inc(c_var, 1)
            opening((("conv_out", 0), ("conv_out", 1)), hh, hl, META, (m_lo, 0))
            gemm("conv_out", hh, hl, META, None, first=2)

        def conv_act(act, step, ahead, residual):
            def diagonals(j):
                if j >= 2:
                    act.wait_ge(c_pe, j - 1)
                for n in range(PE_TAPS):
                    ins = nc.scalar.activation(cdiag[:, (j + 1) % 2, n, :], ident[:], ACT.Copy,
                                               scale=col("conv_w", CONV * j + CONV - PE_TAPS + n))
                ins.then_inc(c_diag, 1)

            act.wait_ge(shape_ok, 1)
            diagonals(0)
            for j in range(KD):
                b = BASE["conv_in"] + 2 * j
                ahead(b)
                act.wait_ge(c_g, j + 1)
                if j >= 2:
                    act.wait_ge(c_u, j - 1)
                nc.scalar.activation(ts[:, j % 2, META:], tg[:, j % 2, META:], ACT.Sigmoid, bias=col("conv_bg", j)).then_inc(c_s, 1)
                ahead(b + 1)
                if j + 1 < KD:
                    diagonals(j + 1)
            act.wait_ge(sum_ok, 1)
            for j in range(KD):
                act.wait_ge(c_d, j + 1)
                nc.scalar.activation(sq[:, j, META:], cv[:, j, :], ACT.Square).then_inc(c_sq, 1)
            act.wait_ge(c_var, 1)
            act.wait_ge(rms_ok, 1)
            nc.scalar.activation(root[:, META:], mix[1][:, 0:SEQ], ACT.Sqrt, bias=eps[:, 2:3]).then_inc(c_root, 1)
            for j in range(KD):
                act.wait_ge(c_z, j + 1)
                nc.scalar.activation(cv[:, j, :], cv[:, j, :], ACT.Silu, scale=col("ln_g", j), bias=col("ln_b", j)).then_inc(c_w, 1)
                act.wait_ge(c_w, j + 1)
                nc.scalar.activation(hh[:, j, META:], cv[:, j, :], ACT.Copy).then_inc(m_hi, 1)
            for m in range(KD):
                residual(1, m, BASE["conv_out"] + m)

        def conv_dve(dve, step, ahead, tail):
            taps = 0

            def low(j):
                dve.wait_ge(m_hi, j + 1)
                nc.vector.tensor_tensor(hl[:, j, META:], cv[:, j, :], hh[:, j, META:].bitcast(F32), ALU.subtract).then_inc(m_lo, 1)

            def summed(j):
                dve.wait_ge(c_tap, (j + 1) * (CONV - PE_TAPS))
                dve.wait_ge(c_pe, j + 1)
                step(nc.vector.tensor_tensor(cv[:, j, :], cw[:, j % 2, 0, :], mix[1 + (j + 1) % 2][:, 0:SEQ], ALU.add))
                nc.vector.tensor_tensor(cv[:, j, :], cv[:, j, :], cw[:, j % 2, 1, :], ALU.add).then_inc(c_v, 1)
                dve.wait_ge(c_v, j + 1)

            for j in range(KD):
                b = BASE["conv_in"] + 2 * j
                dve.wait_ge(used, b + 1)
                step(nc.vector.tensor_tensor(tu[:, j % 2, META:], bank("conv_in", 2 * j)[:, 0:SEQ], rx[:, META:], ALU.mult))
                ahead(b)
                dve.wait_ge(used, b + 2)
                nc.vector.tensor_tensor(tg[:, j % 2, META:], bank("conv_in", 2 * j + 1)[:, 0:SEQ], rx[:, META:], ALU.mult).then_inc(c_g, 1)
                dve.wait_ge(c_g, j + 1)
                dve.sem_inc(acc_used, 2)
                ahead(b + 1)
                dve.wait_ge(c_s, j + 1)
                dve.wait_ge(c_pad, 1)
                nc.vector.scalar_tensor_tensor(cu[:, j, CONV - 1:], tu[:, j % 2, META:], col("conv_ba", j),
                                               ts[:, j % 2, META:], ALU.add, ALU.mult).then_inc(c_u, 1)
                dve.wait_ge(c_u, j + 1)
                for n in range(CONV - PE_TAPS):
                    if n >= 2:
                        dve.wait_ge(c_tap, taps - 1)
                    w = col("conv_w", CONV * j + n)
                    if n == 0:
                        ins = nc.vector.tensor_scalar(cw[:, j % 2, 0, :], cu[:, j, 0:SEQ], w, col("conv_b", j), ALU.mult, ALU.add)
                    elif n == 1:
                        ins = nc.vector.tensor_scalar(cw[:, j % 2, 1, :], cu[:, j, 1:1 + SEQ], w, None, ALU.mult)
                    else:
                        ins = nc.vector.scalar_tensor_tensor(cw[:, j % 2, n % 2, :], cu[:, j, n:n + SEQ], w, cw[:, j % 2, n % 2, :], ALU.mult, ALU.add)
                    ins.then_inc(c_tap, 1)
                    taps += 1
                if j:
                    summed(j - 1)
            summed(KD - 1)
            dve.wait_ge(c_mu, 1)
            for j in range(KD):
                nc.vector.tensor_tensor(cv[:, j, :], cv[:, j, :], mix[0][:, 0:SEQ], ALU.subtract).then_inc(c_d, 1)
            dve.wait_ge(c_root, 1)
            step(nc.vector.reciprocal(ry[:, META:], root[:, META:]))
            for j in range(KD):
                dve.wait_ge(c_sq, j + 1)
                nc.vector.tensor_tensor(cv[:, j, :], cv[:, j, :], ry[:, META:], ALU.mult).then_inc(c_z, 1)
                if j:
                    low(j - 1)
            low(KD - 1)
            for m in range(KD):
                tail(1, m, "conv_out", BASE["conv_out"] + m)

        mixers.setdefault("pool", {})[0] = conv_pool
        mixers.setdefault("pe", {})[0] = conv_pe
        mixers.setdefault("act", {})[0] = conv_act
        mixers.setdefault("dve", {})[0] = conv_dve
        ident, rot, bones, rowmask = sb("ident", [P, P]), sb("rot", [P, P]), sb("bones", [P, P]), sb("rowmask", [P, 4])
        cosT, sinT = sb("cosT", [P, SEQ + L]), sb("sinT", [P, SEQ + L])
        tab_ok, in_pos, shape_ok = sem("tab_ok"), sem("in_pos"), sem("shape_ok")
        tpos, tang, tint, tred = (scr[:, 6000 + n * 528:6528 + n * 528] for n in range(4))

        def tables_pool(pool, step):
            pool.iota(tpos[:, SEQ:], [[1, L]], base=0, channel_multiplier=0, allow_small_or_imprecise_dtypes=True).then_inc(tab_ok, 1)
            pool.dma_start(tint[:, 0:SEQ].bitcast(I32), a["positions"].partition_broadcast(P)).then_inc(in_pos, 16)
            step(pool.memset(ident[:], 0.0))
            step(pool.memset(rot[:], 0.0))
            step(pool.memset(bones[:], 0.0))
            step(pool.memset(rowmask[:], 0.0))
            shapes = [0]

            def shape(ins):
                shapes[0] += 1
                ins.then_inc(shape_ok, 1)
                pool.wait_ge(shape_ok, shapes[0])

            shape(pool.affine_select(out=ident[:], in_=ident[:], compare_op=ALU.not_equal, fill=1.0, base=0,
                                     pattern=[[-1, P]], channel_multiplier=1))
            for h in range(2):
                for s in range(2):
                    v = rot[:, DH * h + 8 * s:DH * h + 8 * s + 8]
                    shape(pool.affine_select(out=v, in_=v, compare_op=ALU.not_equal, fill=1.0, base=-(DH * h + 8 * (1 - s)),
                                             pattern=[[-1, 8]], channel_multiplier=1))
                shape(pool.memset(bones[DH * h:DH * h + DH, DH * h:DH * h + DH], 1.0 / DH))
            for r in range(4):
                shape(pool.memset(rowmask[32 * r:32 * r + 32, r:r + 1], 1.0))

        def tables_dve(dve, step):
            dve.wait_ge(in_pos, 16)
            dve.wait_ge(in_par, 16)
            dve.wait_ge(tab_ok, 1)
            step(nc.vector.tensor_copy(tpos[:, 0:SEQ], tint[:, 0:SEQ].bitcast(I32)))
            step(nc.vector.tensor_scalar(tang, tpos, col("inv_freq"), None, ALU.mult))
            step(nc.vector.tensor_scalar(tint.bitcast(I32), tang, float(np_.float32(1 / (2 * np_.pi))), None, ALU.mult))
            step(nc.vector.tensor_copy(tred, tint.bitcast(I32)))
            for part in TWO_PI:
                step(nc.vector.scalar_tensor_tensor(tang, tred, -part, tang, ALU.mult, ALU.add))
            step(nc.vector.tensor_scalar(tang, tang, PI_BELOW, -PI_BELOW, ALU.min, ALU.max))
            nc.vector.scalar_tensor_tensor(tred, tang, -1.0, tang, ALU.mult, ALU.max).then_inc(tab_ok, 1)
            dve.wait_ge(tab_ok, 4)
            nc.vector.tensor_scalar(sinT[:], sinT[:], col("rope_sign"), None, ALU.mult).then_inc(tab_ok, 1)

        def tables_act(act):
            act.wait_ge(tab_ok, 2)
            nc.scalar.activation(sinT[:], tang, ACT.Sin).then_inc(tab_ok, 1)
            nc.scalar.activation(cosT[:], tred, ACT.Sin, scale=-1.0, bias=eps[:, 3:4]).then_inc(tab_ok, 1)

        at = {"o": 0}

        def area(n):
            at["o"] += n
            assert at["o"] <= SCRATCH, at["o"]
            return scr[:, at["o"] - n:at["o"]]

        nw1 = area(4096).rearrange("p (c l e) -> p c l e", c=2, l=32)
        nw2 = area(128).rearrange("p (c e) -> p c e", c=2)
        nk = area(1536).rearrange("p (m t) -> p m t", m=6)
        nvt = area(1024).rearrange("p (b n) -> p b n", b=2)
        ngate = area(96).rearrange("p (a n) -> p a n", a=2)
        nkc = area(32).rearrange("p (t n) -> p t n", t=2)
        nhk = area(64).rearrange("p (g n) -> p g n", g=4)
        nhv = area(512).rearrange("p (g r n) -> p g r n", g=4, r=4)
        nvc = area(1024).rearrange("p (g r d) -> p g r d", g=4, r=4)
        nmask = area(384)
        ncm = area(32).rearrange("p (a n) -> p a n", a=2)
        nc01 = area(32).rearrange("p (a n) -> p a n", a=2)
        nbias = area(2)
        nstat = area(64)
        nroot = area(512).rearrange("p (b t) -> p b t", b=2)
        nr = area(256)
        nt = area(256)
        _sm = area(2304)
        nsq = _sm[:, 0:2048].rearrange("p (m t) -> p m t", m=8)
        nS, nP, nPT = (_sm[:, 768 * n:768 * n + 768].rearrange("p (b n) -> p b n", b=2) for n in range(3))
        nq = sq[:, :, META:]
        nv = y[:, :, META:]
        npc = scr[:, 0:1024].rearrange("p (h b n) -> p h b n", h=2, b=4)
        npct = scr[:, 1024:2048].rearrange("p (h t q) -> p h t q", h=2, t=2)
        ncs = scr[:, 2048:2560].rearrange("p (h a n) -> p h a n", h=2, a=2)
        n_w, n_a, n_v, n_gate, n_sig, n_sq, n_mean, n_root, n_n, n_perm, n_k = (
            sem("n_" + s) for s in ("w", "a", "v", "gate", "sig", "sq", "mean", "root", "n", "perm", "k"))
        n_mask, n_tr, n_vt, n_gt, n_hid, n_pos, n_gelu, n_comp, n_kc, n_vc = (
            sem("n_" + s) for s in ("mask", "tr", "vt", "gt", "hid", "pos", "gelu", "comp", "kc", "vc"))
        n_cs, n_cexp, n_csub, n_cp, n_ct, n_cpt = (sem("n_" + s) for s in ("cs", "cexp", "csub", "cp", "ct", "cpt"))
        n_s, n_min, n_exp, n_p, n_pt, n_ptc, n_o = (sem("n_" + s) for s in ("s", "min", "exp", "p", "pt", "ptc", "o"))
        KTILES = (0, 1, 4, 5, 8, 9)
        VTILES = (2, 3, 6, 7, 10, 11)
        UNITS = [(j, h, b) for j in range(KD) for h in range(2) for b in range(2)]

        def nsa_pool(pool, step):
            pool.wait_ge(m_lo, 8)
            pool.wait_ge(tab_ok, 5)
            pool.dma_start(nw1, a["cmp_w1"].rearrange("p (c l e) -> p c l e", c=2, l=32)).then_inc(n_w, 16)
            pool.dma_start(nw2[0:DH], a["cmp_w2"].rearrange("p (c e) -> p c e", c=2)).then_inc(n_w, 16)
            step(pool.memset(nmask, 0.0))
            step(pool.memset(ncm, 0.0))
            step(pool.memset(nc01, 1.0))
            for s in (0, 256):
                pool.affine_select(out=nmask[:, s:s + P], in_=nmask[:, s:s + P], compare_op=ALU.is_ge, fill=BIG, base=0,
                                   pattern=[[-1, P]], channel_multiplier=1).then_inc(n_mask, 1)
            for m, fill in ((ncm, BIG), (nc01, 0.0)):
                pool.affine_select(out=m, in_=m, compare_op=ALU.is_ge, fill=fill, base=-31,
                                   pattern=[[P, 2], [-16, 16]], channel_multiplier=1).then_inc(n_mask, 1)
            pool.memset(nhk, 0.0).then_inc(n_mask, 1)
            pool.memset(nhv, 0.0).then_inc(n_mask, 1)

        def nsa_pe(pe, gemm, begin, opening):
            pe.wait_ge(shape_ok, 11)

            def mean(m):
                pe.wait_ge(n_sq, m + 1)
                if m >= 1:
                    pe.wait_ge(n_root, m if m < 6 else m - 3 if m >= 10 else 6)
                nc.tensor.matmul(mean_bank(m)[:, 0:SEQ], bones[:], nsq[:, m % 8, :], start=True, stop=True).then_inc(n_mean, 1)

            def perm(m):
                pe.wait_ge(n_n, m + 1)
                if m >= 2:
                    pe.wait_ge(n_k, m - 1)
                v = nk[:, m, :] if m < 6 else nq[:, m - 6, :]
                nc.tensor.matmul(mix[1 + m % 2][:, 0:SEQ], rot[:], v, start=True, stop=True).then_inc(n_perm, 1)

            begin(2, ("nsa_kv", 0), ("nsa_kv", 1))
            gemm("nsa_kv", xh, xl, META, None, first=2)
            gemm("nsa_gate", xh, xl, META, None)
            for m in range(KD):
                if m < 6:
                    mean(m)
                gemm("nsa_q", xh, xl, META, None, first=m, last=m + 1)
                if m < 6:
                    perm(m)
            pe.wait_ge(acc_used, TILE["nsa_q"] + 8)
            for m in range(6, 10):
                mean(m)
            pe.wait_ge(n_sig, 1)
            for qt in range(2):
                ins = nc.tensor.transpose(stat[:, P * qt:P * qt + P], tg[:, 1, META + P * qt:META + P * qt + P], ident[:])
            ins.then_inc(n_tr, 1)
            perm(6)
            for m in range(10, 14):
                mean(m)
                perm(m - 3)
            pe.wait_ge(n_w, 32)
            pe.wait_ge(n_k, 2)
            pe.wait_ge(n_v, 2)
            pe.wait_ge(n_root, 14)
            for l in range(32):
                for c in range(2):
                    ins = nc.tensor.matmul(acc[2][0:DH, c:c + 1], nw1[0:DH, c, l, :], par[0:DH, COL["cmp_pos"] + 32 * c + l:COL["cmp_pos"] + 32 * c + l + 1],
                                           start=(l == 0 and c == 0), stop=(l == 31), skip_group_check=True)
            ins.then_inc(n_pos, 1)
            for h in range(2):
                for c in range(2):
                    src = (nk, nv)[c]
                    for l in range(32):
                        ins = nc.tensor.matmul(acc[h][0:DH, 32 * c:32 * c + 2 * NCMP], nw1[DH * h:DH * h + DH, c, l, :],
                                               src[DH * h:DH * h + DH, 0:2, l:l + 16 * (NCMP - 1) + 1:16],
                                               start=(l == 0), stop=(l == 31))
                ins.then_inc(n_hid, 1)
            for m in range(11, 14):
                perm(m)
            pe.wait_ge(n_v, 6)
            pe.wait_ge(n_gt, 1)
            for b in range(2):
                for kt in range(2):
                    for t in range(2):
                        ins = nc.tensor.transpose((stat, acc[3])[b][:, 256 * kt + P * t:256 * kt + P * t + P],
                                                  nv[:, 2 + 2 * b + t, P * kt:P * kt + P], ident[:])
                ins.then_inc(n_tr, 1)
            pe.wait_ge(n_gelu, 6)
            for h in range(2):
                for t in range(2):
                    nc.tensor.matmul(acc[2][DH * h:DH * h + DH, 16 * t:16 * t + 16], nw2[0:DH, 0, :], nhk[0:DH, 2 * t + h, :],
                                     start=(t == 0), stop=True, skip_group_check=True)
            for g in range(4):
                ins = nc.tensor.matmul(mix[0][:, DH * g:DH * g + DH], nhv[0:DH, g].rearrange("p r n -> p (r n)"), nw2[0:DH, 1, :],
                                       start=True, stop=True)
            ins.then_inc(n_comp, 1)
            pe.wait_ge(n_kc, 1)
            pe.wait_ge(n_k, 14)
            for h in range(2):
                for qt in range(2):
                    for j in range(KD):
                        ins = nc.tensor.matmul(acc[h][:, P * qt + 16 * j:P * qt + 16 * j + 16], nq[DH * h:DH * h + DH, j, P * qt:P * qt + P],
                                               nkc[DH * h:DH * h + DH, j // 4, :], start=True, stop=True)
                ins.then_inc(n_cs, 1)

            def scores(n):
                j, h, b = UNITS[n]
                if n >= 3:
                    pe.wait_ge(n_min, n - 2)
                else:
                    pe.wait_ge(n_csub, 2)
                for qt in range(2):
                    ins = nc.tensor.matmul(acc[n % 3][:, P * qt:P * qt + P * (qt + 1)], nq[DH * h:DH * h + DH, j, P * qt:P * qt + P],
                                           nk[DH * h:DH * h + DH, 2 + 2 * b + j // 4, 0:P * (qt + 1)], start=True, stop=True)
                ins.then_inc(n_s, 1)

            def turned(n):
                pe.wait_ge(n_p, n + 1)
                if n >= 2:
                    pe.wait_ge(n_ptc, n - 1)
                else:
                    pe.wait_ge(n_cpt, 4)
                dst = (acc[3], stat)[n % 2]
                for at_, src in ((0, 0), (P, P), (2 * P, 2 * P)):
                    ins = nc.tensor.transpose(dst[:, at_:at_ + P], nP[:, n % 2, src:src + P], ident[:])
                ins.then_inc(n_pt, 1)

            def values(n):
                j, h, b = UNITS[n]
                t = j // 4
                g = 2 * t + h
                dst = mix[j % 2][DH * h:DH * h + DH]
                if b == 0:
                    if j >= 2:
                        pe.wait_ge(m_lo, 8 + j - 1)
                    nc.tensor.matmul(dst[:, 0:SEQ], nvc[:, g, j % 4, :], npct[:, h, t, :], start=True, stop=False)
                pe.wait_ge(n_ptc, n + 1)
                nc.tensor.matmul(dst[:, 0:SEQ], nvt[:, b, DH * g:DH * g + DH], nPT[:, n % 2, 0:SEQ], start=False, stop=False)
                ins = nc.tensor.matmul(dst[:, P:SEQ], nvt[:, b, 256 + DH * g:256 + DH * g + DH], nPT[:, n % 2, SEQ:SEQ + P],
                                       start=False, stop=(b == 1))
                ins.then_inc(n_o, 1)

            scores(0)
            scores(1)
            pe.wait_ge(n_cp, 2)
            for h in range(2):
                for t in range(2):
                    pe.wait_ge(n_vt, 2)
                    if t == 1 or h == 1:
                        pe.wait_ge(n_cpt, 2 * h + t)
                    for qt in range(2):
                        ins = nc.tensor.transpose(stat[:, P * qt:P * qt + P], npc[:, h, 2 * qt + t, :], ident[:])
                    ins.then_inc(n_ct, 1)
            pe.wait_ge(n_vc, 4)
            for n in range(len(UNITS) + 1):
                if n + 2 < len(UNITS):
                    scores(n + 2)
                if n < len(UNITS):
                    turned(n)
                if n:
                    values(n - 1)
            pe.wait_ge(m_lo, 16)
            gemm("nsa_out", hh, hl, META, (m_lo, 8))

        def mean_bank(m):
            return mix[0] if m < 6 else acc[(m - 6) % 4]

        def nsa_act(act, step, ahead, residual):
            def squared(m, src, more=None):
                act.wait_ge(n_a, m + 1)
                if m >= 8:
                    act.wait_ge(n_mean, m - 7)
                nc.scalar.activation(nsq[:, m % 8, :], src, ACT.Square).then_inc(n_sq, 1)

            def rooted(m):
                act.wait_ge(n_mean, m + 1)
                if m >= 2:
                    act.wait_ge(n_n, m - 1)
                s = 1.0 if m < 6 else 64.0
                nc.scalar.activation(nroot[:, m % 2, :], mean_bank(m)[:, 0:SEQ], ACT.Sqrt, scale=s,
                                     bias=eps[:, 0:1] if m < 6 else eps[:, 4:5]).then_inc(n_root, 1)

            for m in range(12):
                ahead(BASE["nsa_kv"] + m)
                if m in KTILES:
                    i = KTILES.index(m)
                    squared(i, nk[:, i, :])
            act.wait_ge(n_gate, 1)
            nc.scalar.activation(tg[:, 1, META:], tg[:, 0, META:], ACT.Sigmoid).then_inc(n_sig, 1)
            ahead(BASE["nsa_gate"])
            for m in range(KD):
                if m < 6:
                    rooted(m)
                ahead(BASE["nsa_q"] + m)
                squared(6 + m, nq[:, m, :])
            for m in range(6, 14):
                rooted(m)
            act.wait_ge(n_hid, 2)
            act.wait_ge(n_pos, 2)
            act.wait_ge(n_mask, 6)
            for h in range(2):
                nc.scalar.activation(nhk[0:DH, h:4:2, 0:NCMP], acc[h][0:DH, 0:2 * NCMP].rearrange("p (t n) -> p t n", t=2),
                                     ACT.Gelu_apprx_tanh, bias=nbias[0:DH, 0:1]).then_inc(n_gelu, 1)
                for t in range(2):
                    src = acc[h][0:DH, 32 + NCMP * t:32 + NCMP * t + NCMP]
                    nc.scalar.activation(nhv[0:DH, 2 * t + h, :, 0:NCMP], src.unsqueeze(1).to_broadcast([DH, 4, NCMP]),
                                         ACT.Gelu_apprx_tanh, bias=nbias[0:DH, 1:2]).then_inc(n_gelu, 1)
            act.wait_ge(n_tr, 3)
            nc.scalar.activation(nvt[:, 0, :], stat[:, :], ACT.Copy).then_inc(n_vt, 1)
            nc.scalar.activation(nvt[:, 1, :], acc[3][:, :], ACT.Copy).then_inc(n_vt, 1)
            for h in range(2):
                act.wait_ge(n_csub, h + 1)
                nc.scalar.activation(ncs[:, h], ncs[:, h], ACT.Exp, scale=-1.0).then_inc(n_cexp, 1)

            def exps(n):
                act.wait_ge(n_min, n + 1)
                if n >= 2:
                    act.wait_ge(n_pt, n - 1)
                for qt in range(2):
                    s = slice(P * qt, P * qt + P * (qt + 1))
                    act.wait_ge(n_p, n - 1) if n >= 2 else None
                    nc.scalar.activation(nP[:, n % 2, s], nS[:, n % 2, s], ACT.Exp, scale=-1.0, bias=nstat[:, 2 * (n % 2) + qt:2 * (n % 2) + qt + 1],
                                         accum_out=nstat[:, 8 + 2 * (n % 2) + qt:9 + 2 * (n % 2) + qt]).then_inc(n_exp, 1)

            exps(0)
            for n in range(4):
                h, t = divmod(n, 2)
                act.wait_ge(n_ct, n + 1)
                nc.scalar.activation(npct[:, h, t, :], stat[:, 0:SEQ], ACT.Copy).then_inc(n_cpt, 1)
            for n in range(len(UNITS)):
                if n + 1 < len(UNITS):
                    exps(n + 1)
                act.wait_ge(n_pt, n + 1)
                if n >= 2:
                    act.wait_ge(n_o, n - 1)
                nc.scalar.activation(nPT[:, n % 2, :], (acc[3], stat)[n % 2][:, 0:384], ACT.Copy).then_inc(n_ptc, 1)
                if n % 4 == 0 and n:
                    attn_hi(act, n // 4 - 1, n_o, n)
            attn_hi(act, KD - 1, n_o, len(UNITS))
            for m in range(KD):
                residual(3, m, BASE["nsa_out"] + m)

        def attn_hi(act, j, o, count, idx=1):
            act.wait_ge(o, count)
            nc.scalar.activation(hh[:, j, META:], mix[j % 2][:, 0:SEQ], ACT.Copy).then_inc(m_hi, 1)

        def attn_lo(dve, j, idx=1):
            dve.wait_ge(m_hi, 8 * idx + j + 1)
            nc.vector.tensor_tensor(hl[:, j, META:], mix[j % 2][:, 0:SEQ], hh[:, j, META:].bitcast(F32), ALU.subtract).then_inc(m_lo, 1)

        def nsa_dve(dve, step, ahead, tail):
            def normed(m):
                v = nk[:, m, :] if m < 6 else nq[:, m - 6, :]
                dve.wait_ge(n_root, m + 1)
                if m:
                    dve.wait_ge(n_n, m)
                step(nc.vector.reciprocal(nr, nroot[:, m % 2, :]))
                nc.vector.scalar_tensor_tensor(v, v, col("k_gain", m // 2) if m < 6 else col("q_gain"), nr,
                                               ALU.mult, ALU.mult).then_inc(n_n, 1)

            def rotated(m):
                v = nk[:, m, :] if m < 6 else nq[:, m - 6, :]
                dve.wait_ge(n_perm, m + 1)
                if m:
                    dve.wait_ge(n_k, m)
                step(nc.vector.tensor_tensor(nt, mix[1 + m % 2][:, 0:SEQ], sinT[:, 0:SEQ], ALU.mult))
                step(nc.vector.tensor_tensor(v, v, cosT[:, 0:SEQ], ALU.mult))
                nc.vector.tensor_tensor(v, v, nt, ALU.add).then_inc(n_k, 1)

            dve.wait_ge(tab_ok, 5)
            for m in range(12):
                b = BASE["nsa_kv"] + m
                dve.wait_ge(used, b + 1)
                if m in KTILES:
                    ins = nc.vector.tensor_tensor(nk[:, KTILES.index(m), :], bank("nsa_kv", m)[:, 0:SEQ], rx[:, META:], ALU.mult)
                    ins.then_inc(n_a, 1)
                    dve.wait_ge(n_a, KTILES.index(m) + 1)
                else:
                    ins = nc.vector.tensor_tensor(nv[:, VTILES.index(m), :], bank("nsa_kv", m)[:, 0:SEQ], rx[:, META:], ALU.mult)
                    ins.then_inc(n_v, 1)
                    dve.wait_ge(n_v, VTILES.index(m) + 1)
                dve.sem_inc(acc_used, 1)
                ahead(b)
            dve.wait_ge(used, BASE["nsa_gate"] + 1)
            nc.vector.tensor_tensor(tg[:, 0, META:], bank("nsa_gate", 0)[:, 0:SEQ], rx[:, META:], ALU.mult).then_inc(n_gate, 1)
            dve.wait_ge(n_gate, 1)
            dve.sem_inc(acc_used, 1)
            ahead(BASE["nsa_gate"])
            for m in range(KD):
                if m < 6:
                    normed(m)
                dve.wait_ge(used, BASE["nsa_q"] + m + 1)
                dve.wait_ge(sum_ok, 3)
                nc.vector.scalar_tensor_tensor(nq[:, m, :], bank("nsa_q", m)[:, 0:SEQ], -1.0, rx[:, META:],
                                               ALU.mult, ALU.mult).then_inc(n_a, 1)
                dve.wait_ge(n_a, 6 + m + 1)
                dve.sem_inc(acc_used, 1)
                ahead(BASE["nsa_q"] + m)
                if m < 6:
                    rotated(m)
            normed(6)
            dve.wait_ge(n_tr, 1)
            nc.vector.tensor_copy(ngate, stat[:, 0:SEQ].rearrange("p (a n) -> p a n", a=2)[:, :, 0:48]).then_inc(n_gt, 1)
            for m in range(7, 14):
                normed(m)
                rotated(m - 1)
            dve.wait_ge(n_pos, 1)
            nc.vector.tensor_tensor(nbias[0:DH, :], acc[2][0:DH, 0:2], par[0:DH, COL["cmp_b1"]:COL["cmp_b1"] + 2], ALU.add).then_inc(n_pos, 1)
            rotated(13)
            dve.wait_ge(n_comp, 1)
            nc.vector.tensor_copy(nkc, acc[2][:, 0:32].rearrange("p (t n) -> p t n", t=2)).then_inc(n_kc, 1)
            for r in range(4):
                nc.vector.tensor_scalar(nvc[:, :, r, :], mix[0][:, 0:SEQ].rearrange("p (g d) -> p g d", g=4), rowmask[:, r:r + 1],
                                        None, ALU.mult).then_inc(n_vc, 1)
            step(nc.vector.memset(npc.rearrange("p h b n -> p (h b n)"), 0.0))
            for h in range(2):
                dve.wait_ge(n_cs, h + 1)
                s = ncs[:, h].rearrange("p a (j n) -> p a j n", j=KD)
                step(nc.vector.tensor_tensor(s, acc[h][:, 0:SEQ].rearrange("p (a j n) -> p a j n", a=2, j=KD),
                                             ncm.unsqueeze(2).to_broadcast([P, 2, KD, 16]), ALU.add))
                least = nstat[:, 16:32].rearrange("p (a j) -> p a j", a=2)
                step(nc.vector.tensor_reduce(least, s, AX.X, ALU.min))
                nc.vector.tensor_tensor(s, s, least.unsqueeze(3).to_broadcast([P, 2, KD, 16]), ALU.subtract).then_inc(n_csub, 1)
            for h in range(2):
                dve.wait_ge(n_cexp, h + 1)
                s = ncs[:, h].rearrange("p a (j n) -> p a j n", j=KD)
                tot = nstat[:, 32:48]
                tot3 = tot.rearrange("p (a j) -> p a j", a=2)
                step(nc.vector.tensor_reduce(tot3, s, AX.X, ALU.add))
                step(nc.vector.reciprocal(tot, tot))
                step(nc.vector.tensor_tensor(tot.rearrange("p (a t r) -> p a t r", a=2, t=2), tot.rearrange("p (a t r) -> p a t r", a=2, t=2),
                                             ngate[:, :, 0:16].rearrange("p a (t g r) -> p a t g r", t=2, g=2)[:, :, :, h, :], ALU.mult))
                step(nc.vector.tensor_tensor(s, s, tot3.unsqueeze(3).to_broadcast([P, 2, KD, 16]), ALU.mult))
                nc.vector.tensor_tensor(npc[:, h].rearrange("p (a t) (r n) -> p a (t r) n", a=2, n=32)[:, :, :, 0:16], s,
                                        nc01.unsqueeze(2).to_broadcast([P, 2, KD, 16]), ALU.mult).then_inc(n_cp, 1)

            def least(n):
                dve.wait_ge(n_s, n + 1)
                dve.wait_ge(n_mask, 4)
                if n >= 2:
                    dve.wait_ge(n_exp, 2 * n - 2)
                for qt in range(2):
                    s = slice(P * qt, P * qt + P * (qt + 1))
                    ins = nc.vector.tensor_tensor_reduce(nS[:, n % 2, s], acc[n % 3][:, s], nmask[:, s], 1.0, 3e38, ALU.add,
                                                         ALU.min, nstat[:, 2 * (n % 2) + qt:2 * (n % 2) + qt + 1])
                ins.then_inc(n_min, 1)

            least(0)
            for n in range(len(UNITS)):
                if n + 1 < len(UNITS):
                    least(n + 1)
                j, h, b = UNITS[n]
                head = 8 * (j // 4) + 4 * h + j % 4
                dve.wait_ge(n_exp, 2 * n + 2)
                rec = nstat[:, 12:14]
                if n:
                    dve.wait_ge(n_p, n)
                step(nc.vector.reciprocal(rec, nstat[:, 8 + 2 * (n % 2):10 + 2 * (n % 2)]))
                for qt in range(2):
                    s = slice(P * qt, P * qt + P * (qt + 1))
                    g = 16 * (b + 1) + head
                    ins = nc.vector.tensor_scalar(nP[:, n % 2, s], nP[:, n % 2, s], rec[:, qt:qt + 1], ngate[:, qt, g:g + 1],
                                                  ALU.mult, ALU.mult)
                ins.then_inc(n_p, 1)
                if n % 4 == 1 and n > 4:
                    attn_lo(dve, n // 4 - 1)
            attn_lo(dve, KD - 1)
            for m in range(KD):
                tail(3, m, "nsa_out", BASE["nsa_out"] + m)

        mixers["pool"][2], mixers["pe"][2], mixers["act"][2], mixers["dve"][2] = nsa_pool, nsa_pe, nsa_act, nsa_dve
        at["o"] = 0
        gls = area(1536).rearrange("p (a n) -> p a n", a=3)
        ge = area(1536).rearrange("p (a n) -> p a n", a=3)
        gv = scr[:, 0:3072].rearrange("p (a n) -> p a n", a=3)
        gb = area(1088).rearrange("p (h t) -> p h t", h=4)
        gkk = area(1088).rearrange("p (h t) -> p h t", h=4)
        gq = area(1088).rearrange("p (h t) -> p h t", h=4)
        gk = area(1088).rearrange("p (h t) -> p h t", h=4)
        gkt = area(1536).rearrange("p (a n) -> p a n", a=3)
        gS = area(1024).rearrange("p (h n) -> p h n", h=4)
        gatt = area(512).rearrange("p (b h n) -> p b h n", b=2, h=4)
        gwg = area(512)
        gdec = area(20).rearrange("p (h n) -> p h n", h=4)
        gtri = area(128)
        gsq = scr[:, 3072:3072 + 2176].rearrange("p (m t) -> p m t", m=8)
        gkr, gqr = (tg, ts), (tu, th)
        g_w, g_tri, g_lr, g_z, g_e, g_ln, g_ls, g_kr, g_b, g_bc, g_qr, g_dif, g_eq = (
            sem("g_" + s) for s in ("w", "tri", "lr", "z", "e", "ln", "ls", "kr", "b", "bc", "qr", "dif", "eq"))
        g_dec, g_v, g_vt, g_vc, g_kt, g_kc, g_r, g_rs, g_att, g_attc, g_kv, g_S, g_o, g_oc = (
            sem("g_" + s) for s in ("dec", "v", "vt", "vc", "kt", "kc", "r", "rs", "att", "attc", "kv", "S", "o", "oc"))
        g_sq, g_mean, g_root, g_f = (sem("g_" + s) for s in ("sq", "mean", "root", "f"))
        TOK = ((0, META), (META, P), (META + P, P))
        CHUNKS = [(0, META, 0, 0)] + [(META + 64 * n, 64, 1 + n // 2, 64 * (n % 2)) for n in range(4)]

        def gla_pool(pool, step):
            pool.wait_ge(m_lo, 16)
            step(pool.memset(gwg[0:64, :], 0.0))
            pool.dma_start(gwg[0:16, :], a["w_gate"]).then_inc(g_w, 16)
            pool.dma_start(gwg[32:33, :], a["gate_row"]).then_inc(g_w, 16)
            step(pool.memset(gtri, 1.0))
            step(pool.affine_select(out=gtri, in_=gtri, compare_op=ALU.is_ge, fill=0.0, base=0, pattern=[[1, P]], channel_multiplier=-1))
            pool.memset(gtri[0:64, 64:P], 0.0).then_inc(g_tri, 1)
            pool.memset(gatt.rearrange("p b h n -> p (b h n)"), 0.0).then_inc(g_tri, 1)

        def gla_pe(pe, gemm, begin, opening):
            begin(5, ("gla_lr", 0), ("gla_k", 0))
            pe.wait_ge(g_w, 32)
            pe.wait_ge(g_lr, 2)
            for n, (s, w) in enumerate(TOK):
                ins = nc.tensor.matmul(mix[n][0:w, :], ry[0:33, s:s + w], gwg[0:33, :], start=True, stop=True)
            ins.then_inc(g_z, 1)
            gemm("gla_k", xh, xl, 0, None, first=1)
            pe.wait_ge(g_ls, 3)
            pe.wait_ge(g_tri, 2)
            for h in range(4):
                for n, (s, w) in enumerate(TOK):
                    ins = nc.tensor.matmul((mix + [stat])[h][:, s:s + w], gls[0:w, n, P * h:P * h + P], gtri[0:w, 0:w], start=True, stop=True)
                ins.then_inc(g_b, 1)
            gemm("gla_q", xh, xl, 0, None)
            gemm("gla_v", xh, xl, 0, None)
            pe.wait_ge(g_bc, 4)
            for n, (s, w) in enumerate(TOK):
                for e in range(2):
                    i = 2 * n + e
                    pe.wait_ge(g_v, 4 * e + 4)
                    if i >= 3:
                        pe.wait_ge(g_vc, i - 2)
                    for m in range(4):
                        ins = nc.tensor.transpose(mix[i % 3][0:w, P * m:P * m + P], y[:, 4 * e + m, s:s + w], ident[:])
                    ins.then_inc(g_vt, 1)
            pe.wait_ge(g_eq, 12)
            for n, (s, w) in enumerate(TOK):
                pe.wait_ge(g_vc, 4 + n)
                for h in range(4):
                    ins = nc.tensor.transpose(mix[n][0:w, P * h:P * h + P], gkk[:, h, s:s + w], ident[:])
                ins.then_inc(g_kt, 1)
            gemm("gla_r", xh, xl, 0, None)
            pe.wait_ge(acc_used, TILE["gla_r"] + 8)
            pe.wait_ge(g_kc, 3)

            def att(c):
                s, w, n, base = CHUNKS[c]
                if c >= 2:
                    pe.wait_ge(g_attc, c - 1)
                for h in range(4):
                    ins = nc.tensor.matmul(acc[c % 2][base:base + w, 64 * h:64 * h + w], gk[:, h, s:s + w], gq[:, h, s:s + w],
                                           start=True, stop=True)
                ins.then_inc(g_att, 1)

            def kv(c):
                s, w, n, base = CHUNKS[c]
                if c:
                    pe.wait_ge(g_S, 4 * c)
                for h in range(4):
                    ins = nc.tensor.matmul((mix[2], stat)[h // 2][:, 256 * (h % 2):256 * (h % 2) + 256], gkt[base:base + w, n, P * h:P * h + P],
                                           gv[base:base + w, n, 256 * h:256 * h + 256], start=True, stop=True)
                ins.then_inc(g_kv, 1)

            att(0)
            kv(0)
            for c, (s, w, n, base) in enumerate(CHUNKS):
                if c + 1 < 5:
                    att(c + 1)
                pe.wait_ge(g_attc, c + 1)
                if c >= 2:
                    pe.wait_ge(g_oc, c - 1)
                for h in range(4):
                    if c:
                        pe.wait_ge(g_S, 4 * (c - 1) + h + 1)
                    for v in range(2):
                        dst = acc[2 + c % 2][:, 64 * (2 * h + v):64 * (2 * h + v) + w]
                        ins = nc.tensor.matmul(dst, gv[base:base + w, n, 256 * h + P * v:256 * h + P * v + P], gatt[base:base + w, c % 2, h, 0:w],
                                               start=True, stop=(c == 0))
                        if c:
                            ins = nc.tensor.matmul(dst, gS[:, h, P * v:P * v + P], gq[:, h, s:s + w], start=False, stop=True)
                ins.then_inc(g_o, 1)
                if 0 < c + 1 < 4:
                    kv(c + 1)
            for h in range(4):
                pe.wait_ge(g_sq, 2 * h + 2)
                if h == 3:
                    pe.wait_ge(g_root, 1)
                for v in range(2):
                    ins = nc.tensor.matmul(mix[h % 3][:, 0:L], ones[:], gsq[:, 2 * h + v, :], start=(v == 0), stop=(v == 1))
                ins.then_inc(g_mean, 1)
            opening((("gla_out", 0), ("gla_out", 1)), hh, hl, 0, (m_lo, 16))
            gemm("gla_out", hh, hl, 0, None, first=2)

        def gla_act(act, step, ahead, residual):
            ahead(BASE["gla_lr"])
            act.wait_ge(g_z, 1)
            for n, (s, w) in enumerate(TOK):
                nc.scalar.activation(ge[0:w, n, :], mix[n][0:w, :], ACT.Abs).then_inc(g_e, 1)
            for m in range(2):
                ahead(BASE["gla_k"] + m)
            for n, (s, w) in enumerate(TOK):
                act.wait_ge(g_e, n + 1)
                nc.scalar.activation(ge[0:w, n, :], ge[0:w, n, :], ACT.Exp, scale=-1.0).then_inc(g_e, 1)
            act.wait_ge(g_e, 6)
            for n, (s, w) in enumerate(TOK):
                nc.scalar.activation(ge[0:w, n, :], ge[0:w, n, :], ACT.Ln, bias=1.0).then_inc(g_ln, 1)
            for m in range(2, 4):
                ahead(BASE["gla_k"] + m)
            for h in range(4):
                act.wait_ge(g_b, h + 1)
                src = (mix + [stat])[h][:, 0:L]
                nc.scalar.activation(gb[:, h, :], src, ACT.Copy).then_inc(g_bc, 1)
                nc.scalar.activation(gq[:, h, :], src, ACT.Exp, scale=1.0 / 16).then_inc(g_e, 1)
                nc.scalar.activation(gk[:, h, :], src, ACT.Exp, scale=-1.0 / 16).then_inc(g_e, 1)
                ahead(BASE["gla_q"] + h)
            act.wait_ge(g_bc, 4)
            act.wait_ge(g_dif, 3)
            nc.scalar.activation(gkk.rearrange("p h t -> p (h t)"), gkk.rearrange("p h t -> p (h t)"), ACT.Exp, scale=1.0 / 16).then_inc(g_e, 1)
            nc.scalar.activation(gdec.rearrange("p h t -> p (h t)"), gdec.rearrange("p h t -> p (h t)"), ACT.Exp, scale=1.0 / 16).then_inc(g_dec, 1)
            for m in range(KD):
                ahead(BASE["gla_v"] + m)
            for i in range(6):
                n, e = divmod(i, 2)
                act.wait_ge(g_vt, i + 1)
                w = TOK[n][1]
                nc.scalar.activation(gv[0:w, n, 512 * e:512 * e + 512], mix[i % 3][0:w, :], ACT.Copy).then_inc(g_vc, 1)
            for n in range(3):
                act.wait_ge(g_kt, n + 1)
                w = TOK[n][1]
                nc.scalar.activation(gkt[0:w, n, :], mix[n][0:w, :], ACT.Copy).then_inc(g_kc, 1)
            for m in range(KD):
                ahead(BASE["gla_r"] + m)
                act.wait_ge(g_r, m + 1)
                nc.scalar.activation(sq[:, m, :], sq[:, m, :], ACT.Silu).then_inc(g_rs, 1)
            for c, (s, w, n, base) in enumerate(CHUNKS):
                act.wait_ge(g_o, c + 1)
                nc.scalar.activation(y[:, :, s:s + w], acc[2 + c % 2][:, :].rearrange("p (m t) -> p m t", m=8)[:, :, 0:w], ACT.Copy).then_inc(g_oc, 1)
            act.wait_ge(g_oc, 5)
            for m in range(KD):
                nc.scalar.activation(gsq[:, m, :], y[:, m, :], ACT.Square).then_inc(g_sq, 1)
            for h in range(4):
                act.wait_ge(g_mean, h + 1)
                nc.scalar.activation(gsq[:, 2 * h, :], mix[h % 3][:, 0:L], ACT.Sqrt, scale=4.0, bias=eps[:, 0:1]).then_inc(g_root, 1)
            for m in range(KD):
                act.wait_ge(g_f, m + 1)
                nc.scalar.activation(hh[:, m, :], y[:, m, :], ACT.Copy).then_inc(m_hi, 1)
            for m in range(KD):
                residual(6, m, BASE["gla_out"] + m)

        def gla_dve(dve, step, ahead, tail):
            def evac(name, m, out_, signal, count, scale=None):
                b = BASE[name] + m
                dve.wait_ge(used, b + 1)
                src = bank(name, m)[:, 0:L]
                if scale is None:
                    ins = nc.vector.tensor_tensor(out_, src, rx[:], ALU.mult)
                else:
                    ins = nc.vector.scalar_tensor_tensor(out_, src, scale, rx[:], ALU.mult, ALU.mult)
                ins.then_inc(signal, 1)
                dve.wait_ge(signal, count)
                dve.sem_inc(acc_used, 1)
                ahead(b)

            evac("gla_lr", 0, ry[:], g_lr, 1)
            nc.vector.memset(ry[32:33, :], 1.0).then_inc(g_lr, 1)
            for m in range(4):
                evac("gla_k", m, gkr[m // 2][:, m % 2, :], g_kr, m + 1)
                if m:
                    n, w = m - 1, TOK[m - 1][1]
                    dve.wait_ge(g_ln, n + 1)
                    nc.vector.scalar_tensor_tensor(gls[0:w, n, :], mix[n][0:w, :], 0.0, ge[0:w, n, :], ALU.min, ALU.subtract).then_inc(g_ls, 1)
            for m in range(4):
                evac("gla_q", m, gqr[m // 2][:, m % 2, :], g_qr, m + 1, float(P) ** -0.5)
            dve.wait_ge(g_bc, 4)
            for h in range(4):
                v = gb[:, h, META:].rearrange("p (c t) -> p c t", c=4)
                nc.vector.tensor_tensor(gkk[:, h, META:].rearrange("p (c t) -> p c t", c=4), v[:, :, 63:64].to_broadcast([P, 4, 64]), v,
                                        ALU.subtract).then_inc(g_dif, 1) if h == 3 else \
                    nc.vector.tensor_tensor(gkk[:, h, META:].rearrange("p (c t) -> p c t", c=4), v[:, :, 63:64].to_broadcast([P, 4, 64]), v,
                                            ALU.subtract)
            nc.vector.tensor_tensor(gkk[:, :, 0:META], gb[:, :, META - 1:META].to_broadcast([P, 4, META]), gb[:, :, 0:META],
                                    ALU.subtract).then_inc(g_dif, 1)
            nc.vector.tensor_copy(gdec, gb[:, :, META - 1:L:64]).then_inc(g_dif, 1)
            for m in range(KD):
                evac("gla_v", m, y[:, m, :], g_v, m + 1)
                if m < 4:
                    r, q = gkr[m // 2][:, m % 2, :], gqr[m // 2][:, m % 2, :]
                    dve.wait_ge(g_e, 15)
                    nc.vector.tensor_tensor(gq[:, m, :], gq[:, m, :], q, ALU.mult).then_inc(g_eq, 1)
                    nc.vector.tensor_tensor(gk[:, m, :], gk[:, m, :], r, ALU.mult).then_inc(g_eq, 1)
                    nc.vector.tensor_tensor(gkk[:, m, :], gkk[:, m, :], r, ALU.mult).then_inc(g_eq, 1)
            dve.wait_ge(sum_ok, norm_of(5) + 1)
            for m in range(KD):
                evac("gla_r", m, sq[:, m, :], g_r, m + 1)
            dve.wait_ge(g_dec, 1)

            def masked(c):
                s, w, n, base = CHUNKS[c]
                dve.wait_ge(g_att, c + 1)
                if c >= 2:
                    dve.wait_ge(g_o, c - 1)
                rows = slice(base, base + w)
                mask = gtri[rows, base:base + w].bitcast(I32).unsqueeze(1).to_broadcast([w, 4, w])
                nc.vector.copy_predicated(gatt[rows, c % 2, :, 0:w], mask,
                                          acc[c % 2][rows, 0:256].rearrange("p (h t) -> p h t", h=4)[:, :, 0:w]).then_inc(g_attc, 1)

            masked(0)
            for c in range(5):
                if c + 1 < 5:
                    masked(c + 1)
                if c < 4:
                    dve.wait_ge(g_kv, c + 1)
                    if c:
                        dve.wait_ge(g_o, c + 1)
                    for h in range(4):
                        src = (mix[2], stat)[h // 2][:, 256 * (h % 2):256 * (h % 2) + 256]
                        if c == 0:
                            nc.vector.tensor_copy(gS[:, h, :], src).then_inc(g_S, 1)
                        else:
                            nc.vector.scalar_tensor_tensor(gS[:, h, :], gS[:, h, :], gdec[:, h, c:c + 1], src, ALU.mult, ALU.add).then_inc(g_S, 1)
                    dve.wait_ge(g_S, 4 * c + 4)
            dve.wait_ge(g_rs, 8)

            def low(m):
                dve.wait_ge(m_hi, 16 + m + 1)
                nc.vector.tensor_tensor(hl[:, m, :], y[:, m, :], hh[:, m, :].bitcast(F32), ALU.subtract).then_inc(m_lo, 1)

            for h in range(4):
                dve.wait_ge(g_root, h + 1)
                step(nc.vector.reciprocal(gsq[:, 2 * h, :], gsq[:, 2 * h, :]))
                for v in range(2):
                    m = 2 * h + v
                    step(nc.vector.scalar_tensor_tensor(y[:, m, :], y[:, m, :], col("gla_norm", v), gsq[:, 2 * h, :], ALU.mult, ALU.mult))
                    nc.vector.tensor_tensor(y[:, m, :], y[:, m, :], sq[:, m, :], ALU.mult).then_inc(g_f, 1)
                    if m:
                        low(m - 1)
            low(7)
            for m in range(KD):
                tail(6, m, "gla_out", BASE["gla_out"] + m)

        mixers["pool"][5], mixers["pe"][5], mixers["act"][5], mixers["dve"][5] = gla_pool, gla_pe, gla_act, gla_dve
        at["o"] = 0
        sk = area(544).rearrange("p (m t) -> p m t", m=2)
        svt = area(544).rearrange("p (m t) -> p m t", m=2)
        sv = area(768).rearrange("p (a n) -> p a n", a=3)
        smask = area(416)
        snk = area(16)
        sstat = area(32)
        snt = area(272)
        sS = area(832).rearrange("p (b n) -> p b n", b=2)
        sP = area(832).rearrange("p (b n) -> p b n", b=2)
        sPT = area(768).rearrange("p (b n) -> p b n", b=2)
        sPM = area(512).rearrange("p (b n) -> p b n", b=2)
        sq_q = y[:, :, META:]
        kv_hi, kv_lo, s_kv, s_q, s_perm, s_k, s_tr, s_v, s_mask, s_nk = (
            sem("s_" + n) for n in ("kvhi", "kvlo", "kv", "q", "perm", "k", "tr", "v", "mask", "nk"))
        s_s, s_min, s_exp, s_es, s_p, s_pt, s_ptc, s_pmc, s_o = (
            sem("s_" + n) for n in ("s", "min", "exp", "es", "p", "pt", "ptc", "pmc", "o"))
        SUNITS = [(j, h) for j in range(KD) for h in range(2)]
        SQ = ((0, 144, 0), (144, 272, P))

        def swa_pool(pool, step):
            pool.wait_ge(m_lo, 24)
            step(pool.memset(smask, 0.0))
            for s in (META, 144 + META + P):
                v = smask[:, s:s + P]
                pool.affine_select(out=v, in_=v, compare_op=ALU.is_ge, fill=BIG, base=0, pattern=[[-1, P]], channel_multiplier=1).then_inc(s_mask, 1)
            v = smask[:, 144 + META:144 + META + P]
            pool.affine_select(out=v, in_=v, compare_op=ALU.is_gt, fill=BIG, base=0, pattern=[[1, P]], channel_multiplier=-1).then_inc(s_mask, 1)

        def kv_pe(pe, gemm, opening, mean):
            opening((("kv", 0), ("kv", 1)), hh, hl, 0, (kv_lo, 0))
            gemm("kv", hh, hl, 0, None, first=2, last=3)
            mean(norm_of(7), c0(7))
            gemm("kv", hh, hl, 0, None, first=3)

        def kv_act(act, k):
            nc.scalar.activation(hh[:, k, :], x[:, k, :], ACT.Copy, scale=col("kv_norm", k)).then_inc(kv_hi, 1)

        def kv_low(dve, k):
            dve.wait_ge(kv_hi, k + 1)
            nc.vector.scalar_tensor_tensor(hl[:, k, :], x[:, k, :], col("kv_norm", k), hh[:, k, :].bitcast(F32), ALU.mult, ALU.subtract).then_inc(kv_lo, 1)

        def kv_dve(dve, ahead):
            for m in range(4):
                b = BASE["kv"] + m
                dve.wait_ge(used, b + 1)
                nc.vector.tensor_tensor((sk, svt)[m // 2][:, m % 2, :], bank("kv", m)[:, 0:L], rx[:], ALU.mult).then_inc(s_kv, 1)
                dve.wait_ge(s_kv, m + 1)
                dve.sem_inc(acc_used, 1)
                ahead(b)

        def swa_pe(pe, gemm, begin, opening):
            begin(8, ("swa_q", 0), ("swa_q", 1))
            pe.wait_ge(s_kv, 4)
            for m in range(2):
                ins = nc.tensor.matmul(mix[1 + m][:, 0:L], rot[:], sk[:, m, :], start=True, stop=True)
                ins.then_inc(s_perm, 1)
            pe.wait_ge(root_ok, norm_of(8) + 1)
            for kt in range(2):
                for t in range(2):
                    nc.tensor.transpose(stat[:, 256 * kt + P * t:256 * kt + P * t + P], svt[:, t, META + P * kt:META + P * kt + P], ident[:])
            for t in range(2):
                ins = nc.tensor.transpose(mix[0][0:META, P * t:P * t + P], svt[:, t, 0:META], ident[:])
            ins.then_inc(s_tr, 1)

            def perm(m):
                pe.wait_ge(s_q, m + 1)
                pe.wait_ge(s_k, m + 1)
                nc.tensor.matmul(mix[1 + m % 2][:, 0:SEQ], rot[:], sq_q[:, m, :], start=True, stop=True).then_inc(s_perm, 1)

            for m in range(KD):
                if m >= 2:
                    gemm("swa_q", xh, xl, META, None, first=m, last=m + 1)
                if m:
                    perm(m - 1)
            perm(KD - 1)
            pe.wait_ge(acc_used, TILE["swa_q"] + 8)
            pe.wait_ge(s_v, 2)

            def scores(n):
                j, h = SUNITS[n]
                pe.wait_ge(s_k, 2 + j + 1)
                if n >= 2:
                    pe.wait_ge(s_min, n - 1)
                for qt, (c, e, q) in enumerate(SQ):
                    ins = nc.tensor.matmul(acc[n % 2][:, c:c + e], sq_q[DH * h:DH * h + DH, j, q:q + P], sk[DH * h:DH * h + DH, j // 4, 0:e],
                                           start=True, stop=True)
                ins.then_inc(s_s, 1)

            def turned(n):
                pe.wait_ge(s_p, n + 1)
                if n >= 2:
                    pe.wait_ge(s_ptc, n - 1)
                    pe.wait_ge(s_pmc, n - 1)
                for d, s in ((0, META), (P, 144 + META), (2 * P, 144 + META + P)):
                    nc.tensor.transpose(acc[2 + n % 2][:, d:d + P], sP[:, n % 2, s:s + P], ident[:])
                for qt in range(2):
                    ins = nc.tensor.transpose((stat, mix[2])[n % 2][0:META, P * qt:P * qt + P], sP[:, n % 2, 144 * qt:144 * qt + META], ident[:])
                ins.then_inc(s_pt, 1)

            def values(n):
                j, h = SUNITS[n]
                g = 2 * (j // 4) + h
                dst = mix[j % 2][DH * h:DH * h + DH]
                if j >= 2 and h == 0:
                    pe.wait_ge(m_lo, 24 + j - 1)
                elif j < 2:
                    pe.wait_ge(s_k, 10)
                pe.wait_ge(s_ptc, n + 1)
                w = slice(DH * g, DH * g + DH)
                nc.tensor.matmul(dst[:, 0:SEQ], sv[:, 0, w], sPT[:, n % 2, 0:SEQ], start=True, stop=False)
                nc.tensor.matmul(dst[:, P:SEQ], sv[:, 1, w], sPT[:, n % 2, SEQ:SEQ + P], start=False, stop=False)
                pe.wait_ge(s_pmc, n + 1)
                nc.tensor.matmul(dst[:, 0:SEQ], sv[0:META, 2, w], sPM[0:META, n % 2, :], start=False, stop=True).then_inc(s_o, 1)

            scores(0)
            for n in range(len(SUNITS) + 1):
                if n + 1 < len(SUNITS):
                    scores(n + 1)
                if n:
                    values(n - 1)
                if n < len(SUNITS):
                    turned(n)
            gemm("swa_out", hh, hl, META, (m_lo, 24))

        def swa_act(act, step, ahead, residual):
            act.wait_ge(s_tr, 1)
            nc.scalar.activation(sv[:, 0:2, :].rearrange("p a n -> p (a n)"), stat[:, :], ACT.Copy).then_inc(s_v, 1)
            nc.scalar.activation(sv[0:META, 2, :], mix[0][0:META, 0:256], ACT.Copy).then_inc(s_v, 1)
            for m in range(KD):
                ahead(BASE["swa_q"] + m)

            def exps(n):
                j, h = SUNITS[n]
                head = 2 * j + h
                act.wait_ge(s_min, n + 1)
                if n >= 2:
                    act.wait_ge(s_pt, n - 1)
                b = 2 * (n % 2)
                for qt, (c, e, q) in enumerate(SQ):
                    nc.scalar.activation(sP[:, n % 2, c:c + e], sS[:, n % 2, c:c + e], ACT.Exp, scale=-1.0, bias=sstat[:, b + qt:b + qt + 1],
                                         accum_out=sstat[:, 8 + b + qt:9 + b + qt]).then_inc(s_exp, 1)
                nc.scalar.activation(sstat[:, 16 + b:18 + b], sstat[:, b:b + 2], ACT.Exp, bias=col("sinks", head)).then_inc(s_es, 1)

            exps(0)
            for n in range(len(SUNITS)):
                if n + 1 < len(SUNITS):
                    exps(n + 1)
                act.wait_ge(s_pt, n + 1)
                if n >= 2:
                    act.wait_ge(s_o, n - 1)
                nc.scalar.activation(sPT[:, n % 2, :], acc[2 + n % 2][:, 0:384], ACT.Copy).then_inc(s_ptc, 1)
                if n % 2 == 0 and n:
                    attn_hi(act, n // 2 - 1, s_o, n)
            attn_hi(act, KD - 1, s_o, len(SUNITS))
            for m in range(KD):
                residual(9, m, BASE["swa_out"] + m)

        def swa_dve(dve, step, ahead, tail):
            def rotated(i, v, w, tab):
                dve.wait_ge(s_perm, i + 1)
                if i:
                    dve.wait_ge(s_k, i)
                step(nc.vector.tensor_tensor(snt[:, 0:w], mix[1 + i % 2][:, 0:w], sinT[:, tab:], ALU.mult))
                step(nc.vector.tensor_tensor(v, v, cosT[:, tab:], ALU.mult))
                nc.vector.tensor_tensor(v, v, snt[:, 0:w], ALU.add).then_inc(s_k, 1)

            nc.vector.tensor_scalar(snk, par[:, COL["sinks"]:COL["sinks"] + 16], -1.0, None, ALU.mult).then_inc(s_nk, 1)
            for m in range(2):
                rotated(m, sk[:, m, :], L, SEQ)
            for m in range(KD):
                b = BASE["swa_q"] + m
                dve.wait_ge(used, b + 1)
                nc.vector.scalar_tensor_tensor(sq_q[:, m, :], bank("swa_q", m)[:, 0:SEQ], -0.125, rx[:, META:], ALU.mult, ALU.mult).then_inc(s_q, 1)
                dve.wait_ge(s_q, m + 1)
                dve.sem_inc(acc_used, 1)
                ahead(b)
                if m:
                    rotated(m + 1, sq_q[:, m - 1, :], SEQ, SEQ + META)
            rotated(KD + 1, sq_q[:, KD - 1, :], SEQ, SEQ + META)
            dve.wait_ge(s_nk, 1)
            dve.wait_ge(s_mask, 3)

            def least(n):
                j, h = SUNITS[n]
                dve.wait_ge(s_s, n + 1)
                if n >= 2:
                    dve.wait_ge(s_es, n - 1)
                b = 2 * (n % 2)
                for qt, (c, e, q) in enumerate(SQ):
                    ins = nc.vector.tensor_tensor_reduce(sS[:, n % 2, c:c + e], acc[n % 2][:, c:c + e], smask[:, c:c + e], 1.0,
                                                         snk[:, 2 * j + h:2 * j + h + 1], ALU.add, ALU.min, sstat[:, b + qt:b + qt + 1])
                ins.then_inc(s_min, 1)

            least(0)
            for n in range(len(SUNITS)):
                b = 2 * (n % 2)
                if n + 1 < len(SUNITS):
                    least(n + 1)
                dve.wait_ge(s_es, n + 1)
                tot = sstat[:, 24:26]
                if n:
                    dve.wait_ge(s_p, n)
                step(nc.vector.tensor_tensor(tot, sstat[:, 8 + b:10 + b], sstat[:, 16 + b:18 + b], ALU.add))
                step(nc.vector.reciprocal(tot, tot))
                for qt, (c, e, q) in enumerate(SQ):
                    ins = nc.vector.tensor_scalar(sP[:, n % 2, c:c + e], sP[:, n % 2, c:c + e], tot[:, qt:qt + 1], None, ALU.mult)
                ins.then_inc(s_p, 1)
                if n % 2 == 1 and n > 1:
                    attn_lo(dve, n // 2 - 1, 3)
                dve.wait_ge(s_pt, n + 1)
                if n >= 2:
                    dve.wait_ge(s_o, n - 1)
                nc.vector.tensor_copy(sPM[0:META, n % 2, :], (stat, mix[2])[n % 2][0:META, 0:SEQ]).then_inc(s_pmc, 1)
            attn_lo(dve, KD - 1, 3)
            for m in range(KD):
                tail(9, m, "swa_out", BASE["swa_out"] + m)

        mixers["pool"][8], mixers["pe"][8], mixers["act"][8], mixers["dve"][8] = swa_pool, swa_pe, swa_act, swa_dve
        block = ctx.enter_context(nc.Block())

        @block.sync
        def _(sp):
            for s in range(RING):
                if s == 2:
                    sp.wait_ge(in_x, 32)
                sp.dma_start(raw[:, s, :], a["w"][s]).then_inc(raw_in[s], 16)
            with sp.Fori(1, HALVES // RING) as i:
                for s in range(RING):
                    sp.wait_ge(w_lo, RING * i - RING + s + 1)
                    sp.dma_start(raw[:, s, :], a["w"][bass.ds(RING * i + s, 1)].rearrange("a p n -> p (a n)")) \
                        .then_inc(raw_in[s], 16)
            for n in range(HALVES // RING * RING, HALVES):
                sp.wait_ge(w_lo, n - RING + 1)
                sp.dma_start(raw[:, n % RING, :], a["w"][n]).then_inc(raw_in[n % RING], 16)
            for k in range(KD):
                sp.wait_ge(x_new[k % 2], updated(upto, k))
                sp.dma_start(out[k], x[:, k, META:]).then_inc(out_ok, 16)
            sp.wait_ge(out_ok, 16 * KD)

        @block.gpsimd
        def _(pool):
            step = Chain(pool, pool_step)
            pool.memset(ones[:], 1.0 / D).then_inc(const_ok, 1)
            pool.memset(ones4[:], 4.0 / D).then_inc(const_ok, 1)
            for n, v in enumerate((1e-6, 4e-6, 1e-5, HALF_PI, 64e-6)):
                pool.memset(eps[:, n:n + 1], v).then_inc(const_ok, 1)

            tables_pool(pool, step)

            def norm_sum(v, c, between=()):
                between = dict(between)
                pool.wait_ge(sq_new, 8 * v + 2)
                if v:
                    pool.wait_ge(mean_ok, v)
                step(pool.tensor_tensor(sumsq[:, c:], sq[:, 0, c:], sq[:, 1, c:], ALU.add))
                for k in range(2, KD):
                    if k in between:
                        between[k]()
                    pool.wait_ge(sq_new, 8 * v + k + 1)
                    ins = pool.tensor_tensor(sumsq[:, c:], sumsq[:, c:], sq[:, k, c:], ALU.add)
                    if k < KD - 1:
                        step(ins)
                ins.then_inc(sum_ok, 1)

            def post_update(u):
                norm_sum(norm_of(u, True), c0(u))

                def add(k):
                    pool.wait_ge(t_new, 8 * (u - 5) + k + 1)
                    pool.tensor_tensor(x[:, k, c0(u):], x[:, k, c0(u):], y[:, k, c0(u):], ALU.add).then_inc(x_new[0], 1)

                add(0)
                add(2)
                if u < upto and u != 7:
                    norm_sum(norm_of(u), c0(u), ((2, lambda: add(4)), (3, lambda: add(6))))
                else:
                    add(4)
                    add(6)
                    if u < upto:
                        norm_sum(norm_of(u), c0(u))

            for u in range(0, upto + 1):
                if u in mixers.get("pool", {}):
                    mixers["pool"][u](pool, step)
                if u >= 5:
                    post_update(u)
                elif u < upto:
                    norm_sum(norm_of(u), c0(u))

        @block.tensor
        def _(pe):
            pe.wait_ge(const_ok, 7)

            def half(h, q, name, t, part, hi, lo, c, kt, wait):
                pe.wait_ge(w_lo, h.n + 1)
                if part == 0 and q is not None:
                    pe.wait_ge(acc_used, q - 3)
                ks = range(part * KD, min(kt, part * KD + KD))
                for k in ks:
                    if wait:
                        pe.wait_ge(wait[0], wait[1] + k + 1)
                    w = slice((k % KD) * P, (k % KD + 1) * P)
                    for w_part, v_part in ((wh, hi), (wh, lo), (wl, hi)):
                        ins = nc.tensor.matmul(bank(name, t)[:, 0:L - c], w_part[:, h.slot, w], v_part[:, k, c:],
                                               start=(k == 0 and w_part is wh and v_part is hi),
                                               stop=(k == kt - 1 and w_part is wl))
                ins.then_inc(used, 1)

            def gemm(name, hi, lo, c, wait, kt=KD, first=0, last=None):
                parts = -(-kt // KD)
                last = SIZE[name] // parts if last is None else last

                def tiles(i, ts):
                    for t in ts:
                        for part in range(parts):
                            b = BASE[name] + t * parts + part
                            q = TILE[name] + t + 8 * i
                            if isinstance(q, int) and q < 4:
                                q = None
                            half(Half(b, i * (2 * parts)), q, name, t, part, hi, lo, c, kt,
                                 wait if t == 0 else None)

                peel = min(4, last) if first else 0
                tiles(0, range(first, peel))
                first = max(first, peel)
                rounds = (last - first) // 8
                if rounds > 1:
                    with pe.Fori(0, rounds) as i:
                        tiles(i, range(first, first + 8))
                    first += 8 * rounds
                tiles(0, range(first, last))

            def opening(pair, hi, lo, c, wait):
                for name, t in pair:
                    pe.wait_ge(w_lo, BASE[name] + t + 1)
                    if TILE[name] + t >= 4:
                        pe.wait_ge(acc_used, TILE[name] + t - 3)
                for k in range(KD):
                    pe.wait_ge(wait[0], wait[1] + k + 1)
                    w = slice(k * P, (k + 1) * P)
                    for name, t in pair:
                        slot = (BASE[name] + t) % RING
                        for w_part, v_part in ((wh, hi), (wh, lo), (wl, hi)):
                            ins = nc.tensor.matmul(bank(name, t)[:, 0:L - c], w_part[:, slot, w], v_part[:, k, c:],
                                                   start=(k == 0 and w_part is wh and v_part is hi),
                                                   stop=(k == KD - 1 and w_part is wl))
                        if k == KD - 1:
                            ins.then_inc(used, 1)

            def mean(v, c):
                pe.wait_ge(sum_ok, v + 1)
                if v:
                    pe.wait_ge(root_ok, v)
                nc.tensor.matmul(stat[:, 0:L - c], (ones4 if halved(v) else ones)[:], sumsq[:, c:], start=True,
                                 stop=True).then_inc(mean_ok, 1)

            def begin(u, *pair):
                opening(pair, xh, xl, cg(u), (x_lo, 8 * u))
                mean(norm_of(u), c0(u))

            for u in range(0, upto):
                f = FFN_AFTER.get(u)
                if u == 7:
                    kv_pe(pe, gemm, opening, mean)
                    gemm("ffn4_a", xh, xl, cg(u), (x_lo, 8 * u))
                elif f is not None:
                    begin(u, (f"ffn{f}_a", 0), (f"ffn{f}_a", 1))
                    gemm(f"ffn{f}_a", xh, xl, cg(u), None, first=2)
                else:
                    mixers["pe"][u](pe, gemm, begin, opening)
                if f is not None:
                    gemm(f"ffn{f}_b", hh, hl, cg(u), (f_lo, KF * f), KF)
                if u + 1 >= 5:
                    mean(norm_of(u + 1, True), c0(u + 1))

        @block.scalar
        def _(act):
            step = Chain(act, act_step)

            def split(h):
                act.wait_ge(raw_in[h.slot], 16 * h.round + 16)
                if not (isinstance(h.n, int) and h.n < RING):
                    act.wait_ge(used, h.n - RING + 1)
                nc.scalar.activation(wh[:, h.slot, :], raw[:, h.slot, :], ACT.Copy).then_inc(w_hi, 1)

            def ahead(b, i=0):
                if not isinstance(i, int) or b + RING * i + RING < HALVES:
                    split(Half(b + RING, i))

            def x_parts(u, k):
                c = c0(u)
                if u:
                    act.wait_ge(x_new[k % 2], updated(u, k))
                else:
                    act.wait_ge(in_x, 32)
                if u < upto:
                    nc.scalar.activation(xh[:, k, c:], x[:, k, c:], ACT.Copy, scale=col(NEXT_GAIN[u], k)).then_inc(x_hi, 1)
                    squares(x, norm_of(u), k, c)

            def squares(src, v, k, c):
                if v:
                    act.wait_ge(sum_ok, v)
                nc.scalar.activation(sq[:, k, c:], src[:, k, c:], ACT.Square).then_inc(sq_new, 1)

            def ffn(f, u):
                base = BASE[f"ffn{f}_a"]
                c = cg(u)

                def high_h(i, t):
                    act.wait_ge(f_h, KF * f + t + 1 + 2 * i)
                    act.wait_ge(const_ok, 7)
                    nc.scalar.activation(hh[:, bass.ds(2 * i + t, 1), c:], th[:, t:t + 1, c:], ACT.Copy).then_inc(f_hi, 1)

                def two(i, first):
                    for t in range(2):
                        ahead(base + 2 * t, i)
                        act.wait_ge(f_g, KF * f + t + 2 * i + 1)
                        nc.scalar.activation(ts[:, t, c:], tg[:, t, c:], ACT.Silu).then_inc(f_s, 1)
                        if t:
                            high_h(i, 0)
                        elif not first:
                            high_h(i - 1, 1)
                        ahead(base + 2 * t + 1, i)

                two(0, True)
                with act.Fori(1, KF // 2) as i:
                    two(i, False)
                high_h(KF // 2 - 1, 1)
                if f == 0:
                    tables_act(act)
                base = BASE[f"ffn{f}_b"]
                for m in range(KD):
                    for part in range(KF_PARTS - 1):
                        ahead(base + m * KF_PARTS + part)
                    residual(u + 1, m, base + m * KF_PARTS + KF_PARTS - 1)

            def rooted(v, c):
                act.wait_ge(mean_ok, v + 1)
                if v:
                    act.wait_ge(rms_ok, v)
                nc.scalar.activation(root[:, c:], stat[:, 0:L - c], ACT.Sqrt,
                                     bias=eps[:, 1:2] if halved(v) else eps[:, 0:1]).then_inc(root_ok, 1)

            def residual(u, m, b):
                if m < KD - 1:
                    ahead(b)
                if u < 5:
                    x_parts(u, m)
                else:
                    act.wait_ge(y_new, 8 * (u - 5) + m + 1)
                    squares(y, norm_of(u, True), m, c0(u))
                if m == KD - 1:
                    if u >= 5:
                        rooted(norm_of(u, True), c0(u))
                    if u == 7 and u < upto:
                        for k in range(KD):
                            act.wait_ge(x_new[k % 2], updated(u, k))
                            kv_act(act, k)
                    if u >= 5:
                        for k in range(KD):
                            x_parts(u, k)
                    ahead(b)

            act.dma_start(par[:], a["par"]).then_inc(in_par, 16)
            for h in range(2):
                act.dma_start(x[:, 4 * h:4 * h + 4, :], a["x"][:, 4 * h:4 * h + 4, :]).then_inc(in_x, 16)
            act.wait_ge(const_ok, 7)
            split(Half(0))
            split(Half(1))
            act.wait_ge(in_par, 16)
            for k in range(KD):
                x_parts(0, k)
            split(Half(2))
            split(Half(3))
            for u in range(0, upto):
                rooted(norm_of(u), c0(u))
                if u == 7:
                    for m in range(4):
                        ahead(BASE["kv"] + m)
                f = FFN_AFTER.get(u)
                if f is not None:
                    ffn(f, u)
                else:
                    mixers["act"][u](act, step, ahead, residual)

        @block.vector
        def _(dve):
            step = Chain(dve, dve_step)

            def split(h):
                dve.wait_ge(w_hi, h.n + 1)
                nc.vector.tensor_tensor(wl[:, h.slot, :], raw[:, h.slot, :], wh[:, h.slot, :].bitcast(F32),
                                        ALU.subtract).then_inc(w_lo, 1)

            def ahead(b, i=0):
                if not isinstance(i, int) or b + RING * i + RING < HALVES:
                    split(Half(b + RING, i))

            def low_x(u, k):
                if u < upto:
                    c = c0(u)
                    dve.wait_ge(x_hi, 8 * u + k + 1)
                    nc.vector.scalar_tensor_tensor(xl[:, k, c:], x[:, k, c:], col(NEXT_GAIN[u], k),
                                                   xh[:, k, c:].bitcast(F32), ALU.mult, ALU.subtract).then_inc(x_lo, 1)

            def rms(v, c, dst):
                dve.wait_ge(root_ok, v + 1)
                nc.vector.reciprocal(dst[:, c:], root[:, c:]).then_inc(rms_ok, 1)
                dve.wait_ge(rms_ok, v + 1)

            def post_norm(u):
                c = c0(u)
                rms(norm_of(u, True), c, ry)

                def scaled(k):
                    nc.vector.scalar_tensor_tensor(y[:, k, c:], y[:, k, c:], col(POST_GAIN[u], k), ry[:, c:],
                                                   ALU.mult, ALU.mult).then_inc(t_new, 1)

                def add(k):
                    if k % 2:
                        dve.wait_ge(t_new, 8 * (u - 5) + k + 1)
                        nc.vector.tensor_tensor(x[:, k, c:], x[:, k, c:], y[:, k, c:], ALU.add).then_inc(x_new[1], 1)

                for k in range(4):
                    scaled(k)
                    if k:
                        add(k - 1)
                add(3)
                for k in range(KD):
                    if u == 7 and u < upto:
                        kv_low(dve, k)
                    else:
                        low_x(u, k)
                    if k + 4 < KD:
                        scaled(k + 4)
                        add(k + 4)
                if u == 7 and u < upto:
                    for k in range(KD):
                        low_x(u, k)

            def ffn(f, u):
                name = f"ffn{f}_a"
                c = cg(u)

                def low_h(i, t):
                    dve.wait_ge(f_hi, KF * f + t + 1 + 2 * i)
                    nc.vector.tensor_tensor(hl[:, bass.ds(2 * i + t, 1), c:], th[:, t:t + 1, c:],
                                            hh[:, bass.ds(2 * i + t, 1), c:].bitcast(F32), ALU.subtract).then_inc(f_lo, 1)

                def two(i, first):
                    for t in range(2):
                        n = KF * f + t + 2 * i + 1
                        b = BASE[name] + 2 * t
                        dve.wait_ge(used, Half(b, i).n + 1)
                        nc.vector.tensor_tensor(tg[:, t, c:], bank(name, 2 * t)[:, 0:L - c], rx[:, c:], ALU.mult).then_inc(f_g, 1)
                        dve.wait_ge(f_g, n)
                        dve.sem_inc(acc_used, 1)
                        ahead(b, i)
                        if t:
                            low_h(i, 0)
                        elif not first:
                            low_h(i - 1, 1)
                        dve.wait_ge(used, Half(b + 1, i).n + 1)
                        nc.vector.tensor_tensor(tu[:, t, c:], bank(name, 2 * t + 1)[:, 0:L - c], rx[:, c:],
                                                ALU.mult).then_inc(acc_used, 1)
                        dve.wait_ge(acc_used, TILE[name] + 4 * i + 2 * t + 2)
                        dve.wait_ge(f_s, n)
                        nc.vector.tensor_tensor(th[:, t, c:], tu[:, t, c:], ts[:, t, c:], ALU.mult).then_inc(f_h, 1)
                        ahead(b + 1, i)

                two(0, True)
                with dve.Fori(1, KF // 2) as i:
                    two(i, False)
                low_h(KF // 2 - 1, 1)
                if f == 0:
                    tables_dve(dve, step)
                name = f"ffn{f}_b"
                for m in range(KD):
                    for part in range(KF_PARTS):
                        b = BASE[name] + m * KF_PARTS + part
                        if part == KF_PARTS - 1:
                            tail(u + 1, m, name, b)
                        else:
                            ahead(b)

            def tail(u, m, name, b):
                dve.wait_ge(used, b + 1)
                c = c0(u)
                if u < 5:
                    nc.vector.tensor_tensor(x[:, m, META:], x[:, m, META:], bank(name, m)[:, 0:SEQ], ALU.add).then_inc(x_new[m % 2], 1)
                    dve.wait_ge(x_new[m % 2], updated(u, m))
                else:
                    nc.vector.tensor_copy(y[:, m, c:], bank(name, m)[:, 0:L - c]).then_inc(y_new, 1)
                    dve.wait_ge(y_new, 8 * (u - 5) + m + 1)
                dve.sem_inc(acc_used, 1)
                if m < KD - 1:
                    ahead(b)
                if u < 5:
                    low_x(u, m)
                if m == KD - 1:
                    if u >= 5:
                        post_norm(u)
                    ahead(b)

            split(Half(0))
            split(Half(1))
            dve.wait_ge(in_par, 16)
            for k in range(KD):
                low_x(0, k)
            split(Half(2))
            split(Half(3))
            for u in range(0, upto):
                rms(norm_of(u), c0(u), rx)
                if u == 7:
                    kv_dve(dve, ahead)
                f = FFN_AFTER.get(u)
                if f is not None:
                    ffn(f, u)
                else:
                    mixers["dve"][u](dve, step, ahead, tail)


def _tiles(w):
    import numpy as np
    w = np.asarray(w)
    n = w.shape[1]
    pad = -n % P
    if pad:
        w = np.concatenate([w, np.zeros((w.shape[0], pad), w.dtype)], axis=1)
    return np.ascontiguousarray(w.reshape(-1, P, (n + pad) // P, P).transpose(2, 1, 0, 3)).reshape((n + pad) // P, P, -1)


def _pairs(w):
    import numpy as np
    n = w.shape[1] // 2
    return np.stack([_tiles(w[:, :n]), _tiles(w[:, n:])], axis=1).reshape(-1, P, KD * P)


def _down(w):
    import numpy as np
    w = np.asarray(w)
    w = np.concatenate([w, np.zeros((KF_PARTS * D - FF, D), w.dtype)])
    return w.reshape(KF_PARTS, KD, P, KD, P).transpose(3, 0, 2, 1, 4).reshape(-1, P, KD * P)


def _cols(v):
    import numpy as np
    return np.asarray(v).reshape(-1, P).T


def kernel(**t):
    import numpy as np
    import concourse.bacc as bacc
    from concourse.bass_utils import run_bass_kernel_spmd as run

    t = {k: np.asarray(v) for k, v in t.items()}
    half = ROPE // 2
    heads = [g * 4 + r for t2 in range(2) for r in range(4) for g in (2 * t2, 2 * t2 + 1)]
    hcols = np.concatenate([np.arange(h * DH, h * DH + DH) for h in heads])
    nsa, gla = t["nsa_w_in"][0], t["gla_w_in_2"][0]
    w_ffn_in, w_ffn_out = t["w_ffn_in_2"], t["w_ffn_out_2"]
    by_name = {
        "conv_in": _pairs(t["conv_w_in"][0]), "conv_out": _tiles(t["conv_w_out"][0]),
        "nsa_kv": _tiles(nsa[:, 1024:2560]), "nsa_gate": _tiles(nsa[:, 2560:]), "nsa_q": _tiles(nsa[:, hcols]),
        "nsa_out": _tiles(t["nsa_w_out"][0][hcols]),
        "gla_lr": _tiles(gla[:, 3072:]), "gla_k": _tiles(gla[:, 512:1024]), "gla_q": _tiles(gla[:, :512]),
        "gla_v": _tiles(gla[:, 1024:2048]), "gla_r": _tiles(gla[:, 2048:3072]), "gla_out": _tiles(t["gla_w_out_2"][0]),
        "kv": _tiles(t["w_kv_2"]), "swa_q": _tiles(t["swa_w_q_2"][0][:, hcols]), "swa_out": _tiles(t["swa_w_out_2"][0][hcols]),
    }
    for f in range(2):
        by_name[f"ffn{f}_a"], by_name[f"ffn{f}_b"] = _pairs(t["ffn_w_in"][f]), _down(t["ffn_w_out"][f])
    for f in range(4):
        by_name[f"ffn{2 + f}_a"], by_name[f"ffn{2 + f}_b"] = _pairs(w_ffn_in[f // 2, f % 2]), _down(w_ffn_out[f // 2, f % 2])
    stream = np.concatenate([by_name[name] for name, _ in STAGES])
    assert stream.shape[0] == HALVES

    f32 = np.float32
    two = lambda v: np.concatenate([v, v], axis=-1)[..., None]
    conv_b = t["conv_b_in"][0]
    rope = np.zeros((P, 2), f32)
    for h in range(2):
        for d in range(ROPE):
            rope[h * DH + d] = (f32(THETA) ** (-f32(d % half) / f32(half)), -1.0 if d < half else 1.0)
    pieces = {
        "mix0": _cols(t["norm_mix"][0]), "mix1": _cols(t["norm_mix"][1]),
        "ffn0": _cols(t["norm_ffn"][0]), "ffn1": _cols(t["norm_ffn"][1]),
        "conv_ba": _cols(conv_b[:D]), "conv_bg": _cols(conv_b[D:]),
        "conv_w": t["conv_w_dw"][0].reshape(CONV, KD, P).transpose(2, 1, 0).reshape(P, -1),
        "conv_b": _cols(t["conv_b_dw"][0]), "ln_g": _cols(t["conv_ln_g"][0]), "ln_b": _cols(t["conv_ln_b"][0]),
        "q_gain": two(t["nsa_q_gain"][0]), "k_gain": np.tile(t["nsa_k_gain"][0].T, (2, 1)),
        "cmp_b1": np.tile(t["nsa_cmp_b1"][0].T, (2, 1)),
        "cmp_pos": np.tile(t["nsa_cmp_pos"][0].transpose(2, 0, 1).reshape(DH, 64), (2, 1)),
        "g2": _cols(t["norm_gains_2"]), "kv_norm": _cols(t["kv_norm_2"]), "gate_b": _cols(t["gla_b_gate_2"][0]),
        "gla_norm": _cols(t["gla_norm_2"][0]), "sinks": np.broadcast_to(t["swa_sinks_2"][0][heads], (P, 16)),
        "inv_freq": rope[:, 0:1], "rope_sign": rope[:, 1:2],
    }
    arrays = {
        "w": stream,
        "par": np.ascontiguousarray(np.concatenate([pieces[name].reshape(P, n) for name, n in PARAMS], axis=1)),
        "x": np.ascontiguousarray(np.concatenate([t["meta_tokens_2"], t["x"][0]]).T.reshape(KD, P, L).transpose(1, 0, 2)),
        "positions": t["positions"],
        "cmp_w1": np.ascontiguousarray(np.tile(t["nsa_cmp_w1"][0].reshape(2, 32, DH, DH).transpose(2, 0, 1, 3), (2, 1, 1, 1))).reshape(P, -1),
        "cmp_w2": np.ascontiguousarray(t["nsa_cmp_w2"][0].transpose(1, 0, 2)).reshape(DH, -1),
        "w_gate": t["gla_w_gate_2"][0], "gate_row": t["gla_b_gate_2"],
    }
    nc = bacc.Bacc("TRN2", target_bir_lowering=False, num_devices=1)
    drams = {k: nc.dram_tensor("in_" + k, v.shape, mybir.dt.from_np(v.dtype), kind="ExternalInput").ap() for k, v in arrays.items()}
    out = nc.dram_tensor("out", (KD, P, SEQ), F32, kind="ExternalOutput").ap()
    build(nc, drams, out, UPDATES)
    r = run(nc, [{"in_" + k: v for k, v in arrays.items()}], core_ids=[0])
    return np.ascontiguousarray(r.results[0]["out"].reshape(D, SEQ).T)[None]
```

```python
from contextlib import ExitStack

import numpy as np_

import concourse.bass as bass
from concourse import mybir

ALU = mybir.AluOpType
ACT = mybir.ActivationFunctionType
AX = mybir.AxisListType
F32 = mybir.dt.float32
F32R = mybir.dt.float32r
I32 = mybir.dt.int32

P = 128
D = 1024
KD = D // P
SEQ = 256
META = 16
L = SEQ + META
FF = 2816
KF = FF // P
KF_PARTS = -(-KF // KD)
RING = 4
CONV = 31
PE_TAPS = 16
BIG = 1e30
ROPE = 16
THETA = 500000.0
DH = 64
TWO_PI = (6.28125, 0.0019350051879882812, 3.019915981956752e-07)
PI_BELOW = 3.1415925
HALF_PI = 1.5707963267948966
NCMP = (SEQ - 32) // 16 + 1

FFN_A, FFN_B = 2 * KF, KD * KF_PARTS
STAGES = [("conv_in", 16), ("conv_out", 8), ("ffn0_a", FFN_A), ("ffn0_b", FFN_B),
          ("nsa_kv", 12), ("nsa_gate", 1), ("nsa_q", 8), ("nsa_out", 8), ("ffn1_a", FFN_A), ("ffn1_b", FFN_B),
          ("ffn2_a", FFN_A), ("ffn2_b", FFN_B),
          ("gla_lr", 1), ("gla_k", 4), ("gla_q", 4), ("gla_v", 8), ("gla_r", 8), ("gla_out", 8),
          ("ffn3_a", FFN_A), ("ffn3_b", FFN_B), ("kv", 4),
          ("ffn4_a", FFN_A), ("ffn4_b", FFN_B), ("swa_q", 8), ("swa_out", 8),
          ("ffn5_a", FFN_A), ("ffn5_b", FFN_B)]
BASE, TILE, SIZE = {}, {}, {}
HALVES = TILES = 0
for _name, _n in STAGES:
    BASE[_name], TILE[_name], SIZE[_name] = HALVES, TILES, _n
    HALVES += _n
    TILES += _n // KF_PARTS if _name.endswith("_b") else _n

PARAMS = [("mix0", 8), ("ffn0", 8), ("mix1", 8), ("ffn1", 8),
          ("conv_ba", 8), ("conv_bg", 8), ("conv_w", 8 * CONV), ("conv_b", 8), ("ln_g", 8), ("ln_b", 8),
          ("q_gain", 1), ("k_gain", 3), ("cmp_b1", 2), ("cmp_pos", 64),
          ("g2", 96), ("kv_norm", 8), ("gate_b", 4), ("gla_norm", 2), ("sinks", 16),
          ("inv_freq", 1), ("rope_sign", 1)]
COL = {}
_c = 0
for _name, _n in PARAMS:
    COL[_name] = _c
    _c += _n
NPAR = _c

NEXT_GAIN = [COL["mix0"], COL["ffn0"], COL["mix1"], COL["ffn1"]] + \
            [COL["g2"] + 8 * g for g in (0, 2, 4)] + [COL["g2"] + 48 + 8 * g for g in (0, 2, 4)]
POST_GAIN = {u: COL["g2"] + 48 * (n // 3) + 8 * (1 + 2 * (n % 3)) for n, u in enumerate(range(5, 11))}


def last(name):
    return BASE[name] + SIZE[name]


class Half:

    def __init__(self, b, i=0):
        self.slot = b % RING
        self.round = b // RING + i
        self.n = b + RING * i


class Chain:

    def __init__(self, eng, sem):
        self.eng, self.sem, self.n, self.i, self.per, self.at = eng, sem, 0, None, 0, 0

    def __call__(self, ins):
        self.n += 1
        ins.then_inc(self.sem, 1)
        self.eng.wait_ge(self.sem, self.n if self.i is None else self.n + self.i * self.per)

    def enter(self, i, per):
        self.i, self.per, self.at = (None, 0, self.n) if isinstance(i, int) else (i, per, self.n)
        return self

    def leave(self, rounds):
        if self.i is not None:
            assert self.n - self.at == self.per, (self.n - self.at, self.per)
            self.n = self.at + self.per * rounds
            self.i = None

SCRATCH = 12360
UPDATES = 10
FFN_AFTER = {1: 0, 3: 1, 4: 2, 6: 3, 7: 4, 9: 5}


def build(nc, a, out, upto):
    with ExitStack() as ctx:
        def sb(name, shape, dt=F32):
            return ctx.enter_context(nc.sbuf_tensor(name, shape, dt))

        def sem(name):
            return ctx.enter_context(nc.semaphore(name))

        x = sb("x", [P, KD, L])
        xh, xl = sb("xh", [P, KD, L], F32R), sb("xl", [P, KD, L], F32R)
        sq = sb("sq", [P, KD, L])
        y = sb("y", [P, KD, L])
        sumsq, root, rx, ry = sb("sumsq", [P, L]), sb("root", [P, L]), sb("rx", [P, L]), sb("ry", [P, L])
        hh, hl = sb("hh", [P, KF, L], F32R), sb("hl", [P, KF, L], F32R)
        raw = sb("raw", [P, RING, KD * P])
        wh, wl = sb("wh", [P, RING, KD * P], F32R), sb("wl", [P, RING, KD * P], F32R)
        par = sb("par", [P, NPAR])
        tg, ts, tu, th = (sb(n, [P, 2, L]) for n in ("tg", "ts", "tu", "th"))
        ones, ones4 = sb("ones", [P, P]), sb("ones4", [P, P])
        eps = sb("eps", [P, 5])
        scr = sb("scr", [P, SCRATCH])

        acc = [ctx.enter_context(nc.psum_tensor(f"acc{i}", [P, 512], F32)) for i in range(4)]
        stat = ctx.enter_context(nc.psum_tensor("stat", [P, 512], F32))
        mix = [ctx.enter_context(nc.psum_tensor(f"mix{i}", [P, 512], F32)) for i in range(3)]

        const_ok = sem("const_ok")
        in_x, in_par = sem("in_x"), sem("in_par")
        raw_in = [sem(f"raw_in{i}") for i in range(RING)]
        w_hi, w_lo, used, acc_used = sem("w_hi"), sem("w_lo"), sem("used"), sem("acc_used")
        x_new = [sem("x_even"), sem("x_odd")]
        x_hi, x_lo = sem("x_hi"), sem("x_lo")
        sq_new, sum_ok, mean_ok, root_ok, rms_ok = (sem(n) for n in ("sq_new", "sum_ok", "mean_ok", "root_ok", "rms_ok"))
        y_new, t_new = sem("y_new"), sem("t_new")
        f_g, f_s, f_h, f_hi, f_lo = (sem(n) for n in ("f_g", "f_s", "f_h", "f_hi", "f_lo"))
        m_hi, m_lo = sem("m_hi"), sem("m_lo")
        out_ok = sem("out_ok")
        dve_step, act_step, pool_step = sem("dve_step"), sem("act_step"), sem("pool_step")

        def col(name, k=0):
            c = (COL[name] if isinstance(name, str) else name) + k
            return par[:, c:c + 1]

        def c0(u):
            return 0 if 4 <= u <= 7 else META

        def cg(u):
            return max(c0(u), c0(u + 1))

        def norm_of(u, post=False):
            return u if u < 5 else 5 + 2 * (u - 5) + (not post)

        def bank(name, t):
            if name == "gla_r":
                return mix[t % 2]
            return mix[2] if name == "swa_q" and t >= 3 else acc[(TILE[name] + t) % 4]

        def updated(u, k):
            return 4 * (u - 1) + k // 2 + 1

        def halved(v):
            return v in [norm_of(u, True) for u in (5, 7, 8, 10)]

        mixers = {}
        cu = scr[:, 0:KD * (SEQ + CONV - 1)].rearrange("p (k t) -> p k t", k=KD)
        _o = KD * (SEQ + CONV - 1)
        cv = scr[:, _o:_o + KD * SEQ].rearrange("p (k t) -> p k t", k=KD)
        _o += KD * SEQ
        cw = scr[:, _o:_o + 4 * SEQ].rearrange("p (b k t) -> p b k t", b=2, k=2)
        _o = 8200
        cdiag = scr[:, _o:_o + 2 * PE_TAPS * P].rearrange("p (b n c) -> p b n c", b=2, n=PE_TAPS)
        c_u, c_diag, c_pe = sem("c_u"), sem("c_diag"), sem("c_pe")
        c_g, c_s, c_v, c_mu, c_d, c_sq, c_var, c_root, c_z, c_w, c_pad, c_tap = (
            sem(n) for n in ("c_g", "c_s", "c_v", "c_mu", "c_d", "c_sq", "c_var", "c_root", "c_z", "c_w", "c_pad", "c_tap"))

        def conv_pool(pool, step):
            pool.memset(cu[:, :, 0:CONV - 1], 0.0).then_inc(c_pad, 1)

        def conv_pe(pe, gemm, begin, opening):
            begin(0, ("conv_in", 0), ("conv_in", 1))
            for j in range(KD + 2):
                if 0 < j < KD:
                    gemm("conv_in", xh, xl, META, None, first=2 * j, last=2 * j + 2)
                if 0 < j <= KD:
                    pe.wait_ge(c_u, j)
                    pe.wait_ge(c_diag, j)
                    if j >= 3:
                        pe.wait_ge(c_v, j - 2)
                    for n in range(PE_TAPS):
                        s = CONV - PE_TAPS + n
                        ins = nc.tensor.matmul(mix[1 + j % 2][:, 0:SEQ], cdiag[:, j % 2, n, :], cu[:, j - 1, s:s + SEQ],
                                               start=(n == 0), stop=(n == PE_TAPS - 1))
                    ins.then_inc(c_pe, 1)
                if j >= 2:
                    pe.wait_ge(c_v, j - 1)
                    ins = nc.tensor.matmul(mix[0][:, 0:SEQ], ones[:], cv[:, j - 2, :], start=(j == 2), stop=(j == KD + 1))
            ins.then_inc(c_mu, 1)
            for j in range(KD):
                pe.wait_ge(c_sq, j + 1)
                ins = nc.tensor.matmul(mix[1][:, 0:SEQ], ones[:], sq[:, j, META:], start=(j == 0), stop=(j == KD - 1))
            ins.then_inc(c_var, 1)
            opening((("conv_out", 0), ("conv_out", 1)), hh, hl, META, (m_lo, 0))
            gemm("conv_out", hh, hl, META, None, first=2)

        def conv_act(act, step, ahead, residual):
            def diagonals(j):
                if j >= 2:
                    act.wait_ge(c_pe, j - 1)
                for n in range(PE_TAPS):
                    ins = nc.scalar.activation(cdiag[:, (j + 1) % 2, n, :], ident[:], ACT.Copy,
                                               scale=col("conv_w", CONV * j + CONV - PE_TAPS + n))
                ins.then_inc(c_diag, 1)

            act.wait_ge(shape_ok, 1)
            diagonals(0)
            for j in range(KD):
                b = BASE["conv_in"] + 2 * j
                ahead(b)
                act.wait_ge(c_g, j + 1)
                if j >= 2:
                    act.wait_ge(c_u, j - 1)
                nc.scalar.activation(ts[:, j % 2, META:], tg[:, j % 2, META:], ACT.Sigmoid, bias=col("conv_bg", j)).then_inc(c_s, 1)
                ahead(b + 1)
                if j + 1 < KD:
                    diagonals(j + 1)
            act.wait_ge(sum_ok, 1)
            for j in range(KD):
                act.wait_ge(c_d, j + 1)
                nc.scalar.activation(sq[:, j, META:], cv[:, j, :], ACT.Square).then_inc(c_sq, 1)
            act.wait_ge(c_var, 1)
            act.wait_ge(rms_ok, 1)
            nc.scalar.activation(root[:, META:], mix[1][:, 0:SEQ], ACT.Sqrt, bias=eps[:, 2:3]).then_inc(c_root, 1)
            for j in range(KD):
                act.wait_ge(c_z, j + 1)
                nc.scalar.activation(cv[:, j, :], cv[:, j, :], ACT.Silu, scale=col("ln_g", j), bias=col("ln_b", j)).then_inc(c_w, 1)
                act.wait_ge(c_w, j + 1)
                nc.scalar.activation(hh[:, j, META:], cv[:, j, :], ACT.Copy).then_inc(m_hi, 1)
            for m in range(KD):
                residual(1, m, BASE["conv_out"] + m)

        def conv_dve(dve, step, ahead, tail):
            taps = 0

            def low(j):
                dve.wait_ge(m_hi, j + 1)
                nc.vector.tensor_tensor(hl[:, j, META:], cv[:, j, :], hh[:, j, META:].bitcast(F32), ALU.subtract).then_inc(m_lo, 1)

            def summed(j):
                dve.wait_ge(c_tap, (j + 1) * (CONV - PE_TAPS))
                dve.wait_ge(c_pe, j + 1)
                step(nc.vector.tensor_tensor(cv[:, j, :], cw[:, j % 2, 0, :], mix[1 + (j + 1) % 2][:, 0:SEQ], ALU.add))
                nc.vector.tensor_tensor(cv[:, j, :], cv[:, j, :], cw[:, j % 2, 1, :], ALU.add).then_inc(c_v, 1)
                dve.wait_ge(c_v, j + 1)

            for j in range(KD):
                b = BASE["conv_in"] + 2 * j
                dve.wait_ge(used, b + 1)
                step(nc.vector.tensor_tensor(tu[:, j % 2, META:], bank("conv_in", 2 * j)[:, 0:SEQ], rx[:, META:], ALU.mult))
                ahead(b)
                dve.wait_ge(used, b + 2)
                nc.vector.tensor_tensor(tg[:, j % 2, META:], bank("conv_in", 2 * j + 1)[:, 0:SEQ], rx[:, META:], ALU.mult).then_inc(c_g, 1)
                dve.wait_ge(c_g, j + 1)
                dve.sem_inc(acc_used, 2)
                ahead(b + 1)
                dve.wait_ge(c_s, j + 1)
                dve.wait_ge(c_pad, 1)
                nc.vector.scalar_tensor_tensor(cu[:, j, CONV - 1:], tu[:, j % 2, META:], col("conv_ba", j),
                                               ts[:, j % 2, META:], ALU.add, ALU.mult).then_inc(c_u, 1)
                dve.wait_ge(c_u, j + 1)
                for n in range(CONV - PE_TAPS):
                    if n >= 2:
                        dve.wait_ge(c_tap, taps - 1)
                    w = col("conv_w", CONV * j + n)
                    if n == 0:
                        ins = nc.vector.tensor_scalar(cw[:, j % 2, 0, :], cu[:, j, 0:SEQ], w, col("conv_b", j), ALU.mult, ALU.add)
                    elif n == 1:
                        ins = nc.vector.tensor_scalar(cw[:, j % 2, 1, :], cu[:, j, 1:1 + SEQ], w, None, ALU.mult)
                    else:
                        ins = nc.vector.scalar_tensor_tensor(cw[:, j % 2, n % 2, :], cu[:, j, n:n + SEQ], w, cw[:, j % 2, n % 2, :], ALU.mult, ALU.add)
                    ins.then_inc(c_tap, 1)
                    taps += 1
                if j:
                    summed(j - 1)
            summed(KD - 1)
            dve.wait_ge(c_mu, 1)
            for j in range(KD):
                nc.vector.tensor_tensor(cv[:, j, :], cv[:, j, :], mix[0][:, 0:SEQ], ALU.subtract).then_inc(c_d, 1)
            dve.wait_ge(c_root, 1)
            step(nc.vector.reciprocal(ry[:, META:], root[:, META:]))
            for j in range(KD):
                dve.wait_ge(c_sq, j + 1)
                nc.vector.tensor_tensor(cv[:, j, :], cv[:, j, :], ry[:, META:], ALU.mult).then_inc(c_z, 1)
                if j:
                    low(j - 1)
            low(KD - 1)
            for m in range(KD):
                tail(1, m, "conv_out", BASE["conv_out"] + m)

        mixers.setdefault("pool", {})[0] = conv_pool
        mixers.setdefault("pe", {})[0] = conv_pe
        mixers.setdefault("act", {})[0] = conv_act
        mixers.setdefault("dve", {})[0] = conv_dve
        ident, rot, bones, rowmask = sb("ident", [P, P]), sb("rot", [P, P]), sb("bones", [P, P]), sb("rowmask", [P, 4])
        cosT, sinT = sb("cosT", [P, SEQ + L]), sb("sinT", [P, SEQ + L])
        tab_ok, in_pos, shape_ok = sem("tab_ok"), sem("in_pos"), sem("shape_ok")
        tpos, tang, tint, tred = (scr[:, 6000 + n * 528:6528 + n * 528] for n in range(4))

        def tables_pool(pool, step):
            pool.iota(tpos[:, SEQ:], [[1, L]], base=0, channel_multiplier=0, allow_small_or_imprecise_dtypes=True).then_inc(tab_ok, 1)
            pool.dma_start(tint[:, 0:SEQ].bitcast(I32), a["positions"].partition_broadcast(P)).then_inc(in_pos, 16)
            step(pool.memset(ident[:], 0.0))
            step(pool.memset(rot[:], 0.0))
            step(pool.memset(bones[:], 0.0))
            step(pool.memset(rowmask[:], 0.0))
            shapes = [0]

            def shape(ins):
                shapes[0] += 1
                ins.then_inc(shape_ok, 1)
                pool.wait_ge(shape_ok, shapes[0])

            shape(pool.affine_select(out=ident[:], in_=ident[:], compare_op=ALU.not_equal, fill=1.0, base=0,
                                     pattern=[[-1, P]], channel_multiplier=1))
            for h in range(2):
                for s in range(2):
                    v = rot[:, DH * h + 8 * s:DH * h + 8 * s + 8]
                    shape(pool.affine_select(out=v, in_=v, compare_op=ALU.not_equal, fill=1.0, base=-(DH * h + 8 * (1 - s)),
                                             pattern=[[-1, 8]], channel_multiplier=1))
                shape(pool.memset(bones[DH * h:DH * h + DH, DH * h:DH * h + DH], 1.0 / DH))
            for r in range(4):
                shape(pool.memset(rowmask[32 * r:32 * r + 32, r:r + 1], 1.0))

        def tables_dve(dve, step):
            dve.wait_ge(in_pos, 16)
            dve.wait_ge(in_par, 16)
            dve.wait_ge(tab_ok, 1)
            step(nc.vector.tensor_copy(tpos[:, 0:SEQ], tint[:, 0:SEQ].bitcast(I32)))
            step(nc.vector.tensor_scalar(tang, tpos, col("inv_freq"), None, ALU.mult))
            step(nc.vector.tensor_scalar(tint.bitcast(I32), tang, float(np_.float32(1 / (2 * np_.pi))), None, ALU.mult))
            step(nc.vector.tensor_copy(tred, tint.bitcast(I32)))
            for part in TWO_PI:
                step(nc.vector.scalar_tensor_tensor(tang, tred, -part, tang, ALU.mult, ALU.add))
            step(nc.vector.tensor_scalar(tang, tang, PI_BELOW, -PI_BELOW, ALU.min, ALU.max))
            nc.vector.scalar_tensor_tensor(tred, tang, -1.0, tang, ALU.mult, ALU.max).then_inc(tab_ok, 1)
            dve.wait_ge(tab_ok, 4)
            nc.vector.tensor_scalar(sinT[:], sinT[:], col("rope_sign"), None, ALU.mult).then_inc(tab_ok, 1)

        def tables_act(act):
            act.wait_ge(tab_ok, 2)
            nc.scalar.activation(sinT[:], tang, ACT.Sin).then_inc(tab_ok, 1)
            nc.scalar.activation(cosT[:], tred, ACT.Sin, scale=-1.0, bias=eps[:, 3:4]).then_inc(tab_ok, 1)

        at = {"o": 0}

        def area(n):
            at["o"] += n
            assert at["o"] <= SCRATCH, at["o"]
            return scr[:, at["o"] - n:at["o"]]

        nw1 = area(4096).rearrange("p (c l s e) -> p c l s e", c=2, l=16, s=2)
        nw2 = area(128).rearrange("p (c e) -> p c e", c=2)
        nk = area(1536).rearrange("p (m t) -> p m t", m=6)
        nvt = area(1024).rearrange("p (b n) -> p b n", b=2)
        ngate = area(96).rearrange("p (a n) -> p a n", a=2)
        nkc = area(64).rearrange("p (t h n) -> p t h n", t=2, h=2)
        nhk = area(64).rearrange("p (g n) -> p g n", g=4)
        nhv = area(512).rearrange("p (g r n) -> p g r n", g=4, r=4)
        nvc = area(1024).rearrange("p (g r d) -> p g r d", g=4, r=4)
        nmask = area(384)
        ncm = area(32).rearrange("p (a n) -> p a n", a=2)
        nc01 = area(32).rearrange("p (a n) -> p a n", a=2)
        nbias = area(2)
        nstat = area(64)
        npb = area(128)
        nunit = area(1)
        nt = area(256)
        _sm = area(2304)
        nsq = _sm[:, 0:2048].rearrange("p (m t) -> p m t", m=8)
        nS, nP, nPT = (_sm[:, 768 * n:768 * n + 768].rearrange("p (b n) -> p b n", b=2) for n in range(3))
        nprod = scr[:, 4224:8320].rearrange("p (c l e) -> p c l e", c=2, l=32)
        nhead = area(32)[:, 0:31]
        nfold = area(64)
        nev = area(120).rearrange("p (h n) -> p h n", h=2)
        nrotg = ts[:].rearrange("p k t -> p (k t)")[:, 0:512].rearrange("p (g n) -> p g n", g=4)
        nsel = [b[0:16].rearrange("p k t -> p (k t)")[:, 0:512].rearrange("p (m n) -> p m n", m=4)
                for b in (tu, th)]
        nroot = ry[0:16, 0:SEQ]
        nr = y[0:16, 6:8, 0:SEQ]
        nq = sq[:, :, META:]
        nv = y[:, :, META:]
        n_oc = sem("n_oc")
        npc = scr[:, 0:1024].rearrange("p (h b n) -> p h b n", h=2, b=4)
        npct = scr[:, 1024:2048].rearrange("p (h t q) -> p h t q", h=2, t=2)
        ncs = scr[:, 2048:2560].rearrange("p (h a n) -> p h a n", h=2, a=2)
        n_w, n_a, n_v, n_gate, n_sig, n_sq, n_mean, n_root, n_rec, n_perm, n_bc, n_used = (
            sem("n_" + s) for s in ("w", "a", "v", "gate", "sig", "sq", "mean", "root", "rec", "perm", "bc", "used"))
        n_late, n_ev, n_fold = sem("n_late"), sem("n_ev"), sem("n_fold")
        n_mask, n_tr, n_vt, n_gt, n_hid, n_pos, n_gelu, n_comp, n_kc, n_vc = (
            sem("n_" + s) for s in ("mask", "tr", "vt", "gt", "hid", "pos", "gelu", "comp", "kc", "vc"))
        n_cs, n_cexp, n_csub, n_cp, n_ct, n_cpt = (sem("n_" + s) for s in ("cs", "cexp", "csub", "cp", "ct", "cpt"))
        n_s, n_min, n_exp, n_p, n_pt, n_ptc, n_o = (sem("n_" + s) for s in ("s", "min", "exp", "p", "pt", "ptc", "o"))
        KTILES = (0, 1, 4, 5, 8, 9)
        VTILES = (2, 3, 6, 7, 10, 11)
        SMALL = [("p", i) for i in range(6)]
        for _i in range(6):
            SMALL += [("p", 6 + _i), ("r", _i)]
        SMALL += [("p", i) for i in (12, 13)] + [("r", i) for i in range(6, 14)]
        KEY_AFTER = {3: (0, 1), 5: (2,), 6: (3,), 9: (4,), 10: (5,)}
        UNITS = [(j, h, b) for j in range(KD) for h in range(2) for b in range(2)]

        def nsa_pool(pool, step):
            pool.wait_ge(m_lo, 8)
            pool.wait_ge(tab_ok, 5)
            pool.dma_start(nw1, a["cmp_w1"].rearrange("p (c l s e) -> p c l s e", c=2, l=16, s=2)).then_inc(n_w, 16)
            pool.dma_start(nw2[0:DH], a["cmp_w2"].rearrange("p (c e) -> p c e", c=2)).then_inc(n_w, 16)
            pool.wait_ge(n_w, 32)
            flat = nprod.rearrange("p c l e -> p (c l) e")
            step(pool.tensor_tensor(flat, nw1.rearrange("p c l s e -> p (c l s) e"),
                                    par[:, COL["cmp_pos"]:COL["cmp_pos"] + 64].unsqueeze(2).to_broadcast([P, 64, DH]), ALU.mult))
            for w in (16, 8, 4, 2):
                step(pool.tensor_tensor(nprod[:, :, 0:w, :], nprod[:, :, 0:w, :], nprod[:, :, w:2 * w, :], ALU.add))
            step(pool.tensor_tensor(npb.rearrange("p (c e) -> p c e", c=2), nprod[:, :, 0, :], nprod[:, :, 1, :], ALU.add))
            step(pool.memset(nunit, 1.0))
            step(pool.memset(nmask, 0.0))
            step(pool.memset(ncm, 0.0))
            step(pool.memset(nc01, 1.0))
            for s in (0, 256):
                pool.affine_select(out=nmask[:, s:s + P], in_=nmask[:, s:s + P], compare_op=ALU.is_ge, fill=BIG, base=0,
                                   pattern=[[-1, P]], channel_multiplier=1).then_inc(n_mask, 1)
            for m, fill in ((ncm, BIG), (nc01, 0.0)):
                pool.affine_select(out=m, in_=m, compare_op=ALU.is_ge, fill=fill, base=-31,
                                   pattern=[[P, 2], [-16, 16]], channel_multiplier=1).then_inc(n_mask, 1)
            pool.memset(nhk, 0.0).then_inc(n_mask, 1)
            pool.memset(nkc, 0.0).then_inc(n_mask, 1)
            pool.memset(nhv, 0.0).then_inc(n_mask, 1)

        def nsa_pool_late(pool, step):
            pool.wait_ge(used, last("ffn0_b"))
            for g in range(4):
                pool.tensor_scalar(nrotg[:, g, :], rot[:], col("k_gain", g) if g < 3 else col("q_gain"), None, ALU.mult).then_inc(n_late, 1)
            step(pool.memset(nhead, 0.0))
            for h in range(2):
                pool.memset(nhead[DH * h:DH * h + DH, 15 + h:16 + h], 1.0 / DH).then_inc(n_late, 1)
                pool.wait_ge(n_late, 5 + h)
            for i in range(2):
                v = nsel[i].rearrange("p m (h d) -> p m h d", h=2)
                step(pool.memset(nsel[i], 0.0))
                pool.affine_select(out=v, in_=v, compare_op=ALU.not_equal, fill=1.0, base=-8 * i,
                                   pattern=[[-2, 4], [-1, 2], [0, DH]], channel_multiplier=1).then_inc(n_late, 1)
                pool.wait_ge(n_late, 7 + i)
            pool.tensor_tensor(nfold, ident[:, 0:DH], ident[:, DH:P], ALU.add).then_inc(n_late, 1)
            pool.wait_ge(n_hid, 2)
            pool.memset(npc, 0.0).then_inc(n_late, 1)

        def nsa_pe(pe, gemm, begin, opening):
            pe.wait_ge(shape_ok, 11)

            def mean(m):
                g = m % 6 if m < 6 else m - 6
                pe.wait_ge(n_sq, m + 1)
                if m == 6:
                    pe.wait_ge(n_root, 1)
                nc.tensor.matmul(mix[0][0:16, 0:SEQ], nhead[:, 15 - 2 * g:31 - 2 * g], nsq[:, m % 8, :],
                                 start=(g == 0), stop=(m in (5, 13))).then_inc(n_mean, 1)

            def small(kind, m):
                n = SMALL.index((kind, m))
                if n >= 3:
                    pe.wait_ge(n_used, n - 2)
                dst = (mix[1], mix[2], stat)[n % 3][:, 0:SEQ]
                g = m if m < 6 else m - 6
                if kind == "p":
                    pe.wait_ge(n_a, m + 1)
                    v = nk[:, m, :] if m < 6 else nq[:, m - 6, :]
                    nc.tensor.matmul(dst, nrotg[:, m // 2 if m < 6 else 3, :], v, start=True, stop=True).then_inc(n_perm, 1)
                else:
                    pe.wait_ge(n_rec, 1 if m < 6 else 2)
                    nc.tensor.matmul(dst, nsel[g // 4][:, g % 4, :], nr[:, m // 6 if m < 12 else 1, :], start=True, stop=True).then_inc(n_bc, 1)

            begin(2, ("nsa_kv", 0), ("nsa_kv", 1))
            for t in range(2, 12):
                gemm("nsa_kv", xh, xl, META, None, first=t, last=t + 1)
                if t == 3:
                    pe.wait_ge(n_late, 9)
                    pe.wait_ge(root_ok, norm_of(2) + 1)
                for m in KEY_AFTER.get(t, ()):
                    small("p", m)
                    mean(m)
            gemm("nsa_gate", xh, xl, META, None)
            for m in range(KD):
                gemm("nsa_q", xh, xl, META, None, first=m, last=m + 1)
                if m:
                    small("p", 5 + m)
                    mean(5 + m)
                if 0 < m < 7:
                    small("r", m - 1)
            pe.wait_ge(acc_used, TILE["nsa_q"] + 8)
            small("p", 13)
            mean(13)
            pe.wait_ge(n_w, 32)
            pe.wait_ge(n_v, 2)
            for h in range(2):
                for c in range(2):
                    src = (nk, nv)[c]
                    for l in range(16):
                        ins = nc.tensor.matmul(acc[h][:, 32 * c:32 * c + 32], nw1[DH * h:DH * h + DH, c, l].rearrange("p s e -> p (s e)"),
                                               src[DH * h:DH * h + DH, 0:2, l:SEQ:16], start=(l == 0), stop=(l == 15))
                ins.then_inc(n_hid, 1)
            for c in range(2):
                ins = nc.tensor.matmul(acc[2][0:DH, c:c + 1], npb[0:DH, DH * c:DH * c + DH], nunit[0:DH, :], start=True, stop=True)
            ins.then_inc(n_pos, 1)
            for m in range(6, 9):
                small("r", m)
            for h in range(2):
                pe.wait_ge(n_ev, 2 * h + 2)
                nc.tensor.matmul(acc[h][0:DH, 64:64 + 4 * NCMP], nfold, nev[:, h, :], start=True, stop=True).then_inc(n_fold, 1)
            for m in range(9, 14):
                small("r", m)
            pe.wait_ge(n_sig, 1)
            pe.wait_ge(n_used, len(SMALL))
            for qt in range(2):
                ins = nc.tensor.transpose(stat[:, P * qt:P * qt + P], tg[:, 1, META + P * qt:META + P * qt + P], ident[:])
            ins.then_inc(n_tr, 1)
            pe.wait_ge(n_v, 6)
            pe.wait_ge(n_gt, 1)
            for b in range(2):
                for kt in range(2):
                    for t in range(2):
                        ins = nc.tensor.transpose((stat, acc[3])[b][:, 256 * kt + P * t:256 * kt + P * t + P],
                                                  nv[:, 2 + 2 * b + t, P * kt:P * kt + P], ident[:])
                ins.then_inc(n_tr, 1)
            pe.wait_ge(n_gelu, 6)
            for h in range(2):
                for t in range(2):
                    nc.tensor.matmul(acc[2][DH * h:DH * h + DH, 16 * t:16 * t + 16], nw2[0:DH, 0, :], nhk[0:DH, 2 * t + h, :],
                                     start=(t == 0), stop=True, skip_group_check=True)
            for g in range(4):
                ins = nc.tensor.matmul(mix[0][:, DH * g:DH * g + DH], nhv[0:DH, g].rearrange("p r n -> p (r n)"), nw2[0:DH, 1, :],
                                       start=True, stop=True)
            ins.then_inc(n_comp, 1)
            pe.wait_ge(n_kc, 2)
            for qt in range(2):
                for j in range(KD):
                    c = 256 * qt + 32 * j
                    ins = nc.tensor.matmul(acc[0][:, c:c + 32], nq[:, j, P * qt:P * qt + P], nkc[:, j // 4].rearrange("p h n -> p (h n)"),
                                           start=True, stop=True)
            ins.then_inc(n_cs, 1)

            def scores(n):
                j, h, b = UNITS[n]
                if n >= 3:
                    pe.wait_ge(n_min, n - 2)
                elif n == 2:
                    pe.wait_ge(n_csub, 2)
                for qt in range(2):
                    ins = nc.tensor.matmul(acc[(n + 1) % 3][:, P * qt:P * qt + P * (qt + 1)], nq[DH * h:DH * h + DH, j, P * qt:P * qt + P],
                                           nk[DH * h:DH * h + DH, 2 + 2 * b + j // 4, 0:P * (qt + 1)], start=True, stop=True)
                ins.then_inc(n_s, 1)

            def turned(n):
                pe.wait_ge(n_p, n + 1)
                if n >= 2:
                    pe.wait_ge(n_ptc, n - 1)
                else:
                    pe.wait_ge(n_vt, 2)
                dst = (acc[3], stat)[n % 2]
                for at_, src in ((0, 0), (P, P), (2 * P, 2 * P)):
                    ins = nc.tensor.transpose(dst[:, at_:at_ + P], nP[:, n % 2, src:src + P], ident[:])
                ins.then_inc(n_pt, 1)

            def values(n):
                j, h, b = UNITS[n]
                t = j // 4
                g = 2 * t + h
                dst = mix[j % 2][DH * h:DH * h + DH]
                if b == 0 and j >= 2:
                    pe.wait_ge(m_lo, 8 + j - 1)
                    nc.tensor.matmul(dst[:, 0:SEQ], nvc[:, g, j % 4, :], npct[:, h, t, :], start=True, stop=False)
                pe.wait_ge(n_ptc, n + 1)
                nc.tensor.matmul(dst[:, 0:SEQ], nvt[:, b, DH * g:DH * g + DH], nPT[:, n % 2, 0:SEQ], start=(b == 0 and j < 2), stop=False)
                ins = nc.tensor.matmul(dst[:, P:SEQ], nvt[:, b, 256 + DH * g:256 + DH * g + DH], nPT[:, n % 2, SEQ:SEQ + P],
                                       start=False, stop=(b == 1 and j >= 2))
                ins.then_inc(n_o, 1)

            def compressed_turned(h, t):
                pe.wait_ge(n_cp, h + 1)
                if t == 1 or h == 1:
                    pe.wait_ge(n_cpt, 2 * h + t)
                for qt in range(2):
                    ins = nc.tensor.transpose(mix[2][:, P * qt:P * qt + P], npc[:, h, 2 * qt + t, :], ident[:])
                ins.then_inc(n_ct, 1)

            scores(0)
            scores(1)
            pe.wait_ge(n_vc, 4)
            for n in range(len(UNITS) + 1):
                if n + 2 < len(UNITS):
                    scores(n + 2)
                if n < len(UNITS):
                    turned(n)
                if n:
                    values(n - 1)
                if 2 <= n < 6:
                    compressed_turned((n - 2) // 2, n % 2)
                if n == 8:
                    pe.wait_ge(n_cpt, 4)
                    for j in range(2):
                        for h in range(2):
                            ins = nc.tensor.matmul(mix[j][DH * h:DH * h + DH, 0:SEQ], nvc[:, h, j, :], npct[:, h, 0, :], start=False, stop=True)
                        ins.then_inc(n_oc, 1)
            pe.wait_ge(m_lo, 16)
            gemm("nsa_out", hh, hl, META, (m_lo, 8))

        def nsa_act(act, step, ahead, residual):
            def squared(m, src, more=None):
                act.wait_ge(n_a, m + 1)
                if m >= 8:
                    act.wait_ge(n_mean, m - 7)
                nc.scalar.activation(nsq[:, m % 8, :], src, ACT.Square).then_inc(n_sq, 1)

            def rooted(g):
                act.wait_ge(n_mean, (6, 14)[g])
                if g:
                    act.wait_ge(n_rec, 1)
                nc.scalar.activation(nroot, mix[0][0:16, 0:SEQ], ACT.Sqrt, scale=(1.0, 64.0)[g],
                                     bias=eps[0:16, 0:1] if g == 0 else eps[0:16, 4:5]).then_inc(n_root, 1)

            for m in range(12):
                ahead(BASE["nsa_kv"] + m)
                if m in KTILES:
                    i = KTILES.index(m)
                    squared(i, nk[:, i, :])
            act.wait_ge(n_gate, 1)
            nc.scalar.activation(tg[:, 1, META:], tg[:, 0, META:], ACT.Sigmoid).then_inc(n_sig, 1)
            ahead(BASE["nsa_gate"])
            rooted(0)
            for m in range(KD):
                ahead(BASE["nsa_q"] + m)
                squared(6 + m, nq[:, m, :])
            rooted(1)
            for h in range(2):
                act.wait_ge(n_hid, h + 1)
                nc.scalar.activation(nev[0:DH, h, :].rearrange("p (a n) -> p a n", a=4),
                                     acc[h][0:DH, 0:64].rearrange("p (a n) -> p a n", a=4)[:, :, 0:NCMP], ACT.Copy).then_inc(n_ev, 1)
                nc.scalar.activation(nev[DH:P, h, :].rearrange("p (a n) -> p a n", a=4),
                                     acc[h][DH:P, 0:64].rearrange("p (a n) -> p a n", a=4)[:, :, 1:NCMP + 1], ACT.Copy).then_inc(n_ev, 1)
            act.wait_ge(n_fold, 2)
            act.wait_ge(n_pos, 2)
            act.wait_ge(n_mask, 6)
            for h in range(2):
                nc.scalar.activation(nhk[0:DH, h:4:2, 0:NCMP], acc[h][0:DH, 64:64 + 2 * NCMP].rearrange("p (t n) -> p t n", t=2),
                                     ACT.Gelu_apprx_tanh, bias=nbias[0:DH, 0:1]).then_inc(n_gelu, 1)
                for t in range(2):
                    src = acc[h][0:DH, 64 + NCMP * (2 + t):64 + NCMP * (3 + t)]
                    nc.scalar.activation(nhv[0:DH, 2 * t + h, :, 0:NCMP], src.unsqueeze(1).to_broadcast([DH, 4, NCMP]),
                                         ACT.Gelu_apprx_tanh, bias=nbias[0:DH, 1:2]).then_inc(n_gelu, 1)
            act.wait_ge(n_tr, 3)
            nc.scalar.activation(nvt[:, 0, :], stat[:, :], ACT.Copy).then_inc(n_vt, 1)
            nc.scalar.activation(nvt[:, 1, :], acc[3][:, :], ACT.Copy).then_inc(n_vt, 1)
            for h in range(2):
                act.wait_ge(n_csub, h + 1)
                nc.scalar.activation(ncs[:, h], ncs[:, h], ACT.Exp, scale=-1.0).then_inc(n_cexp, 1)

            def exps(n):
                act.wait_ge(n_min, n + 1)
                if n >= 2:
                    act.wait_ge(n_pt, n - 1)
                for qt in range(2):
                    s = slice(P * qt, P * qt + P * (qt + 1))
                    act.wait_ge(n_p, n - 1) if n >= 2 else None
                    nc.scalar.activation(nP[:, n % 2, s], nS[:, n % 2, s], ACT.Exp, scale=-1.0, bias=nstat[:, 2 * (n % 2) + qt:2 * (n % 2) + qt + 1],
                                         accum_out=nstat[:, 8 + 2 * (n % 2) + qt:9 + 2 * (n % 2) + qt]).then_inc(n_exp, 1)

            exps(0)
            for n in range(len(UNITS)):
                if n + 1 < len(UNITS):
                    exps(n + 1)
                act.wait_ge(n_pt, n + 1)
                if n >= 2:
                    act.wait_ge(n_o, n - 1)
                nc.scalar.activation(nPT[:, n % 2, :], (acc[3], stat)[n % 2][:, 0:384], ACT.Copy).then_inc(n_ptc, 1)
                if 2 <= n < 6:
                    act.wait_ge(n_ct, n - 1)
                    nc.scalar.activation(npct[:, (n - 2) // 2, n % 2, :], mix[2][:, 0:SEQ], ACT.Copy).then_inc(n_cpt, 1)
                if n == 8:
                    attn_hi(act, 0, n_oc, 1)
                    attn_hi(act, 1, n_oc, 2)
                elif n % 4 == 0 and n > 8:
                    attn_hi(act, n // 4 - 1, n_o, n)
            attn_hi(act, KD - 1, n_o, len(UNITS))
            for m in range(KD):
                residual(3, m, BASE["nsa_out"] + m)

        def attn_hi(act, j, o, count, idx=1):
            act.wait_ge(o, count)
            nc.scalar.activation(hh[:, j, META:], mix[j % 2][:, 0:SEQ], ACT.Copy).then_inc(m_hi, 1)

        def attn_lo(dve, j, idx=1):
            dve.wait_ge(m_hi, 8 * idx + j + 1)
            nc.vector.tensor_tensor(hl[:, j, META:], mix[j % 2][:, 0:SEQ], hh[:, j, META:].bitcast(F32), ALU.subtract).then_inc(m_lo, 1)

        def nsa_dve(dve, step, ahead, tail):
            def tile(m):
                return nk[:, m, :] if m < 6 else nq[:, m - 6, :]

            def rotated(m):
                n, v = SMALL.index(("p", m)), tile(m)
                dve.wait_ge(n_perm, m + 1)
                nc.vector.tensor_tensor(nt, (mix[1], mix[2], stat)[n % 3][:, 0:SEQ], sinT[:, 0:SEQ], ALU.mult).then_inc(n_used, 1)
                dve.wait_ge(n_sq, m + 1)
                step(nc.vector.scalar_tensor_tensor(v, v, col("k_gain", m // 2) if m < 6 else col("q_gain"), cosT[:, 0:SEQ],
                                                    ALU.mult, ALU.mult))
                dve.wait_ge(n_used, n + 1)
                step(nc.vector.tensor_tensor(v, v, nt, ALU.add))

            def scaled(m):
                n, v = SMALL.index(("r", m)), tile(m)
                dve.wait_ge(n_bc, m + 1)
                nc.vector.tensor_tensor(v, v, (mix[1], mix[2], stat)[n % 3][:, 0:SEQ], ALU.mult).then_inc(n_used, 1)

            def inverse(g):
                dve.wait_ge(n_root, g + 1)
                nc.vector.reciprocal(nr[:, g, :], nroot).then_inc(n_rec, 1)

            dve.wait_ge(tab_ok, 5)
            for m in range(12):
                b = BASE["nsa_kv"] + m
                dve.wait_ge(used, b + 1)
                if m in KTILES:
                    ins = nc.vector.tensor_tensor(nk[:, KTILES.index(m), :], bank("nsa_kv", m)[:, 0:SEQ], rx[:, META:], ALU.mult)
                    ins.then_inc(n_a, 1)
                    dve.wait_ge(n_a, KTILES.index(m) + 1)
                else:
                    ins = nc.vector.tensor_tensor(nv[:, VTILES.index(m), :], bank("nsa_kv", m)[:, 0:SEQ], rx[:, META:], ALU.mult)
                    ins.then_inc(n_v, 1)
                    dve.wait_ge(n_v, VTILES.index(m) + 1)
                dve.sem_inc(acc_used, 1)
                ahead(b)
                for i in KEY_AFTER.get(m, ()):
                    rotated(i)
            dve.wait_ge(used, BASE["nsa_gate"] + 1)
            nc.vector.tensor_tensor(tg[:, 0, META:], bank("nsa_gate", 0)[:, 0:SEQ], rx[:, META:], ALU.mult).then_inc(n_gate, 1)
            dve.wait_ge(n_gate, 1)
            dve.sem_inc(acc_used, 1)
            ahead(BASE["nsa_gate"])
            inverse(0)
            for m in range(KD):
                dve.wait_ge(used, BASE["nsa_q"] + m + 1)
                dve.wait_ge(sum_ok, 3)
                nc.vector.scalar_tensor_tensor(nq[:, m, :], bank("nsa_q", m)[:, 0:SEQ], -1.0, rx[:, META:],
                                               ALU.mult, ALU.mult).then_inc(n_a, 1)
                dve.wait_ge(n_a, 6 + m + 1)
                dve.sem_inc(acc_used, 1)
                ahead(BASE["nsa_q"] + m)
                if m:
                    rotated(5 + m)
                if 0 < m < 7:
                    scaled(m - 1)
            rotated(13)
            inverse(1)
            dve.wait_ge(n_pos, 1)
            nc.vector.tensor_tensor(nbias[0:DH, :], acc[2][0:DH, 0:2], par[0:DH, COL["cmp_b1"]:COL["cmp_b1"] + 2], ALU.add).then_inc(n_pos, 1)
            for m in range(6, 14):
                scaled(m)
            dve.wait_ge(n_tr, 1)
            nc.vector.tensor_copy(ngate, stat[:, 0:SEQ].rearrange("p (a n) -> p a n", a=2)[:, :, 0:48]).then_inc(n_gt, 1)
            dve.wait_ge(n_comp, 1)
            dve.wait_ge(n_mask, 7)
            for h in range(2):
                nc.vector.tensor_copy(nkc[DH * h:DH * h + DH, :, h, :], acc[2][DH * h:DH * h + DH, 0:32].rearrange("p (t n) -> p t n", t=2)) \
                    .then_inc(n_kc, 1)
            for r in range(4):
                nc.vector.tensor_scalar(nvc[:, :, r, :], mix[0][:, 0:SEQ].rearrange("p (g d) -> p g d", g=4), rowmask[:, r:r + 1],
                                        None, ALU.mult).then_inc(n_vc, 1)
            dve.wait_ge(n_cs, 1)
            for h in range(2):
                s = ncs[:, h].rearrange("p a (j n) -> p a j n", j=KD)
                step(nc.vector.tensor_tensor(s, acc[0][:, :].rearrange("p (a j h n) -> p a j h n", a=2, j=KD, h=2)[:, :, :, h, :],
                                             ncm.unsqueeze(2).to_broadcast([P, 2, KD, 16]), ALU.add))
                least = nstat[:, 16:32].rearrange("p (a j) -> p a j", a=2)
                step(nc.vector.tensor_reduce(least, s, AX.X, ALU.min))
                nc.vector.tensor_tensor(s, s, least.unsqueeze(3).to_broadcast([P, 2, KD, 16]), ALU.subtract).then_inc(n_csub, 1)

            def compressed(h):
                dve.wait_ge(n_late, 10)
                dve.wait_ge(n_cexp, h + 1)
                s = ncs[:, h].rearrange("p a (j n) -> p a j n", j=KD)
                tot = nstat[:, 32:48]
                tot3 = tot.rearrange("p (a j) -> p a j", a=2)
                step(nc.vector.tensor_reduce(tot3, s, AX.X, ALU.add))
                step(nc.vector.reciprocal(tot, tot))
                step(nc.vector.tensor_tensor(tot.rearrange("p (a t r) -> p a t r", a=2, t=2), tot.rearrange("p (a t r) -> p a t r", a=2, t=2),
                                             ngate[:, :, 0:16].rearrange("p a (t g r) -> p a t g r", t=2, g=2)[:, :, :, h, :], ALU.mult))
                step(nc.vector.tensor_tensor(s, s, tot3.unsqueeze(3).to_broadcast([P, 2, KD, 16]), ALU.mult))
                nc.vector.tensor_tensor(npc[:, h].rearrange("p (a t) (r n) -> p a (t r) n", a=2, n=32)[:, :, :, 0:16], s,
                                        nc01.unsqueeze(2).to_broadcast([P, 2, KD, 16]), ALU.mult).then_inc(n_cp, 1)

            def least(n):
                dve.wait_ge(n_s, n + 1)
                dve.wait_ge(n_mask, 4)
                if n >= 2:
                    dve.wait_ge(n_exp, 2 * n - 2)
                for qt in range(2):
                    s = slice(P * qt, P * qt + P * (qt + 1))
                    ins = nc.vector.tensor_tensor_reduce(nS[:, n % 2, s], acc[(n + 1) % 3][:, s], nmask[:, s], 1.0, 3e38, ALU.add,
                                                         ALU.min, nstat[:, 2 * (n % 2) + qt:2 * (n % 2) + qt + 1])
                ins.then_inc(n_min, 1)

            least(0)
            for n in range(len(UNITS)):
                if n + 1 < len(UNITS):
                    least(n + 1)
                j, h, b = UNITS[n]
                head = 8 * (j // 4) + 4 * h + j % 4
                dve.wait_ge(n_exp, 2 * n + 2)
                rec = nstat[:, 12:14]
                if n:
                    dve.wait_ge(n_p, n)
                step(nc.vector.reciprocal(rec, nstat[:, 8 + 2 * (n % 2):10 + 2 * (n % 2)]))
                for qt in range(2):
                    s = slice(P * qt, P * qt + P * (qt + 1))
                    g = 16 * (b + 1) + head
                    ins = nc.vector.tensor_scalar(nP[:, n % 2, s], nP[:, n % 2, s], rec[:, qt:qt + 1], ngate[:, qt, g:g + 1],
                                                  ALU.mult, ALU.mult)
                ins.then_inc(n_p, 1)
                if n < 2:
                    compressed(n)
                if n == 9:
                    attn_lo(dve, 0)
                    attn_lo(dve, 1)
                elif n % 4 == 1 and n > 9:
                    attn_lo(dve, n // 4 - 1)
            attn_lo(dve, KD - 1)
            for m in range(KD):
                tail(3, m, "nsa_out", BASE["nsa_out"] + m)

        mixers["pool_late"] = {2: nsa_pool_late}
        mixers["pool"][2], mixers["pe"][2], mixers["act"][2], mixers["dve"][2] = nsa_pool, nsa_pe, nsa_act, nsa_dve
        at["o"] = 0
        gls = area(1536).rearrange("p (a n) -> p a n", a=3)
        ge = area(1536).rearrange("p (a n) -> p a n", a=3)
        gv = scr[:, 0:3072].rearrange("p (a n) -> p a n", a=3)
        gb = area(1088).rearrange("p (h t) -> p h t", h=4)
        gkk = area(1088).rearrange("p (h t) -> p h t", h=4)
        gq = area(1088).rearrange("p (h t) -> p h t", h=4)
        gk = area(1088).rearrange("p (h t) -> p h t", h=4)
        gkt = area(1536).rearrange("p (a n) -> p a n", a=3)
        gS = ([area(256) for _ in range(4)], [b[:].rearrange("p k t -> p (k t)")[:, 0:256] for b in (tg, ts, tu, th)])
        gatt = area(512).rearrange("p (b h n) -> p b h n", b=2, h=4)
        gwg = area(512)
        gdec = area(20).rearrange("p (h n) -> p h n", h=4)
        gtri = area(128)
        ghead = area(7)
        gsel = area(512)[0:4].rearrange("p (h n) -> p h n", h=4)
        groot = area(272)[0:4]
        gsq = scr[:, 3072:3072 + 2176].rearrange("p (m t) -> p m t", m=8)
        gkr, gqr = (tg, ts), (tu, th)
        g_w, g_tri, g_lr, g_z, g_e, g_ln, g_ls, g_kr, g_b, g_bc, g_qr, g_dif, g_eq = (
            sem("g_" + s) for s in ("w", "tri", "lr", "z", "e", "ln", "ls", "kr", "b", "bc", "qr", "dif", "eq"))
        g_dec, g_v, g_vt, g_vc, g_kt, g_kc, g_r, g_rs, g_att, g_attc, g_kv, g_S, g_o, g_oc = (
            sem("g_" + s) for s in ("dec", "v", "vt", "vc", "kt", "kc", "r", "rs", "att", "attc", "kv", "S", "o", "oc"))
        g_sq, g_mean, g_root, g_f = (sem("g_" + s) for s in ("sq", "mean", "root", "f"))
        g_late, g_inv, g_spread, g_ys = (sem("g_" + s) for s in ("late", "inv", "spread", "ys"))
        TOK = ((0, META), (META, P), (META + P, P))
        CHUNKS = [(0, META, 0, 0)] + [(META + 64 * n, 64, 1 + n // 2, 64 * (n % 2)) for n in range(4)]

        def gla_pool(pool, step):
            pool.wait_ge(m_lo, 16)
            step(pool.memset(gwg[0:64, :], 0.0))
            pool.dma_start(gwg[0:16, :], a["w_gate"]).then_inc(g_w, 16)
            pool.dma_start(gwg[32:33, :], a["gate_row"]).then_inc(g_w, 16)
            step(pool.memset(gtri, 1.0))
            step(pool.affine_select(out=gtri, in_=gtri, compare_op=ALU.is_ge, fill=0.0, base=0, pattern=[[1, P]], channel_multiplier=-1))
            pool.memset(gtri[0:64, 64:P], 0.0).then_inc(g_tri, 1)
            pool.memset(gatt.rearrange("p b h n -> p (b h n)"), 0.0).then_inc(g_tri, 1)

        def gla_pool_late(pool, step):
            step(pool.memset(ghead, 0.0))
            pool.memset(ghead[:, 3:4], 1.0 / D).then_inc(g_late, 1)
            step(pool.memset(gsel, 0.0))
            pool.affine_select(out=gsel, in_=gsel, compare_op=ALU.not_equal, fill=1.0, base=0, pattern=[[-1, 4], [0, P]],
                               channel_multiplier=1).then_inc(g_late, 1)
            pool.wait_ge(g_rs, 8)
            for m in range(KD):
                pool.wait_ge(g_sq, m + 1)
                pool.tensor_tensor(y[:, m, :], y[:, m, :], sq[:, m, :], ALU.mult).then_inc(g_ys, 1)

        def gla_pe(pe, gemm, begin, opening):
            begin(5, ("gla_lr", 0), ("gla_k", 0))
            gemm("gla_k", xh, xl, 0, None, first=1, last=2)
            pe.wait_ge(g_w, 32)
            pe.wait_ge(g_lr, 2)
            for n, (s, w) in enumerate(TOK):
                ins = nc.tensor.matmul(mix[n][0:w, :], ry[0:33, s:s + w], gwg[0:33, :], start=True, stop=True)
            ins.then_inc(g_z, 1)
            gemm("gla_k", xh, xl, 0, None, first=2)
            gemm("gla_q", xh, xl, 0, None, last=3)
            pe.wait_ge(g_ls, 3)
            pe.wait_ge(g_tri, 2)
            for h in range(4):
                for n, (s, w) in enumerate(TOK):
                    ins = nc.tensor.matmul((mix + [stat])[h][:, s:s + w], gls[0:w, n, P * h:P * h + P], gtri[0:w, 0:w], start=True, stop=True)
                ins.then_inc(g_b, 1)
            gemm("gla_q", xh, xl, 0, None, first=3)
            gemm("gla_v", xh, xl, 0, None)
            pe.wait_ge(g_bc, 4)
            for n, (s, w) in enumerate(TOK):
                for e in range(2):
                    i = 2 * n + e
                    pe.wait_ge(g_v, 4 * e + 4)
                    if i >= 3:
                        pe.wait_ge(g_vc, i - 2)
                    for m in range(4):
                        ins = nc.tensor.transpose(mix[i % 3][0:w, P * m:P * m + P], y[:, 4 * e + m, s:s + w], ident[:])
                    ins.then_inc(g_vt, 1)
            pe.wait_ge(g_eq, 12)
            for n, (s, w) in enumerate(TOK):
                pe.wait_ge(g_vc, 4 + n)
                for h in range(4):
                    ins = nc.tensor.transpose(mix[n][0:w, P * h:P * h + P], gkk[:, h, s:s + w], ident[:])
                ins.then_inc(g_kt, 1)
            pe.wait_ge(acc_used, TILE["gla_r"])
            pe.wait_ge(g_kc, 3)

            def att(c):
                s, w, n, base = CHUNKS[c]
                if c >= 2:
                    pe.wait_ge(g_attc, c - 1)
                for h in range(4):
                    ins = nc.tensor.matmul(acc[c % 2][base:base + w, 64 * h:64 * h + w], gk[:, h, s:s + w], gq[:, h, s:s + w],
                                           start=True, stop=True)
                ins.then_inc(g_att, 1)

            def kv(c):
                s, w, n, base = CHUNKS[c]
                if c:
                    pe.wait_ge(g_S, 4 * c)
                for h in range(4):
                    ins = nc.tensor.matmul((mix[2], stat)[h // 2][:, 256 * (h % 2):256 * (h % 2) + 256], gkt[base:base + w, n, P * h:P * h + P],
                                           gv[base:base + w, n, 256 * h:256 * h + 256], start=True, stop=True)
                ins.then_inc(g_kv, 1)

            att(0)
            kv(0)
            for c, (s, w, n, base) in enumerate(CHUNKS):
                if c + 1 < 5:
                    att(c + 1)
                if c < 4:
                    gemm("gla_r", xh, xl, 0, None, first=2 * c, last=2 * c + 1)
                pe.wait_ge(g_attc, c + 1)
                if c >= 2:
                    pe.wait_ge(g_oc, c - 1)
                for h in range(4):
                    if h == 2 and c < 4:
                        gemm("gla_r", xh, xl, 0, None, first=2 * c + 1, last=2 * c + 2)
                    if c:
                        pe.wait_ge(g_S, 4 * (c - 1) + h + 1)
                    for v in range(2):
                        dst = acc[2 + c % 2][:, 64 * (2 * h + v):64 * (2 * h + v) + w]
                        ins = nc.tensor.matmul(dst, gv[base:base + w, n, 256 * h + P * v:256 * h + P * v + P], gatt[base:base + w, c % 2, h, 0:w],
                                               start=True, stop=(c == 0))
                        if c:
                            ins = nc.tensor.matmul(dst, gS[(c - 1) % 2][h][:, P * v:P * v + P], gq[:, h, s:s + w], start=False, stop=True)
                ins.then_inc(g_o, 1)
                if 0 < c + 1 < 4:
                    kv(c + 1)
            pe.wait_ge(g_late, 2)
            for h in range(4):
                pe.wait_ge(g_sq, 2 * h + 2)
                for v in range(2):
                    ins = nc.tensor.matmul(mix[0][0:4, 0:L], ghead[:, 3 - h:7 - h], gsq[:, 2 * h + v, :],
                                           start=(h == 0 and v == 0), stop=(h == 3 and v == 1))
            ins.then_inc(g_mean, 1)
            pe.wait_ge(g_S, 16)
            pe.wait_ge(g_inv, 1)
            for h in range(4):
                nc.tensor.matmul(spread_bank(h)[:, 0:L], gsel[:, h, :], ry[0:4, :], start=True, stop=True).then_inc(g_spread, 1)
            opening((("gla_out", 0), ("gla_out", 1)), hh, hl, 0, (m_lo, 16))
            gemm("gla_out", hh, hl, 0, None, first=2)

        def spread_bank(h):
            return (mix[1], mix[2], stat, mix[0])[h]

        def gla_act(act, step, ahead, residual):
            ahead(BASE["gla_lr"])
            ahead(BASE["gla_k"])
            act.wait_ge(g_z, 1)
            for n, (s, w) in enumerate(TOK):
                nc.scalar.activation(ge[0:w, n, :], mix[n][0:w, :], ACT.Abs).then_inc(g_e, 1)
            ahead(BASE["gla_k"] + 1)
            for n, (s, w) in enumerate(TOK):
                act.wait_ge(g_e, n + 1)
                nc.scalar.activation(ge[0:w, n, :], ge[0:w, n, :], ACT.Exp, scale=-1.0).then_inc(g_e, 1)
            act.wait_ge(g_e, 6)
            for n, (s, w) in enumerate(TOK):
                nc.scalar.activation(ge[0:w, n, :], ge[0:w, n, :], ACT.Ln, bias=1.0).then_inc(g_ln, 1)
            for m in range(2, 4):
                ahead(BASE["gla_k"] + m)
            for m in range(3):
                ahead(BASE["gla_q"] + m)
            for h in range(4):
                act.wait_ge(g_b, h + 1)
                src = (mix + [stat])[h][:, 0:L]
                nc.scalar.activation(gb[:, h, :], src, ACT.Copy).then_inc(g_bc, 1)
                nc.scalar.activation(gq[:, h, :], src, ACT.Exp, scale=1.0 / 16).then_inc(g_e, 1)
                nc.scalar.activation(gk[:, h, :], src, ACT.Exp, scale=-1.0 / 16).then_inc(g_e, 1)
                if h == 0:
                    ahead(BASE["gla_q"] + 3)
            act.wait_ge(g_bc, 4)
            act.wait_ge(g_dif, 3)
            nc.scalar.activation(gkk.rearrange("p h t -> p (h t)"), gkk.rearrange("p h t -> p (h t)"), ACT.Exp, scale=1.0 / 16).then_inc(g_e, 1)
            nc.scalar.activation(gdec.rearrange("p h t -> p (h t)"), gdec.rearrange("p h t -> p (h t)"), ACT.Exp, scale=1.0 / 16).then_inc(g_dec, 1)
            for m in range(KD):
                ahead(BASE["gla_v"] + m)
            for i in range(6):
                n, e = divmod(i, 2)
                act.wait_ge(g_vt, i + 1)
                w = TOK[n][1]
                nc.scalar.activation(gv[0:w, n, 512 * e:512 * e + 512], mix[i % 3][0:w, :], ACT.Copy).then_inc(g_vc, 1)
            for n in range(3):
                act.wait_ge(g_kt, n + 1)
                w = TOK[n][1]
                nc.scalar.activation(gkt[0:w, n, :], mix[n][0:w, :], ACT.Copy).then_inc(g_kc, 1)
            for c, (s, w, n, base) in enumerate(CHUNKS):
                for m in range(2 * c, min(2 * c + 2, KD)):
                    ahead(BASE["gla_r"] + m)
                    act.wait_ge(g_r, m + 1)
                    nc.scalar.activation(sq[:, m, :], sq[:, m, :], ACT.Silu).then_inc(g_rs, 1)
                act.wait_ge(g_o, c + 1)
                nc.scalar.activation(y[:, :, s:s + w], acc[2 + c % 2][:, :].rearrange("p (m t) -> p m t", m=8)[:, :, 0:w], ACT.Copy).then_inc(g_oc, 1)
            act.wait_ge(g_oc, 5)
            for m in range(KD):
                nc.scalar.activation(gsq[:, m, :], y[:, m, :], ACT.Square).then_inc(g_sq, 1)
            act.wait_ge(g_mean, 1)
            nc.scalar.activation(groot, mix[0][0:4, 0:L], ACT.Sqrt, scale=4.0, bias=eps[0:4, 0:1]).then_inc(g_root, 1)
            for m in range(KD):
                act.wait_ge(g_f, m + 1)
                nc.scalar.activation(hh[:, m, :], y[:, m, :], ACT.Copy).then_inc(m_hi, 1)
            for m in range(KD):
                residual(6, m, BASE["gla_out"] + m)

        def gla_dve(dve, step, ahead, tail):
            def evac(name, m, out_, signal, count, scale=None):
                b = BASE[name] + m
                dve.wait_ge(used, b + 1)
                src = bank(name, m)[:, 0:L]
                if scale is None:
                    ins = nc.vector.tensor_tensor(out_, src, rx[:], ALU.mult)
                else:
                    ins = nc.vector.scalar_tensor_tensor(out_, src, scale, rx[:], ALU.mult, ALU.mult)
                ins.then_inc(signal, 1)
                dve.wait_ge(signal, count)
                dve.sem_inc(acc_used, 1)
                ahead(b)

            evac("gla_lr", 0, ry[:], g_lr, 1)
            nc.vector.memset(ry[32:33, :], 1.0).then_inc(g_lr, 1)
            for m in range(4):
                evac("gla_k", m, gkr[m // 2][:, m % 2, :], g_kr, m + 1)
            for m in range(2):
                evac("gla_q", m, gqr[0][:, m, :], g_qr, m + 1, float(P) ** -0.5)
            for m in range(4):
                if m:
                    n, w = m - 1, TOK[m - 1][1]
                    dve.wait_ge(g_ln, n + 1)
                    nc.vector.scalar_tensor_tensor(gls[0:w, n, :], mix[n][0:w, :], 0.0, ge[0:w, n, :], ALU.min, ALU.subtract).then_inc(g_ls, 1)
            for m in range(2, 4):
                evac("gla_q", m, gqr[m // 2][:, m % 2, :], g_qr, m + 1, float(P) ** -0.5)
            dve.wait_ge(g_bc, 4)
            for h in range(4):
                v = gb[:, h, META:].rearrange("p (c t) -> p c t", c=4)
                nc.vector.tensor_tensor(gkk[:, h, META:].rearrange("p (c t) -> p c t", c=4), v[:, :, 63:64].to_broadcast([P, 4, 64]), v,
                                        ALU.subtract).then_inc(g_dif, 1) if h == 3 else \
                    nc.vector.tensor_tensor(gkk[:, h, META:].rearrange("p (c t) -> p c t", c=4), v[:, :, 63:64].to_broadcast([P, 4, 64]), v,
                                            ALU.subtract)
            nc.vector.tensor_tensor(gkk[:, :, 0:META], gb[:, :, META - 1:META].to_broadcast([P, 4, META]), gb[:, :, 0:META],
                                    ALU.subtract).then_inc(g_dif, 1)
            nc.vector.tensor_copy(gdec, gb[:, :, META - 1:L:64]).then_inc(g_dif, 1)
            for m in range(KD):
                evac("gla_v", m, y[:, m, :], g_v, m + 1)
                if m < 4:
                    r, q = gkr[m // 2][:, m % 2, :], gqr[m // 2][:, m % 2, :]
                    dve.wait_ge(g_e, 15)
                    nc.vector.tensor_tensor(gq[:, m, :], gq[:, m, :], q, ALU.mult).then_inc(g_eq, 1)
                    nc.vector.tensor_tensor(gk[:, m, :], gk[:, m, :], r, ALU.mult).then_inc(g_eq, 1)
                    nc.vector.tensor_tensor(gkk[:, m, :], gkk[:, m, :], r, ALU.mult).then_inc(g_eq, 1)
            dve.wait_ge(sum_ok, norm_of(5) + 1)
            dve.wait_ge(g_dec, 1)

            def masked(c):
                s, w, n, base = CHUNKS[c]
                dve.wait_ge(g_att, c + 1)
                if c >= 2:
                    dve.wait_ge(g_o, c - 1)
                rows = slice(base, base + w)
                mask = gtri[rows, base:base + w].bitcast(I32).unsqueeze(1).to_broadcast([w, 4, w])
                nc.vector.copy_predicated(gatt[rows, c % 2, :, 0:w], mask,
                                          acc[c % 2][rows, 0:256].rearrange("p (h t) -> p h t", h=4)[:, :, 0:w]).then_inc(g_attc, 1)

            masked(0)
            for c in range(5):
                if c + 1 < 5:
                    masked(c + 1)
                if c < 4:
                    dve.wait_ge(g_kv, c + 1)
                    dve.wait_ge(g_eq, 12)
                    if c >= 2:
                        dve.wait_ge(g_o, c)
                    for h in range(4):
                        src = (mix[2], stat)[h // 2][:, 256 * (h % 2):256 * (h % 2) + 256]
                        if c == 0:
                            nc.vector.tensor_copy(gS[0][h], src).then_inc(g_S, 1)
                        else:
                            nc.vector.scalar_tensor_tensor(gS[c % 2][h], gS[(c - 1) % 2][h], gdec[:, h, c:c + 1], src, ALU.mult, ALU.add).then_inc(g_S, 1)
                    dve.wait_ge(g_S, 4 * c + 4)
                    for m in (2 * c, 2 * c + 1):
                        evac("gla_r", m, sq[:, m, :], g_r, m + 1)
            dve.wait_ge(g_rs, 8)

            def low(m):
                dve.wait_ge(m_hi, 16 + m + 1)
                nc.vector.tensor_tensor(hl[:, m, :], y[:, m, :], hh[:, m, :].bitcast(F32), ALU.subtract).then_inc(m_lo, 1)

            dve.wait_ge(g_root, 1)
            nc.vector.reciprocal(ry[0:4, :], groot).then_inc(g_inv, 1)
            for m in range(KD):
                dve.wait_ge(g_spread, m // 2 + 1)
                dve.wait_ge(g_ys, m + 1)
                nc.vector.scalar_tensor_tensor(y[:, m, :], y[:, m, :], col("gla_norm", m % 2), spread_bank(m // 2)[:, 0:L],
                                               ALU.mult, ALU.mult).then_inc(g_f, 1)
                if m:
                    low(m - 1)
            low(7)
            for m in range(KD):
                tail(6, m, "gla_out", BASE["gla_out"] + m)

        mixers["pool_late"][5] = gla_pool_late
        mixers["pool"][5], mixers["pe"][5], mixers["act"][5], mixers["dve"][5] = gla_pool, gla_pe, gla_act, gla_dve
        at["o"] = 0
        sk = area(544).rearrange("p (m t) -> p m t", m=2)
        svt = area(544).rearrange("p (m t) -> p m t", m=2)
        sv = area(768).rearrange("p (a n) -> p a n", a=3)
        smask = area(416)
        snk = area(16)
        sstat = area(32)
        snt = area(272)
        sS = area(832).rearrange("p (b n) -> p b n", b=2)
        sP = area(832).rearrange("p (b n) -> p b n", b=2)
        sPT = area(768).rearrange("p (b n) -> p b n", b=2)
        sPM = area(512).rearrange("p (b n) -> p b n", b=2)
        sq_q = y[:, :, META:]
        kv_hi, kv_lo, s_kv, s_q, s_perm, s_k, s_tr, s_v, s_mask, s_nk = (
            sem("s_" + n) for n in ("kvhi", "kvlo", "kv", "q", "perm", "k", "tr", "v", "mask", "nk"))
        s_s, s_min, s_exp, s_es, s_p, s_pt, s_ptc, s_pmc, s_o = (
            sem("s_" + n) for n in ("s", "min", "exp", "es", "p", "pt", "ptc", "pmc", "o"))
        SUNITS = [(j, h) for j in range(KD) for h in range(2)]
        SQ = ((0, 144, 0), (144, 272, P))

        def swa_pool(pool, step):
            pool.wait_ge(m_lo, 24)
            step(pool.memset(smask, 0.0))
            for s in (META, 144 + META + P):
                v = smask[:, s:s + P]
                pool.affine_select(out=v, in_=v, compare_op=ALU.is_ge, fill=BIG, base=0, pattern=[[-1, P]], channel_multiplier=1).then_inc(s_mask, 1)
            v = smask[:, 144 + META:144 + META + P]
            pool.affine_select(out=v, in_=v, compare_op=ALU.is_gt, fill=BIG, base=0, pattern=[[1, P]], channel_multiplier=-1).then_inc(s_mask, 1)

        def kv_pe(pe, gemm, opening, mean):
            opening((("kv", 0), ("kv", 1)), hh, hl, 0, (kv_lo, 0))
            gemm("kv", hh, hl, 0, None, first=2, last=3)
            mean(norm_of(7), c0(7))
            gemm("kv", hh, hl, 0, None, first=3)

        def kv_act(act, k):
            nc.scalar.activation(hh[:, k, :], x[:, k, :], ACT.Copy, scale=col("kv_norm", k)).then_inc(kv_hi, 1)

        def kv_low(dve, k):
            dve.wait_ge(kv_hi, k + 1)
            nc.vector.scalar_tensor_tensor(hl[:, k, :], x[:, k, :], col("kv_norm", k), hh[:, k, :].bitcast(F32), ALU.mult, ALU.subtract).then_inc(kv_lo, 1)

        def kv_dve(dve, ahead):
            for m in range(4):
                b = BASE["kv"] + m
                dve.wait_ge(used, b + 1)
                nc.vector.tensor_tensor((sk, svt)[m // 2][:, m % 2, :], bank("kv", m)[:, 0:L], rx[:], ALU.mult).then_inc(s_kv, 1)
                dve.wait_ge(s_kv, m + 1)
                dve.sem_inc(acc_used, 1)
                ahead(b)

        def swa_pe(pe, gemm, begin, opening):
            begin(8, ("swa_q", 0), ("swa_q", 1))
            pe.wait_ge(s_kv, 4)
            for m in range(2):
                ins = nc.tensor.matmul(mix[1 + m][:, 0:L], rot[:], sk[:, m, :], start=True, stop=True)
                ins.then_inc(s_perm, 1)
            pe.wait_ge(root_ok, norm_of(8) + 1)
            for kt in range(2):
                for t in range(2):
                    nc.tensor.transpose(stat[:, 256 * kt + P * t:256 * kt + P * t + P], svt[:, t, META + P * kt:META + P * kt + P], ident[:])
            for t in range(2):
                ins = nc.tensor.transpose(mix[0][0:META, P * t:P * t + P], svt[:, t, 0:META], ident[:])
            ins.then_inc(s_tr, 1)

            def perm(m):
                pe.wait_ge(s_q, m + 1)
                pe.wait_ge(s_k, m + 1 if m < 2 else m + 2)
                nc.tensor.matmul(turn_bank(2 + m)[:, 0:SEQ], rot[:], sq_q[:, m, :], start=True, stop=True).then_inc(s_perm, 1)

            gemm("swa_q", xh, xl, META, None, first=2, last=3)
            perm(0)
            perm(1)
            pe.wait_ge(acc_used, TILE["swa_q"] + 3)
            pe.wait_ge(s_v, 2)

            def scores(n):
                j, h = SUNITS[n]
                pe.wait_ge(s_k, 2 + j + 1)
                if n >= 2:
                    pe.wait_ge(s_min, n - 1)
                for qt, (c, e, q) in enumerate(SQ):
                    ins = nc.tensor.matmul(acc[n % 2][:, c:c + e], sq_q[DH * h:DH * h + DH, j, q:q + P], sk[DH * h:DH * h + DH, j // 4, 0:e],
                                           start=True, stop=True)
                ins.then_inc(s_s, 1)

            def turned(n):
                pe.wait_ge(s_p, n + 1)
                if n >= 2:
                    pe.wait_ge(s_ptc, n - 1)
                if n:
                    pe.wait_ge(s_pmc, n)
                for d, s in ((0, META), (P, 144 + META), (2 * P, 144 + META + P)):
                    nc.tensor.transpose(acc[2 + n % 2][:, d:d + P], sP[:, n % 2, s:s + P], ident[:])
                for qt in range(2):
                    ins = nc.tensor.transpose(stat[0:META, P * qt:P * qt + P], sP[:, n % 2, 144 * qt:144 * qt + META], ident[:])
                ins.then_inc(s_pt, 1)

            def values(n):
                j, h = SUNITS[n]
                g = 2 * (j // 4) + h
                dst = mix[j % 2][DH * h:DH * h + DH]
                if j >= 2 and h == 0:
                    pe.wait_ge(m_lo, 24 + j - 1)
                elif j < 2:
                    pe.wait_ge(s_k, 4)
                pe.wait_ge(s_ptc, n + 1)
                w = slice(DH * g, DH * g + DH)
                nc.tensor.matmul(dst[:, 0:SEQ], sv[:, 0, w], sPT[:, n % 2, 0:SEQ], start=True, stop=False)
                nc.tensor.matmul(dst[:, P:SEQ], sv[:, 1, w], sPT[:, n % 2, SEQ:SEQ + P], start=False, stop=False)
                pe.wait_ge(s_pmc, n + 1)
                nc.tensor.matmul(dst[:, 0:SEQ], sv[0:META, 2, w], sPM[0:META, n % 2, :], start=False, stop=True).then_inc(s_o, 1)

            scores(0)
            perm(2)
            for n in range(len(SUNITS) + 1):
                if n + 1 < len(SUNITS):
                    scores(n + 1)
                if n:
                    values(n - 1)
                t = n // 2 + 3
                if t < KD and n % 2 == 0:
                    pe.wait_ge(s_k, t + 2)
                    gemm("swa_q", xh, xl, META, None, first=t, last=t + 1)
                elif t < KD:
                    perm(t)
                if n < len(SUNITS):
                    turned(n)
            gemm("swa_out", hh, hl, META, (m_lo, 24))

        def turn_bank(i):
            return mix[1 + i % 2] if i < 4 else mix[2]

        def swa_act(act, step, ahead, residual):
            act.wait_ge(s_tr, 1)
            nc.scalar.activation(sv[:, 0:2, :].rearrange("p a n -> p (a n)"), stat[:, :], ACT.Copy).then_inc(s_v, 1)
            nc.scalar.activation(sv[0:META, 2, :], mix[0][0:META, 0:256], ACT.Copy).then_inc(s_v, 1)
            for m in range(3):
                ahead(BASE["swa_q"] + m)

            def exps(n):
                j, h = SUNITS[n]
                head = 2 * j + h
                act.wait_ge(s_min, n + 1)
                if n >= 2:
                    act.wait_ge(s_pt, n - 1)
                b = 2 * (n % 2)
                for qt, (c, e, q) in enumerate(SQ):
                    nc.scalar.activation(sP[:, n % 2, c:c + e], sS[:, n % 2, c:c + e], ACT.Exp, scale=-1.0, bias=sstat[:, b + qt:b + qt + 1],
                                         accum_out=sstat[:, 8 + b + qt:9 + b + qt]).then_inc(s_exp, 1)
                nc.scalar.activation(sstat[:, 16 + b:18 + b], sstat[:, b:b + 2], ACT.Exp, bias=col("sinks", head)).then_inc(s_es, 1)

            exps(0)
            for n in range(len(SUNITS)):
                if n + 1 < len(SUNITS):
                    exps(n + 1)
                act.wait_ge(s_pt, n + 1)
                if n >= 2:
                    act.wait_ge(s_o, n - 1)
                nc.scalar.activation(sPT[:, n % 2, :], acc[2 + n % 2][:, 0:384], ACT.Copy).then_inc(s_ptc, 1)
                if n % 2 == 0 and n // 2 + 3 < KD:
                    ahead(BASE["swa_q"] + n // 2 + 3)
                if n % 2 == 0 and n:
                    attn_hi(act, n // 2 - 1, s_o, n)
            attn_hi(act, KD - 1, s_o, len(SUNITS))
            for m in range(KD):
                residual(9, m, BASE["swa_out"] + m)

        def swa_dve(dve, step, ahead, tail):
            def rotated(i, v, w, tab):
                dve.wait_ge(s_perm, i + 1)
                if i:
                    dve.wait_ge(s_k, i)
                step(nc.vector.tensor_tensor(snt[:, 0:w], turn_bank(i)[:, 0:w], sinT[:, tab:], ALU.mult))
                step(nc.vector.tensor_tensor(v, v, cosT[:, tab:], ALU.mult))
                nc.vector.tensor_tensor(v, v, snt[:, 0:w], ALU.add).then_inc(s_k, 1)

            nc.vector.tensor_scalar(snk, par[:, COL["sinks"]:COL["sinks"] + 16], -1.0, None, ALU.mult).then_inc(s_nk, 1)
            for m in range(2):
                rotated(m, sk[:, m, :], L, SEQ)

            def query(m):
                b = BASE["swa_q"] + m
                dve.wait_ge(used, b + 1)
                nc.vector.scalar_tensor_tensor(sq_q[:, m, :], bank("swa_q", m)[:, 0:SEQ], -0.125, rx[:, META:], ALU.mult, ALU.mult).then_inc(s_q, 1)
                dve.wait_ge(s_q, m + 1)
                dve.sem_inc(acc_used, 1)

            for m in range(3):
                query(m)
            for m in range(2):
                rotated(2 + m, sq_q[:, m, :], SEQ, SEQ + META)
                ahead(BASE["swa_q"] + m)
            dve.wait_ge(s_nk, 1)
            dve.wait_ge(s_mask, 3)

            def least(n):
                j, h = SUNITS[n]
                dve.wait_ge(s_s, n + 1)
                if n >= 2:
                    dve.wait_ge(s_es, n - 1)
                b = 2 * (n % 2)
                for qt, (c, e, q) in enumerate(SQ):
                    ins = nc.vector.tensor_tensor_reduce(sS[:, n % 2, c:c + e], acc[n % 2][:, c:c + e], smask[:, c:c + e], 1.0,
                                                         snk[:, 2 * j + h:2 * j + h + 1], ALU.add, ALU.min, sstat[:, b + qt:b + qt + 1])
                ins.then_inc(s_min, 1)

            least(0)
            rotated(4, sq_q[:, 2, :], SEQ, SEQ + META)
            ahead(BASE["swa_q"] + 2)
            for n in range(len(SUNITS)):
                b = 2 * (n % 2)
                dve.wait_ge(s_es, n + 1)
                tot = sstat[:, 24:26]
                if n:
                    dve.wait_ge(s_p, n)
                step(nc.vector.tensor_tensor(tot, sstat[:, 8 + b:10 + b], sstat[:, 16 + b:18 + b], ALU.add))
                step(nc.vector.reciprocal(tot, tot))
                for qt, (c, e, q) in enumerate(SQ):
                    ins = nc.vector.tensor_scalar(sP[:, n % 2, c:c + e], sP[:, n % 2, c:c + e], tot[:, qt:qt + 1], None, ALU.mult)
                ins.then_inc(s_p, 1)
                if n + 1 < len(SUNITS):
                    least(n + 1)
                t = n // 2 + 3
                if t < KD and n % 2 == 0:
                    query(t)
                elif t < KD:
                    rotated(2 + t, sq_q[:, t, :], SEQ, SEQ + META)
                if n % 2 == 1 and n > 1:
                    attn_lo(dve, n // 2 - 1, 3)
                dve.wait_ge(s_pt, n + 1)
                if n >= 2:
                    dve.wait_ge(s_o, n - 1)
                nc.vector.tensor_copy(sPM[0:META, n % 2, :], stat[0:META, 0:SEQ]).then_inc(s_pmc, 1)
                if t < KD and n % 2 == 1:
                    ahead(BASE["swa_q"] + t)
            attn_lo(dve, KD - 1, 3)
            for m in range(KD):
                tail(9, m, "swa_out", BASE["swa_out"] + m)

        mixers["pool"][8], mixers["pe"][8], mixers["act"][8], mixers["dve"][8] = swa_pool, swa_pe, swa_act, swa_dve
        block = ctx.enter_context(nc.Block())

        @block.sync
        def _(sp):
            for s in range(RING):
                if s == 2:
                    sp.wait_ge(in_x, 32)
                sp.dma_start(raw[:, s, :], a["w"][s]).then_inc(raw_in[s], 16)
            with sp.Fori(1, HALVES // RING) as i:
                for s in range(RING):
                    sp.wait_ge(w_lo, RING * i - RING + s + 1)
                    sp.dma_start(raw[:, s, :], a["w"][bass.ds(RING * i + s, 1)].rearrange("a p n -> p (a n)")) \
                        .then_inc(raw_in[s], 16)
            for n in range(HALVES // RING * RING, HALVES):
                sp.wait_ge(w_lo, n - RING + 1)
                sp.dma_start(raw[:, n % RING, :], a["w"][n]).then_inc(raw_in[n % RING], 16)
            for k in range(KD):
                sp.wait_ge(x_new[k % 2], updated(upto, k))
                sp.dma_start(out[k], x[:, k, META:]).then_inc(out_ok, 16)
            sp.wait_ge(out_ok, 16 * KD)

        @block.gpsimd
        def _(pool):
            step = Chain(pool, pool_step)
            pool.memset(ones[:], 1.0 / D).then_inc(const_ok, 1)
            pool.memset(ones4[:], 4.0 / D).then_inc(const_ok, 1)
            for n, v in enumerate((1e-6, 4e-6, 1e-5, HALF_PI, 64e-6)):
                pool.memset(eps[:, n:n + 1], v).then_inc(const_ok, 1)

            tables_pool(pool, step)

            def norm_sum(v, c, between=()):
                between = dict(between)
                pool.wait_ge(sq_new, 8 * v + 2)
                if v:
                    pool.wait_ge(mean_ok, v)
                step(pool.tensor_tensor(sumsq[:, c:], sq[:, 0, c:], sq[:, 1, c:], ALU.add))
                for k in range(2, KD):
                    if k in between:
                        between[k]()
                    pool.wait_ge(sq_new, 8 * v + k + 1)
                    ins = pool.tensor_tensor(sumsq[:, c:], sumsq[:, c:], sq[:, k, c:], ALU.add)
                    if k < KD - 1:
                        step(ins)
                ins.then_inc(sum_ok, 1)

            def post_update(u):
                norm_sum(norm_of(u, True), c0(u))

                def add(k):
                    pool.wait_ge(t_new, 8 * (u - 5) + k + 1)
                    pool.tensor_tensor(x[:, k, c0(u):], x[:, k, c0(u):], y[:, k, c0(u):], ALU.add).then_inc(x_new[0], 1)

                add(0)
                add(2)
                if u < upto and u != 7:
                    norm_sum(norm_of(u), c0(u), ((2, lambda: add(4)), (3, lambda: add(6))))
                else:
                    add(4)
                    add(6)
                    if u < upto:
                        norm_sum(norm_of(u), c0(u))

            for u in range(0, upto + 1):
                if u in mixers.get("pool", {}):
                    mixers["pool"][u](pool, step)
                if u >= 5:
                    post_update(u)
                elif u < upto:
                    norm_sum(norm_of(u), c0(u))
                if u in mixers.get("pool_late", {}):
                    mixers["pool_late"][u](pool, step)

        @block.tensor
        def _(pe):
            pe.wait_ge(const_ok, 7)

            def half(h, q, name, t, part, hi, lo, c, kt, wait):
                pe.wait_ge(w_lo, h.n + 1)
                if part == 0 and q is not None:
                    pe.wait_ge(acc_used, q - (1 if name == "gla_r" else 3))
                ks = range(part * KD, min(kt, part * KD + KD))
                for k in ks:
                    if wait:
                        pe.wait_ge(wait[0], wait[1] + k + 1)
                    w = slice((k % KD) * P, (k % KD + 1) * P)
                    for w_part, v_part in ((wh, hi), (wh, lo), (wl, hi)):
                        ins = nc.tensor.matmul(bank(name, t)[:, 0:L - c], w_part[:, h.slot, w], v_part[:, k, c:],
                                               start=(k == 0 and w_part is wh and v_part is hi),
                                               stop=(k == kt - 1 and w_part is wl))
                ins.then_inc(used, 1)

            def gemm(name, hi, lo, c, wait, kt=KD, first=0, last=None):
                parts = -(-kt // KD)
                last = SIZE[name] // parts if last is None else last

                def tiles(i, ts):
                    for t in ts:
                        for part in range(parts):
                            b = BASE[name] + t * parts + part
                            q = TILE[name] + t + 8 * i
                            if isinstance(q, int) and q < 4:
                                q = None
                            half(Half(b, i * (2 * parts)), q, name, t, part, hi, lo, c, kt,
                                 wait if t == 0 else None)

                peel = min(4, last) if first else 0
                tiles(0, range(first, peel))
                first = max(first, peel)
                rounds = (last - first) // 8
                if rounds > 1:
                    with pe.Fori(0, rounds) as i:
                        tiles(i, range(first, first + 8))
                    first += 8 * rounds
                tiles(0, range(first, last))

            def opening(pair, hi, lo, c, wait):
                for name, t in pair:
                    pe.wait_ge(w_lo, BASE[name] + t + 1)
                    if TILE[name] + t >= 4:
                        pe.wait_ge(acc_used, TILE[name] + t - 3)
                for k in range(KD):
                    pe.wait_ge(wait[0], wait[1] + k + 1)
                    w = slice(k * P, (k + 1) * P)
                    for name, t in pair:
                        slot = (BASE[name] + t) % RING
                        for w_part, v_part in ((wh, hi), (wh, lo), (wl, hi)):
                            ins = nc.tensor.matmul(bank(name, t)[:, 0:L - c], w_part[:, slot, w], v_part[:, k, c:],
                                                   start=(k == 0 and w_part is wh and v_part is hi),
                                                   stop=(k == KD - 1 and w_part is wl))
                        if k == KD - 1:
                            ins.then_inc(used, 1)

            def mean(v, c):
                pe.wait_ge(sum_ok, v + 1)
                if v:
                    pe.wait_ge(root_ok, v)
                nc.tensor.matmul(stat[:, 0:L - c], (ones4 if halved(v) else ones)[:], sumsq[:, c:], start=True,
                                 stop=True).then_inc(mean_ok, 1)

            def begin(u, *pair):
                opening(pair, xh, xl, cg(u), (x_lo, 8 * u))
                mean(norm_of(u), c0(u))

            for u in range(0, upto):
                f = FFN_AFTER.get(u)
                if u == 7:
                    kv_pe(pe, gemm, opening, mean)
                    gemm("ffn4_a", xh, xl, cg(u), (x_lo, 8 * u))
                elif f is not None:
                    begin(u, (f"ffn{f}_a", 0), (f"ffn{f}_a", 1))
                    gemm(f"ffn{f}_a", xh, xl, cg(u), None, first=2)
                else:
                    mixers["pe"][u](pe, gemm, begin, opening)
                if f is not None:
                    gemm(f"ffn{f}_b", hh, hl, cg(u), (f_lo, KF * f), KF)
                if u + 1 >= 5:
                    mean(norm_of(u + 1, True), c0(u + 1))

        @block.scalar
        def _(act):
            step = Chain(act, act_step)

            def split(h):
                act.wait_ge(raw_in[h.slot], 16 * h.round + 16)
                if not (isinstance(h.n, int) and h.n < RING):
                    act.wait_ge(used, h.n - RING + 1)
                nc.scalar.activation(wh[:, h.slot, :], raw[:, h.slot, :], ACT.Copy).then_inc(w_hi, 1)

            def ahead(b, i=0):
                if not isinstance(i, int) or b + RING * i + RING < HALVES:
                    split(Half(b + RING, i))

            def x_parts(u, k):
                c = c0(u)
                if u:
                    act.wait_ge(x_new[k % 2], updated(u, k))
                else:
                    act.wait_ge(in_x, 32)
                if u < upto:
                    nc.scalar.activation(xh[:, k, c:], x[:, k, c:], ACT.Copy, scale=col(NEXT_GAIN[u], k)).then_inc(x_hi, 1)
                    squares(x, norm_of(u), k, c)

            def squares(src, v, k, c):
                if v:
                    act.wait_ge(sum_ok, v)
                nc.scalar.activation(sq[:, k, c:], src[:, k, c:], ACT.Square).then_inc(sq_new, 1)

            def ffn(f, u):
                base = BASE[f"ffn{f}_a"]
                c = cg(u)

                def high_h(i, t):
                    act.wait_ge(f_h, KF * f + t + 1 + 2 * i)
                    act.wait_ge(const_ok, 7)
                    nc.scalar.activation(hh[:, bass.ds(2 * i + t, 1), c:], th[:, t:t + 1, c:], ACT.Copy).then_inc(f_hi, 1)

                def two(i, first):
                    for t in range(2):
                        ahead(base + 2 * t, i)
                        act.wait_ge(f_g, KF * f + t + 2 * i + 1)
                        nc.scalar.activation(ts[:, t, c:], tg[:, t, c:], ACT.Silu).then_inc(f_s, 1)
                        if t:
                            high_h(i, 0)
                        elif not first:
                            high_h(i - 1, 1)
                        ahead(base + 2 * t + 1, i)

                two(0, True)
                with act.Fori(1, KF // 2) as i:
                    two(i, False)
                high_h(KF // 2 - 1, 1)
                if f == 0:
                    tables_act(act)
                base = BASE[f"ffn{f}_b"]
                for m in range(KD):
                    for part in range(KF_PARTS - 1):
                        ahead(base + m * KF_PARTS + part)
                    residual(u + 1, m, base + m * KF_PARTS + KF_PARTS - 1)

            def rooted(v, c):
                act.wait_ge(mean_ok, v + 1)
                if v:
                    act.wait_ge(rms_ok, v)
                nc.scalar.activation(root[:, c:], stat[:, 0:L - c], ACT.Sqrt,
                                     bias=eps[:, 1:2] if halved(v) else eps[:, 0:1]).then_inc(root_ok, 1)

            def residual(u, m, b):
                if m < KD - 1:
                    ahead(b)
                if u < 5:
                    x_parts(u, m)
                else:
                    act.wait_ge(y_new, 8 * (u - 5) + m + 1)
                    squares(y, norm_of(u, True), m, c0(u))
                if m == KD - 1:
                    if u >= 5:
                        rooted(norm_of(u, True), c0(u))
                    if u == 7 and u < upto:
                        for k in range(KD):
                            act.wait_ge(x_new[k % 2], updated(u, k))
                            kv_act(act, k)
                    if u >= 5:
                        for k in range(KD):
                            x_parts(u, k)
                    ahead(b)

            act.dma_start(par[:], a["par"]).then_inc(in_par, 16)
            for h in range(2):
                act.dma_start(x[:, 4 * h:4 * h + 4, :], a["x"][:, 4 * h:4 * h + 4, :]).then_inc(in_x, 16)
            act.wait_ge(const_ok, 7)
            split(Half(0))
            split(Half(1))
            act.wait_ge(in_par, 16)
            for k in range(KD):
                x_parts(0, k)
            split(Half(2))
            split(Half(3))
            for u in range(0, upto):
                rooted(norm_of(u), c0(u))
                if u == 7:
                    for m in range(4):
                        ahead(BASE["kv"] + m)
                f = FFN_AFTER.get(u)
                if f is not None:
                    ffn(f, u)
                else:
                    mixers["act"][u](act, step, ahead, residual)

        @block.vector
        def _(dve):
            step = Chain(dve, dve_step)

            def split(h):
                dve.wait_ge(w_hi, h.n + 1)
                nc.vector.tensor_tensor(wl[:, h.slot, :], raw[:, h.slot, :], wh[:, h.slot, :].bitcast(F32),
                                        ALU.subtract).then_inc(w_lo, 1)

            def ahead(b, i=0):
                if not isinstance(i, int) or b + RING * i + RING < HALVES:
                    split(Half(b + RING, i))

            def low_x(u, k):
                if u < upto:
                    c = c0(u)
                    dve.wait_ge(x_hi, 8 * u + k + 1)
                    nc.vector.scalar_tensor_tensor(xl[:, k, c:], x[:, k, c:], col(NEXT_GAIN[u], k),
                                                   xh[:, k, c:].bitcast(F32), ALU.mult, ALU.subtract).then_inc(x_lo, 1)

            def rms(v, c, dst):
                dve.wait_ge(root_ok, v + 1)
                nc.vector.reciprocal(dst[:, c:], root[:, c:]).then_inc(rms_ok, 1)
                dve.wait_ge(rms_ok, v + 1)

            def post_norm(u):
                c = c0(u)
                rms(norm_of(u, True), c, ry)

                def scaled(k):
                    nc.vector.scalar_tensor_tensor(y[:, k, c:], y[:, k, c:], col(POST_GAIN[u], k), ry[:, c:],
                                                   ALU.mult, ALU.mult).then_inc(t_new, 1)

                def add(k):
                    if k % 2:
                        dve.wait_ge(t_new, 8 * (u - 5) + k + 1)
                        nc.vector.tensor_tensor(x[:, k, c:], x[:, k, c:], y[:, k, c:], ALU.add).then_inc(x_new[1], 1)

                for k in range(4):
                    scaled(k)
                    if k:
                        add(k - 1)
                add(3)
                for k in range(KD):
                    if u == 7 and u < upto:
                        kv_low(dve, k)
                    else:
                        low_x(u, k)
                    if k + 4 < KD:
                        scaled(k + 4)
                        add(k + 4)
                if u == 7 and u < upto:
                    for k in range(KD):
                        low_x(u, k)

            def ffn(f, u):
                name = f"ffn{f}_a"
                c = cg(u)

                def low_h(i, t):
                    dve.wait_ge(f_hi, KF * f + t + 1 + 2 * i)
                    nc.vector.tensor_tensor(hl[:, bass.ds(2 * i + t, 1), c:], th[:, t:t + 1, c:],
                                            hh[:, bass.ds(2 * i + t, 1), c:].bitcast(F32), ALU.subtract).then_inc(f_lo, 1)

                def two(i, first):
                    for t in range(2):
                        n = KF * f + t + 2 * i + 1
                        b = BASE[name] + 2 * t
                        dve.wait_ge(used, Half(b, i).n + 1)
                        nc.vector.tensor_tensor(tg[:, t, c:], bank(name, 2 * t)[:, 0:L - c], rx[:, c:], ALU.mult).then_inc(f_g, 1)
                        dve.wait_ge(f_g, n)
                        dve.sem_inc(acc_used, 1)
                        ahead(b, i)
                        if t:
                            low_h(i, 0)
                        elif not first:
                            low_h(i - 1, 1)
                        dve.wait_ge(used, Half(b + 1, i).n + 1)
                        nc.vector.tensor_tensor(tu[:, t, c:], bank(name, 2 * t + 1)[:, 0:L - c], rx[:, c:],
                                                ALU.mult).then_inc(acc_used, 1)
                        dve.wait_ge(acc_used, TILE[name] + 4 * i + 2 * t + 2)
                        dve.wait_ge(f_s, n)
                        nc.vector.tensor_tensor(th[:, t, c:], tu[:, t, c:], ts[:, t, c:], ALU.mult).then_inc(f_h, 1)
                        ahead(b + 1, i)

                two(0, True)
                with dve.Fori(1, KF // 2) as i:
                    two(i, False)
                low_h(KF // 2 - 1, 1)
                if f == 0:
                    tables_dve(dve, step)
                name = f"ffn{f}_b"
                for m in range(KD):
                    for part in range(KF_PARTS):
                        b = BASE[name] + m * KF_PARTS + part
                        if part == KF_PARTS - 1:
                            tail(u + 1, m, name, b)
                        else:
                            ahead(b)

            def tail(u, m, name, b):
                dve.wait_ge(used, b + 1)
                c = c0(u)
                if u < 5:
                    nc.vector.tensor_tensor(x[:, m, META:], x[:, m, META:], bank(name, m)[:, 0:SEQ], ALU.add).then_inc(x_new[m % 2], 1)
                    dve.wait_ge(x_new[m % 2], updated(u, m))
                else:
                    nc.vector.tensor_copy(y[:, m, c:], bank(name, m)[:, 0:L - c]).then_inc(y_new, 1)
                    dve.wait_ge(y_new, 8 * (u - 5) + m + 1)
                dve.sem_inc(acc_used, 1)
                if m < KD - 1:
                    ahead(b)
                if u < 5:
                    low_x(u, m)
                if m == KD - 1:
                    if u >= 5:
                        post_norm(u)
                    ahead(b)

            split(Half(0))
            split(Half(1))
            dve.wait_ge(in_par, 16)
            for k in range(KD):
                low_x(0, k)
            split(Half(2))
            split(Half(3))
            for u in range(0, upto):
                rms(norm_of(u), c0(u), rx)
                if u == 7:
                    kv_dve(dve, ahead)
                f = FFN_AFTER.get(u)
                if f is not None:
                    ffn(f, u)
                else:
                    mixers["dve"][u](dve, step, ahead, tail)


def _tiles(w):
    import numpy as np
    w = np.asarray(w)
    n = w.shape[1]
    pad = -n % P
    if pad:
        w = np.concatenate([w, np.zeros((w.shape[0], pad), w.dtype)], axis=1)
    return np.ascontiguousarray(w.reshape(-1, P, (n + pad) // P, P).transpose(2, 1, 0, 3)).reshape((n + pad) // P, P, -1)


def _pairs(w):
    import numpy as np
    n = w.shape[1] // 2
    return np.stack([_tiles(w[:, :n]), _tiles(w[:, n:])], axis=1).reshape(-1, P, KD * P)


def _down(w):
    import numpy as np
    w = np.asarray(w)
    w = np.concatenate([w, np.zeros((KF_PARTS * D - FF, D), w.dtype)])
    return w.reshape(KF_PARTS, KD, P, KD, P).transpose(3, 0, 2, 1, 4).reshape(-1, P, KD * P)


def _cols(v):
    import numpy as np
    return np.asarray(v).reshape(-1, P).T


def kernel(**t):
    import numpy as np
    import concourse.bacc as bacc
    from concourse.bass_utils import run_bass_kernel_spmd as run

    t = {k: np.asarray(v) for k, v in t.items()}
    half = ROPE // 2
    heads = [g * 4 + r for t2 in range(2) for r in range(4) for g in (2 * t2, 2 * t2 + 1)]
    hcols = np.concatenate([np.arange(h * DH, h * DH + DH) for h in heads])
    nsa, gla = t["nsa_w_in"][0], t["gla_w_in_2"][0]
    w_ffn_in, w_ffn_out = t["w_ffn_in_2"], t["w_ffn_out_2"]
    by_name = {
        "conv_in": _pairs(t["conv_w_in"][0]), "conv_out": _tiles(t["conv_w_out"][0]),
        "nsa_kv": _tiles(nsa[:, 1024:2560]), "nsa_gate": _tiles(nsa[:, 2560:]), "nsa_q": _tiles(nsa[:, hcols]),
        "nsa_out": _tiles(t["nsa_w_out"][0][hcols]),
        "gla_lr": _tiles(gla[:, 3072:]), "gla_k": _tiles(gla[:, 512:1024]), "gla_q": _tiles(gla[:, :512]),
        "gla_v": _tiles(gla[:, 1024:2048]), "gla_r": _tiles(gla[:, 2048:3072]), "gla_out": _tiles(t["gla_w_out_2"][0]),
        "kv": _tiles(t["w_kv_2"]), "swa_q": _tiles(t["swa_w_q_2"][0][:, hcols]), "swa_out": _tiles(t["swa_w_out_2"][0][hcols]),
    }
    for f in range(2):
        by_name[f"ffn{f}_a"], by_name[f"ffn{f}_b"] = _pairs(t["ffn_w_in"][f]), _down(t["ffn_w_out"][f])
    for f in range(4):
        by_name[f"ffn{2 + f}_a"], by_name[f"ffn{2 + f}_b"] = _pairs(w_ffn_in[f // 2, f % 2]), _down(w_ffn_out[f // 2, f % 2])
    stream = np.concatenate([by_name[name] for name, _ in STAGES])
    assert stream.shape[0] == HALVES

    f32 = np.float32
    two = lambda v: np.concatenate([v, v], axis=-1)[..., None]
    conv_b = t["conv_b_in"][0]
    rope = np.zeros((P, 2), f32)
    for h in range(2):
        for d in range(ROPE):
            rope[h * DH + d] = (f32(THETA) ** (-f32(d % half) / f32(half)), -1.0 if d < half else 1.0)
    pieces = {
        "mix0": _cols(t["norm_mix"][0]), "mix1": _cols(t["norm_mix"][1]),
        "ffn0": _cols(t["norm_ffn"][0]), "ffn1": _cols(t["norm_ffn"][1]),
        "conv_ba": _cols(conv_b[:D]), "conv_bg": _cols(conv_b[D:]),
        "conv_w": t["conv_w_dw"][0].reshape(CONV, KD, P).transpose(2, 1, 0).reshape(P, -1),
        "conv_b": _cols(t["conv_b_dw"][0]), "ln_g": _cols(t["conv_ln_g"][0]), "ln_b": _cols(t["conv_ln_b"][0]),
        "q_gain": two(t["nsa_q_gain"][0]), "k_gain": np.tile(t["nsa_k_gain"][0].T, (2, 1)),
        "cmp_b1": np.tile(t["nsa_cmp_b1"][0].T, (2, 1)),
        "cmp_pos": np.tile(t["nsa_cmp_pos"][0].reshape(2, 2, 16, DH).transpose(3, 0, 2, 1).reshape(DH, 64), (2, 1)),
        "g2": _cols(t["norm_gains_2"]), "kv_norm": _cols(t["kv_norm_2"]), "gate_b": _cols(t["gla_b_gate_2"][0]),
        "gla_norm": _cols(t["gla_norm_2"][0]), "sinks": np.broadcast_to(t["swa_sinks_2"][0][heads], (P, 16)),
        "inv_freq": rope[:, 0:1], "rope_sign": rope[:, 1:2],
    }
    arrays = {
        "w": stream,
        "par": np.ascontiguousarray(np.concatenate([pieces[name].reshape(P, n) for name, n in PARAMS], axis=1)),
        "x": np.ascontiguousarray(np.concatenate([t["meta_tokens_2"], t["x"][0]]).T.reshape(KD, P, L).transpose(1, 0, 2)),
        "positions": t["positions"],
        "cmp_w1": np.ascontiguousarray(np.tile(t["nsa_cmp_w1"][0].reshape(2, 2, 16, DH, DH).transpose(3, 0, 2, 1, 4), (2, 1, 1, 1, 1))).reshape(P, -1),
        "cmp_w2": np.ascontiguousarray(t["nsa_cmp_w2"][0].transpose(1, 0, 2)).reshape(DH, -1),
        "w_gate": t["gla_w_gate_2"][0], "gate_row": t["gla_b_gate_2"],
    }
    nc = bacc.Bacc("TRN2", target_bir_lowering=False, num_devices=1)
    drams = {k: nc.dram_tensor("in_" + k, v.shape, mybir.dt.from_np(v.dtype), kind="ExternalInput").ap() for k, v in arrays.items()}
    out = nc.dram_tensor("out", (KD, P, SEQ), F32, kind="ExternalOutput").ap()
    build(nc, drams, out, UPDATES)
    r = run(nc, [{"in_" + k: v for k, v in arrays.items()}], core_ids=[0])
    return np.ascontiguousarray(r.results[0]["out"].reshape(D, SEQ).T)[None]
```
